# Optimizing a Trainium2 kernel written in Bass

```python
import jax
import jax.numpy as jnp
from jax import lax
import numpy as np

D_MODEL = 1024
BATCH = 1
SEQ = 1024
DEPTH = 1
DEC_BATCH = 8
DEC_SEQ = 8
PAST_LEN = 8192
PAGE_SIZE = 128

MIX_WIDTH = D_MODEL
N_MIXERS = 4
W_GROUP = MIX_WIDTH // N_MIXERS
HEAD_CH = 64
CONV_A = 3
POOL_WINDOWS = (2, 4, 8, 16)
POOL_CH = W_GROUP // len(POOL_WINDOWS)
POOL_STATE = max(POOL_WINDOWS) - 1
CONV_C = 31
CHUNK = 128
N_HEADS_D = W_GROUP // HEAD_CH
HEAD_D = HEAD_CH
IN_COLS = 8 * W_GROUP
N_EXPERT_GROUPS = 4
EXPERTS_PER_GROUP = 8
N_EXPERTS = N_EXPERT_GROUPS * EXPERTS_PER_GROUP
TOP_K_IN_GROUP = 2
D_FF_EXPERT = 128
EPS = 1e-6

kernel_name = 'hybrid_conv_pool_sgu_hmoe_step'

def rmsnorm(x, g):
    xf = x.astype(jnp.float32)
    y = xf * lax.rsqrt(jnp.mean(xf * xf, axis=-1, keepdims=True) + EPS)
    return (y * g.astype(jnp.float32)).astype(x.dtype)

def layernorm(x, g, b):
    xf = x.astype(jnp.float32)
    mu = jnp.mean(xf, axis=-1, keepdims=True)
    var = jnp.mean(jnp.square(xf - mu), axis=-1, keepdims=True)
    y = (xf - mu) * lax.rsqrt(var + EPS) * g.astype(jnp.float32) + b.astype(jnp.float32)
    return y.astype(x.dtype)

def causal_dwconv(x, prev, w):
    k_w, ch = w.shape
    xp = jnp.concatenate([prev.astype(x.dtype), x], axis=1)
    y = lax.conv_general_dilated(xp, w[:, None, :].astype(x.dtype), window_strides=(1,), padding='VALID',
                                 dimension_numbers=('NWC', 'WIO', 'NWC'), feature_group_count=ch)
    return y, xp[:, xp.shape[1] - (k_w - 1):]

def multiscale_pool(x, prev, w_pool, scale, start_pos):
    bsz, t_len, _ = x.shape
    xp = jnp.concatenate([prev.astype(x.dtype), x], axis=1).astype(jnp.float32)
    csum = jnp.concatenate([jnp.zeros_like(xp[:, :1]), jnp.cumsum(xp, axis=1)], axis=1)
    pos = start_pos + jnp.arange(t_len, dtype=jnp.int32)
    end = POOL_STATE + 1
    means = []
    for g, win in enumerate(POOL_WINDOWS):
        ch = slice(g * POOL_CH, (g + 1) * POOL_CH)
        s = csum[:, end:end + t_len, ch] - csum[:, end - win:end - win + t_len, ch]
        cnt = jnp.minimum(pos + 1, win).astype(jnp.float32)[None, :, None]
        means.append(s / cnt)
    d = jnp.concatenate(means, axis=-1) - x.astype(jnp.float32)
    d = d.reshape(bsz, t_len, len(POOL_WINDOWS), POOL_CH).astype(x.dtype)
    y = jnp.einsum('btgc,gce->btge', d, w_pool.astype(x.dtype)).reshape(bsz, t_len, W_GROUP)
    return y * scale.astype(x.dtype), xp[:, xp.shape[1] - POOL_STATE:].astype(x.dtype)

def chunk_spatial_mix(v, w_s, b_s):
    bsz, t_len, _ = v.shape
    L = min(t_len, CHUNK)
    n_chunks = t_len // L
    ws = jnp.where(jnp.tril(jnp.ones((L, L), dtype=bool)), w_s[:, :L, :L], 0.0).astype(v.dtype)
    vh = v.reshape(bsz, n_chunks, L, N_HEADS_D, HEAD_D)
    bias = b_s[:, :L].T[None, None, :, :, None].astype(v.dtype)
    mixed = jnp.einsum('hij,bnjhc->bnihc', ws, vh) + bias
    return mixed.reshape(bsz, t_len, W_GROUP)

def hier_moe(x, rg_w, rg_b, re_w, re_b, w_gate, w_up, w_down):
    bsz, t_len, d = x.shape
    xt = x.reshape(-1, d)
    n_tok = xt.shape[0]
    lg = jnp.matmul(xt, rg_w).astype(jnp.float32) + rg_b.astype(jnp.float32)
    pg = jax.nn.softmax(lg, axis=-1)
    p_top, g_idx = lax.top_k(pg, 1)
    le = (jnp.matmul(xt, re_w).astype(jnp.float32) + re_b.astype(jnp.float32))
    le = le.reshape(n_tok, N_EXPERT_GROUPS, EXPERTS_PER_GROUP)
    le_sel = jnp.einsum('nge,ng->ne', le, jax.nn.one_hot(g_idx[:, 0], N_EXPERT_GROUPS, dtype=jnp.float32))
    v2, e_idx = lax.top_k(le_sel, TOP_K_IN_GROUP)
    w2 = jax.nn.softmax(v2, axis=-1) * p_top
    expert = g_idx * EXPERTS_PER_GROUP + e_idx
    gates = jnp.einsum('nk,nke->ne', w2, jax.nn.one_hot(expert, N_EXPERTS, dtype=jnp.float32)).astype(x.dtype)
    hg = jnp.einsum('nd,edf->nef', xt, w_gate.astype(x.dtype))
    hu = jnp.einsum('nd,edf->nef', xt, w_up.astype(x.dtype))
    act = jax.nn.silu(hg) * hu * gates[:, :, None]
    out = jnp.einsum('nef,efd->nd', act, w_down.astype(x.dtype))
    return out.reshape(bsz, t_len, d)

def _trunk(x, st_a, st_p, st_c, start_pos, weights):
    (g_mix, w_in, conv_a_w, pool_w, pool_scale, conv_c_w, conv_c_b, ln_c_g, ln_c_b, ln_d_g, ln_d_b,
     sgu_w, sgu_b, w_out, g_ffn, router_group_w, router_group_b, router_expert_w, router_expert_b,
     expert_w_gate, expert_w_up, expert_w_down, g_final) = weights
    new_a, new_p, new_c, v_rows = [], [], [], []
    for l in range(DEPTH):
        h = rmsnorm(x, g_mix[l])
        z = jnp.einsum('btd,de->bte', h, w_in[l].astype(x.dtype))
        a_b, a_c, a_x, p_x, c_a, c_g, d_u, d_v = jnp.split(z, 8, axis=-1)
        y_a, sa = causal_dwconv(a_c * a_x, st_a[l], conv_a_w[l])
        y_a = a_b * y_a
        y_p, sp = multiscale_pool(p_x, st_p[l], pool_w[l], pool_scale[l], start_pos)
        y_c, sc = causal_dwconv(c_a * jax.nn.sigmoid(c_g), st_c[l], conv_c_w[l])
        y_c = jax.nn.silu(layernorm(y_c + conv_c_b[l].astype(x.dtype), ln_c_g[l], ln_c_b[l]))
        v_n = layernorm(d_v, ln_d_g[l], ln_d_b[l])
        y_d = d_u * chunk_spatial_mix(v_n, sgu_w[l], sgu_b[l])
        mix = jnp.concatenate([y_a, y_p, y_c, y_d], axis=-1)
        x = x + jnp.einsum('bte,ed->btd', mix, w_out[l].astype(x.dtype))
        h = rmsnorm(x, g_ffn[l])
        x = x + hier_moe(h, router_group_w[l], router_group_b[l], router_expert_w[l], router_expert_b[l],
                         expert_w_gate[l], expert_w_up[l], expert_w_down[l])
        new_a.append(sa)
        new_p.append(sp)
        new_c.append(sc)
        v_rows.append(v_n)
    y = rmsnorm(x, g_final)
    return y, jnp.stack(new_a), jnp.stack(new_p), jnp.stack(new_c), v_rows

def setup_inputs(seed: int = 0) -> dict:
    key = jax.random.key(seed)
    ks = iter(jax.random.split(key, 40))

    def nrm(shape, scale):
        return jax.random.normal(next(ks), shape, jnp.float32) * scale

    def gain(shape):
        return 1.0 + nrm(shape, 0.05)

    return {
        'x_prompt': nrm((BATCH, SEQ, D_MODEL), 1.0),
        'x_sample': nrm((DEC_BATCH, DEC_SEQ, D_MODEL), 1.0),
        'state_conv_a': nrm((DEPTH, DEC_BATCH, CONV_A - 1, W_GROUP), 1.0),
        'state_pool': nrm((DEPTH, DEC_BATCH, POOL_STATE, W_GROUP), 1.0),
        'state_conv_c': nrm((DEPTH, DEC_BATCH, CONV_C - 1, W_GROUP), 0.5),
        'g_mix': gain((DEPTH, D_MODEL)),
        'w_in': nrm((DEPTH, D_MODEL, IN_COLS), D_MODEL ** -0.5),
        'conv_a_w': nrm((DEPTH, CONV_A, W_GROUP), CONV_A ** -0.5),
        'pool_w': nrm((DEPTH, len(POOL_WINDOWS), POOL_CH, POOL_CH), POOL_CH ** -0.5),
        'pool_scale': 1.0 + nrm((DEPTH, W_GROUP), 0.1),
        'conv_c_w': nrm((DEPTH, CONV_C, W_GROUP), CONV_C ** -0.5),
        'conv_c_b': nrm((DEPTH, W_GROUP), 0.02),
        'ln_c_g': gain((DEPTH, W_GROUP)),
        'ln_c_b': nrm((DEPTH, W_GROUP), 0.02),
        'ln_d_g': gain((DEPTH, W_GROUP)),
        'ln_d_b': nrm((DEPTH, W_GROUP), 0.02),
        'sgu_w': nrm((DEPTH, N_HEADS_D, CHUNK, CHUNK), 0.5 * CHUNK ** -0.5),
        'sgu_b': 1.0 + nrm((DEPTH, N_HEADS_D, CHUNK), 0.1),
        'w_out': nrm((DEPTH, MIX_WIDTH, D_MODEL), MIX_WIDTH ** -0.5),
        'g_ffn': gain((DEPTH, D_MODEL)),
        'router_group_w': nrm((DEPTH, D_MODEL, N_EXPERT_GROUPS), D_MODEL ** -0.5),
        'router_group_b': nrm((DEPTH, N_EXPERT_GROUPS), 0.01),
        'router_expert_w': nrm((DEPTH, D_MODEL, N_EXPERTS), D_MODEL ** -0.5),
        'router_expert_b': nrm((DEPTH, N_EXPERTS), 0.01),
        'expert_w_gate': nrm((DEPTH, N_EXPERTS, D_MODEL, D_FF_EXPERT), D_MODEL ** -0.5),
        'expert_w_up': nrm((DEPTH, N_EXPERTS, D_MODEL, D_FF_EXPERT), D_MODEL ** -0.5),
        'expert_w_down': nrm((DEPTH, N_EXPERTS, D_FF_EXPERT, D_MODEL), D_FF_EXPERT ** -0.5),
        'g_final': gain((D_MODEL,)),
    }

def reference(x_prompt, x_sample, state_conv_a, state_pool, state_conv_c, g_mix, w_in, conv_a_w, pool_w,
              pool_scale, conv_c_w, conv_c_b, ln_c_g, ln_c_b, ln_d_g, ln_d_b, sgu_w, sgu_b, w_out, g_ffn,
              router_group_w, router_group_b, router_expert_w, router_expert_b, expert_w_gate, expert_w_up,
              expert_w_down, g_final):
    weights = (g_mix, w_in, conv_a_w, pool_w, pool_scale, conv_c_w, conv_c_b, ln_c_g, ln_c_b, ln_d_g, ln_d_b,
               sgu_w, sgu_b, w_out, g_ffn, router_group_w, router_group_b, router_expert_w, router_expert_b,
               expert_w_gate, expert_w_up, expert_w_down, g_final)
    bsz = x_prompt.shape[0]
    dt = x_prompt.dtype
    zero_a = jnp.zeros((DEPTH, bsz, CONV_A - 1, W_GROUP), dt)
    zero_p = jnp.zeros((DEPTH, bsz, POOL_STATE, W_GROUP), dt)
    zero_c = jnp.zeros((DEPTH, bsz, CONV_C - 1, W_GROUP), dt)
    y_prompt, new_conv_a_prompt, new_pool_prompt, new_conv_c_prompt, _ = _trunk(
        x_prompt, zero_a, zero_p, zero_c, 0, weights)
    y_sample, new_conv_a_sample, new_pool_sample, new_conv_c_sample, v_rows = _trunk(
        x_sample, state_conv_a, state_pool, state_conv_c, PAST_LEN, weights)
    chunk_v_sample = jnp.stack(v_rows)
    return (y_prompt, y_sample, new_conv_a_prompt, new_pool_prompt, new_conv_c_prompt,
            new_conv_a_sample, new_pool_sample, new_conv_c_sample, chunk_v_sample)


_drawn_inputs = setup_inputs


def setup_inputs(seed=0):
    import zlib

    import numpy as np

    out = dict(_drawn_inputs(seed))
    spreads = {}
    factors = {'ln_c_g': 3.148,
     'ln_c_b': 5.09,
     'ln_d_b': 3.043,
     'router_group_b': 35.867,
     'router_expert_b': 5.894}
    for name, (base, spread) in spreads.items():
        noise = np.random.default_rng([zlib.crc32(name.encode()), seed]).standard_normal(out[name].shape)
        drawn = base * np.exp(spread * noise) if base else spread * noise
        out[name] = jnp.asarray(drawn.astype(out[name].dtype))
    for name, factor in factors.items():
        out[name] = (out[name] * factor).astype(out[name].dtype)
    return out
```

```python
from contextlib import ExitStack

import concourse.bass as bass
from concourse import mybir

F32 = mybir.dt.float32
F32R = mybir.dt.float32r
I32 = mybir.dt.int32
U32 = mybir.dt.uint32
ALU = mybir.AluOpType
ACT = mybir.ActivationFunctionType
AX_X = mybir.AxisListType.X

P = 128
D = 1024
KC = D // P
NP = 1024
SB, ST = 8, 8
NS = SB * ST
NT = NP + NS
TILES = NT // P + 1
LAST = TILES - 1
W = 256
HA, HP, HC = 2, 15, 30
EPS = 1e-6
NE, NG, EG, FF = 32, 4, 8, 128
CAPB = -(-NT // P)
TCOLS = NE * CAPB
OVER = (2 * NT - 1) // P
NONE = 1 << 20
NPAR = 31 + 3 + 4

PIECES = [("cg0", 1280), ("ca0", 1024), ("cg1", 1408), ("ca1", 1152), ("v0", 1792), ("v1", 1920),
          ("du0", 1536), ("du1", 1664), ("p0", 768), ("p1", 896),
          ("ac0", 256), ("ax0", 512), ("ab0", 0), ("ac1", 384), ("ax1", 640), ("ab1", 128)]
NPIECE = len(PIECES)
ZS = [n for n, _ in PIECES if n[0] != "v"]
Z_BY = {"cg": "act", "ca": "dve", "du": "act", "p": "act", "ac": "act", "ax": "dve", "ab": "dve"}
Z_USER = [Z_BY[n[:-1]] for n in ZS]
RANGES = [(0, 384), (384, 768), (768, NT)]
LN_RANGES = [(0, 512), (512, 1024), (1024, NT)]

M_USES = [("par", "act"), ("stc", "act"), ("stpa", "act"), ("ws", "act")]
M_USES += [(f"v{i}", "act") for i in range(TILES)]
M_USES += [("cst0", "act"), ("cst1", "act")]
M_USES += [(f"sp{i}", "dve") for i in range(TILES)]
M_USES += [("pst0", "act")] + [(f"pm0{r}", "act") for r in range(3)] + [("pst1", "act")]
M_USES += [(f"pm1{r}", "act") for r in range(3)]
M_USES += [(f"mean{r}", "dve") for r in range(3)] + [("ast0", "act")]
M_USES += [(f"var{r}", "act") for r in range(3)] + [("ast1", "act")]


def _router_uses():
    out = []
    for i in range(TILES + 3):
        if 2 <= i < TILES + 2:
            out.append((f"lg{i - 2}", "dve"))
        if i >= 3:
            out.append((f"cum{i - 3}", "dve"))
    return out


M_USES += _router_uses()
M_AT = {n: i for i, (n, _) in enumerate(M_USES)}


def nth(users, n):
    return sum(u == users[n] for u in users[:n + 1])


class Chain:

    def __init__(self, eng, sem):
        self.eng, self.sem, self.n = eng, sem, {}

    def __call__(self, ins, sem=None):
        sem, key = (self.sem, "chain") if sem is None else (sem, id(sem))
        self.n[key] = self.n.get(key, 0) + 1
        ins.then_inc(sem, 1)
        self.eng.wait_ge(sem, self.n[key])


def rows(i):
    return NS if i == LAST else P


def piece_matmuls(pe, ps, ring, hT, slot, bank):
    first, last = (0, 0, 0), (KC - 1, 1, 0)
    for k in range(KC):
        for wpart, hpart in ((0, 0), (0, 1), (1, 0)):
            for r, (t0, t1) in enumerate(RANGES):
                mm = pe.matmul(ps[:, bank + r, 0:t1 - t0], ring[:, slot, wpart, k * P:(k + 1) * P],
                               hT[:, hpart, k, t0:t1], start=(k, wpart, hpart) == first,
                               stop=(k, wpart, hpart) == last)
    return mm


def build_layer(nc, a):
    with ExitStack() as ctx:
        def sb(name, shape, dt=F32):
            return ctx.enter_context(nc.sbuf_tensor("sb_" + name, shape, dt))

        def sem(name):
            return ctx.enter_context(nc.semaphore(name))

        WL, CL = 1232, HC + NP + SB * (HC + ST)
        o_hT = 0
        o_mix = o_hT + 2 * KC * NT * 4
        o_raw = o_mix + KC * NT * 4
        o_ring = o_raw + 2 * D * 4
        o_x1 = o_ring + 4 * D * 4
        o_w = o_x1 + TILES * D * 4
        o_uc = o_w + 3 * WL * 4
        o_end = o_uc + 2 * CL * 4
        lo, _ = nc.bump_sbuf(o_end)

        def at(name, shape, offset, dt=F32):
            return nc.alloc_sbuf_tensor_at("at_" + name, shape, dt, offset=lo + offset)

        hT = at("hT", [P, 2, KC, NT], o_hT, F32R)
        wo = at("wo", [P, 2, KC, D], o_hT, F32R)
        wexp = at("wexp", [P, 4, 3 * D], o_hT)
        xg = at("xg", [P, 4, D], o_hT + 4 * 3 * D * 4)
        mixT = at("mixT", [P, KC, NT], o_mix)
        hTm = at("hTm", [P, 2, KC, P], o_mix)
        outb = at("outb", [P, 2, D], o_mix + 8192)
        opair = at("opair", [P, 2, 2 * D], o_mix + 16384)
        raw = at("raw", [P, 2, D], o_raw)
        ring = at("ring", [P, 2, 2, D], o_ring, F32R)
        ovt = at("ovt", [1, 2 * OVER + 1], o_raw + 3712, I32)
        gcol = at("gcol", [P, OVER], o_raw + 3904, I32)
        scol = at("scol", [P, OVER], o_raw + 3968, I32)
        sg = at("sg", [P, 2, FF], o_raw)
        actv = at("actv", [P, 2, FF], o_raw + 1024)
        actT = at("actT", [P, 2, P], o_raw + 2048)
        ov = at("ov", [1, 2, NE], o_raw + 3072)
        ovi = at("ovi", [1, NE], o_raw + 3328, I32)
        ovb = at("ovb", [1, 3, OVER], o_raw + 3456)
        x1 = at("x1", [P, TILES, D], o_x1)
        wk = at("wk", [P, 3, WL], o_w)
        vall = at("vall", [P, TILES, W], o_w)
        uc = at("uc", [P, 2, CL], o_uc)
        lnsq = at("lnsq", [P, 2, 2, 512], o_uc)
        lnsq2 = at("lnsq2", [P, 2, NS], o_uc + 8192)
        h2T = at("h2T", [P, 2, KC, P], o_uc)
        st_rows = at("st_rows", [P, 4, W], o_mix + 6 * NT * 4)
        par_rows = at("par_rows", [P, W], o_mix + 7 * NT * 4)
        ws_rows = at("ws_rows", [P, NG, P], o_mix + 7 * NT * 4 + 1024)
        fill = at("fill", [P, TCOLS], o_mix + 5 * NT * 4, I32)
        lng = at("lng", [P, W], o_mix + 2 * NT * 4)
        lnb = at("lnb", [P, W], o_mix + 2 * NT * 4 + W * 4)
        tab = at("tab", [P, TCOLS], o_mix + 32768, I32)
        gidxs = at("gidxs", [P, TCOLS], o_uc + 8192, I32)
        otmp = at("otmp", [1, OVER, NE], o_w)
        otmp2 = at("otmp2", [1, OVER, NE], o_w + 2048)

        ident = sb("ident", [P, P])
        ones = sb("ones", [P, P])
        avg = sb("avg", [P, P])
        upper = sb("upper", [P, P])
        gain = sb("gain", [P, D])
        wsT = sb("wsT", [P, NG, P])
        wsb = sb("wsb", [NS, NG, NS])
        pw = sb("pw", [P, 2, P])
        rw = sb("rw", [P, KC, NG + NE])
        rb = sb("rb", [P, NG + NE])
        biasd = sb("biasd", [P, 2, P])
        par = sb("par", [P, 2, NPAR])
        hist_p = sb("hist_p", [P, 2, SB * HP])
        hist_a = sb("hist_a", [P, 2, SB * HA])
        iwin = sb("iwin", [P, 2])
        topm = sb("topm", [P, 1])
        icnt = sb("icnt", [P, 2, HP])
        sptmp = sb("sptmp", [P, 2, P])
        st6 = sb("st6", [P, TILES, 6])
        mv = sb("mv", [P, TILES, 2])
        rsd = sb("rsd", [P, TILES])
        ss = sb("ss", [P, 3, TILES])
        rs = sb("rs", [P, 3, TILES])
        mhalf = sb("mhalf", [P, TILES])
        epsc = sb("epsc", [P, 1])
        io4 = sb("io4", [P, NG])
        io32 = sb("io32", [P, NE])
        iob = sb("iob", [1, OVER])
        pid = sb("pid", [P, TILES, 2], I32)
        lg8 = sb("lg8", [P, 8])
        le = sb("le", [P, NE])
        m8 = sb("m8", [P, 8])
        i8 = sb("i8", [P, 8], U32)
        sel8 = sb("sel8", [P, 8])
        n8 = sb("n8", [P, 8])
        j8 = sb("j8", [P, 8], U32)
        goh = sb("goh", [P, NG])
        sc = sb("sc", [P, 8])
        acts = sb("acts", [P, 8])
        gidx = sb("gidx", [P, 1])
        gates = sb("gates", [P, TILES, 2])
        eidx = sb("eidx", [P, 2, 2])
        oh = sb("oh", [P, 2, 2, NE])
        msum = sb("msum", [P, 2, NE])
        carry = sb("carry", [P, NE])
        rank = sb("rank", [P, NE])
        rjunk = sb("rjunk", [P, NE])
        rk = sb("rk", [P, 2])
        stage = sb("stage", [P, 3, W])
        rki = sb("rki", [P, 2], I32)
        rlo = sb("rlo", [P, 2], I32)
        rhi = sb("rhi", [P, 2], I32)
        addr = sb("addr", [P, TILES, 2], I32)

        ps = ctx.enter_context(nc.psum_tensor("ps", [P, 8, 512], F32))

        hs = nc.dram_tensor("scratch_h", [NT, D], F32, kind="Internal").ap()
        table = nc.dram_tensor("scratch_table", [P * TCOLS, 1], I32, kind="Internal").ap()
        orow = nc.dram_tensor("scratch_out", [2 * NT, D], F32, kind="Internal").ap()

        s = {n: sem(n) for n in (
            "dve_chain", "act_chain", "pool_chain",
            "const_ready", "ident_ready", "gcol_ready", "scol_ready", "fill_ready", "zero_ready", "small_in", "ws_in", "late_in", "gain_mix_in",
            "gain_ffn_in", "gain_fin_in", "pw_in", "wsT_masked", "wsb_in", "table_filled",
            "sq_done", "rs_ready", "h_ready", "ht_T", "ht_hi", "ht_lo",
            "hi_ready", "lo_pool", "lo_dve", "piece_done", "zf_act", "zf_dve",
            "m_ready", "mf_act", "mf_dve", "uc_ready", "v_stats", "v_rsd", "v_norm",
            "v_ready", "v_out", "px_ready", "pd_ready", "ac_ready", "ua_ready",
            "tail_ready", "sp_done", "c_mean", "c_sq", "c_norm", "c_ready", "conv_ready", "mix_ready",
            "stage_out", "mh_hi", "mh_lo", "o_done", "x1_ready", "h2_ready",
            "t2_done", "h2T_ready", "lgmax", "lgexp", "selmax", "selexp", "m_onehot",
            "addr_ready", "placed", "tab_in", "idx_ready", "ov_ready", "xg_zero",
            "xt_done", "htm_ready", "gu_done", "sg_ready", "act_ready", "at_done", "att_ready",
            "d_done", "ob_act", "ob_dve", "moe_done", "y_sum", "y_done", "y_out")}
        x_in = [sem(f"x_in{i}") for i in range(TILES)]
        raw_in = [sem(f"raw_in{i}") for i in range(2)]
        w_in_sem = [sem(f"expert_in{i}") for i in range(4)]
        gath = [sem(f"gathered{i}") for i in range(4)]
        scat = [sem(f"scattered{i}") for i in range(2)]
        h2_stored = [sem(f"h2_stored{i}") for i in range(2)]
        pair_in = [sem(f"pair_in{i}") for i in range(2)]

        def wait_piece(eng, p):
            if PIECES[p][0][0] == "v":
                eng.wait_ge(s["m_ready"], M_AT[f"v{LAST}"] + 1)
            else:
                eng.wait_ge(s["piece_done"], p + 1 if p < 4 else p - 1)

        def m_bank(name):
            return 6 + M_AT[name] % 2

        def m_wait(eng, name):
            eng.wait_ge(s["m_ready"], M_AT[name] + 1)

        def z_bank(name):
            return 3 * (ZS.index(name) % 2)

        def z_parts(name, prompt, sample):
            b = z_bank(name)
            return [(prompt[:, 0:768].rearrange("p (r t) -> p r t", r=2), ps[:, b:b + 2, 0:384]),
                    (prompt[:, 768:1024], ps[:, b + 2, 0:256]),
                    (sample, ps[:, b + 2, 256:320].rearrange("p (b t) -> p b t", b=SB))]

        def mix_parts(c):
            return mixT[:, c, 0:NP], mixT[:, c, NP:NT].rearrange("p (b t) -> p b t", b=SB)

        def work(row, hist, shift=0):
            sm = row[:, hist + NP:hist + NP + SB * (hist + ST)].rearrange("p (b t) -> p b t", b=SB)
            return (row[:, hist - shift:hist - shift + NP], sm[:, :, hist - shift:hist - shift + ST])

        def mf_wait(eng, name):
            n = M_AT[name]
            eng.wait_ge(s["mf_" + M_USES[n][1]], nth([u for _, u in M_USES], n))

        def zf_wait(eng, name):
            n = ZS.index(name)
            eng.wait_ge(s["zf_" + Z_USER[n]], nth(Z_USER, n))

        def lap(i, j):
            return i + j // 4

        def result_out(eng, i):
            n = rows(i)
            eng.wait_ge(s["y_done"], i + 1)
            dst = a["y_sample"].rearrange("b t d -> (b t) d") if i == LAST \
                else a["y_prompt"][0, i * P:(i + 1) * P, :]
            eng.dma_start(dst, x1[0:n, i, :]).then_inc(s["y_out"], 16)

        block = ctx.enter_context(nc.Block())

        @block.sync
        def _(sp):
            def load_piece(p):
                if p >= 2:
                    sp.wait_ge(s["hi_ready"], p - 1)
                    if p - 2 < NPIECE:
                        sp.wait_ge(s["lo_pool"], p - 1)
                    else:
                        sp.wait_ge(s["lo_dve"], p - 1 - NPIECE)
                if p < NPIECE:
                    c = PIECES[p][1]
                    src = a["w_in"][0, :, c:c + P].rearrange("(q k) n -> q k n", k=KC)
                    dst = raw[:, p % 2, :].rearrange("q (k n) -> q k n", k=KC)
                else:
                    k = p - NPIECE
                    src, dst = a["w_out"][0, k * P:(k + 1) * P, :], raw[:, p % 2, :]
                sp.dma_start(dst, src).then_inc(raw_in[p % 2], 16)

            for i in range(TILES):
                src = a["x_sample"].rearrange("b t d -> (b t) d") if i == LAST \
                    else a["x_prompt"][0, i * P:(i + 1) * P, :]
                sp.dma_start(x1[0:rows(i), i, :], src).then_inc(x_in[i], 16)
                if i in (2, 4):
                    load_piece(i // 2 - 1)
                if i == 0:
                    sp.dma_start(gain[:], a["g_mix"].to_broadcast([P, D]))\
                        .then_inc(s["gain_mix_in"], 16)
            sp.wait_ge(s["fill_ready"], 1)
            sp.dma_start(table.rearrange("(p c) o -> p (c o)", p=P), fill[:])\
                .then_inc(s["table_filled"], 16)
            for p in range(2, NPIECE + KC):
                load_piece(p)
                if p == 4:
                    sp.wait_ge(s["h_ready"], TILES)
                    sp.dma_start(gain[:], a["g_ffn"].to_broadcast([P, D]))\
                        .then_inc(s["gain_ffn_in"], 16)
            for i in range(TILES):
                sp.wait_ge(s["h2_ready"], i + 1)
                sp.dma_start(hs[i * P:i * P + rows(i), :], wk[0:rows(i), i % 2, 0:D])\
                    .then_inc(h2_stored[i % 2], 16)
            sp.dma_start(gain[:], a["g_final"].rearrange("(o d) -> o d", o=1).to_broadcast([P, D]))\
                .then_inc(s["gain_fin_in"], 16)

            def load_expert(i, j, e):
                lap = i + j // 4
                for m, w in enumerate(("expert_w_gate", "expert_w_up", "expert_w_down")):
                    src = a[w][0, bass.ds(e, 1), :, :].rearrange("o (q k) f -> q (o k f)", q=P)
                    sp.dma_start(wexp[:, j % 4, m * D:(m + 1) * D], src)\
                        .then_inc(w_in_sem[j % 4], 16)

            def expert_block(i, j, e, first=False):
                if not first:
                    sp.wait_ge(s["d_done"], i * 4 + j - 3)
                load_expert(i, j, e)

            sp.wait_ge(s["o_done"], TILES)
            for j in range(4):
                expert_block(0, j, j, first=True)
            sp.wait_ge(s["placed"], 16 * 2 * TILES)
            sp.dma_start(tab[:], table.rearrange("(p c) o -> p (c o)", p=P)).then_inc(s["tab_in"], 16)
            with sp.Fori(1, NE // 4) as i:
                for j in range(4):
                    expert_block(i, j, i * 4 + j)
            sp.wait_ge(s["ov_ready"], 1)
            total = sp.value_load(ovt[0:1, 2 * OVER:2 * OVER + 1], min_val=0, max_val=OVER)
            with sp.Fori(0, OVER // 4) as i:
                for j in range(4):
                    with sp.If(i * 4 + j < total):
                        e = sp.value_load(ovt[0:1, bass.ds(i * 4 + j, 1)], min_val=0, max_val=NE - 1)
                        expert_block(i + NE // 4, j, e)
            sp.wait_ge(s["moe_done"], 1)
            for i in range(TILES):
                if i >= 2:
                    sp.wait_ge(s["y_sum"], i - 1)
                n = rows(i)
                src = orow[2 * i * P:2 * (i * P + n), :].rearrange("(t k) d -> t (k d)", k=2)
                sp.dma_start(opair[0:n, i % 2, :], src).then_inc(pair_in[i % 2], 16)
            sp.wait_ge(s["stage_out"], 16 * 7)
            sp.wait_ge(s["v_out"], 16)
            sp.wait_ge(s["y_out"], 16 * TILES)

        @block.scalar
        def _(act):
            do = Chain(act, s["act_chain"])
            A = nc.scalar.activation
            pools = a["state_pool"][0].rearrange("b r c -> (b r) c")
            half = SB // 2
            for h in range(2):
                act.dma_start(st_rows[0:half * HC, h, :],
                              a["state_conv_c"][0, h * half:(h + 1) * half].rearrange("b r c -> (b r) c"))\
                    .then_inc(s["small_in"], 16)
            act.dma_start(st_rows[0:SB * HP, 2, :], pools).then_inc(s["small_in"], 16)
            act.dma_start(st_rows[0:SB * HA, 3, :], a["state_conv_a"][0].rearrange("b r c -> (b r) c"))\
                .then_inc(s["small_in"], 16)
            for name, r0, n in (("conv_c_w", 0, 31), ("conv_a_w", 31, 3)):
                act.dma_start(par_rows[r0:r0 + n, :], a[name][0]).then_inc(s["small_in"], 16)
            for name, r0 in (("pool_scale", 34), ("conv_c_b", 35), ("ln_c_g", 36), ("ln_c_b", 37)):
                act.dma_start(par_rows[r0:r0 + 1, :], a[name]).then_inc(s["small_in"], 16)
            act.dma_start(ws_rows[:], a["sgu_w"][0].rearrange("h i j -> i h j")).then_inc(s["ws_in"], 16)

            def late_inputs():
                for n0, n, w, b in ((0, NG, "router_group_w", "router_group_b"),
                                    (NG, NE, "router_expert_w", "router_expert_b")):
                    act.dma_start(rw[:, :, n0:n0 + n], a[w][0].rearrange("(q k) n -> q k n", k=KC))\
                        .then_inc(s["late_in"], 16)
                    act.dma_start(rb[:, n0:n0 + n], a[b].to_broadcast([P, n])).then_inc(s["late_in"], 16)
                for h in range(NG):
                    act.dma_start(biasd[h % 2 * 64:h % 2 * 64 + 64, h // 2, :],
                                  a["sgu_b"][0, h:h + 1, :].to_broadcast([64, P]))\
                        .then_inc(s["late_in"], 16)
                act.dma_start(lng[:], a["ln_d_g"].to_broadcast([P, W])).then_inc(s["late_in"], 16)
                act.dma_start(lnb[:], a["ln_d_b"].to_broadcast([P, W])).then_inc(s["late_in"], 16)
                act.wait_ge(s["zero_ready"], 1)
                for g in range(4):
                    q = g % 2 * 64
                    act.dma_start(pw[q:q + 64, g // 2, q:q + 64], a["pool_w"][0, g])\
                        .then_inc(s["pw_in"], 16)

            def square(i, norm):
                n = rows(i)
                do(A(wk[0:n, 2, 0:D], x1[0:n, i, :], ACT.Square, accum_out=ss[0:n, norm, i:i + 1]),
                   s["sq_done"])

            def hT_hi(i):
                n = rows(i)
                act.wait_ge(s["ht_T"], i + 1)
                src = ps[:, 2 * (i % 3):2 * (i % 3) + 2, :].rearrange("p b (k t) -> p (b k) t", t=P)
                do(A(hT[:, 0, :, i * P:i * P + n], src[:, :, 0:n], ACT.Copy), s["ht_hi"])

            def m_out(name, dst, src):
                m_wait(act, name)
                for n, (x, y) in enumerate(zip(dst, src)):
                    do(A(x, y, ACT.Copy), s["mf_act"] if n == len(dst) - 1 else None)

            def part_hi(p):
                act.wait_ge(raw_in[p % 2], 16 * (p // 2 + 1))
                if p < NPIECE:
                    if p >= 2:
                        wait_piece(act, p - 2)
                    dst = ring[:, p % 2, 0, :]
                else:
                    if p == NPIECE:
                        wait_piece(act, NPIECE - 1)
                    dst = wo[:, 0, p - NPIECE, :]
                do(A(dst, raw[:, p % 2, :], ACT.Copy), s["hi_ready"])

            for i in range(TILES + 2):
                if i < TILES:
                    act.wait_ge(x_in[i], 16)
                    square(i, 0)
                if i == 1:
                    b6, b7 = ps[:, 6, :], ps[:, 7, :]
                    m_out("par", [par[:]],
                          [b6[:, 0:2 * 64].rearrange("p (c n) -> p c n", c=2)[:, :, 0:NPAR]])
                    smp = [uc[:, c, HC + NP:CL].rearrange("p (b r) -> p b r", b=SB)[:, :, 0:HC]
                           for c in range(2)]
                    m_out("stc", smp, [b7[:, c * 240:c * 240 + 240].rearrange("p (b r) -> p b r", b=SB)
                                       for c in range(2)])
                    m_out("stpa", [hist_p[:], hist_a[:]],
                          [b6[:, 0:240].rearrange("p (c n) -> p c n", c=2),
                           b6[:, 240:272].rearrange("p (c n) -> p c n", c=2)])
                    m_out("ws", [wsT[:]], [b7.rearrange("p (h i) -> p h i", h=NG)])
                    late_inputs()
                if i >= 2:
                    hT_hi(i - 2)
                if i in (5, 7):
                    part_hi((i - 5) // 2)
            act.wait_ge(s["wsT_masked"], 1)
            for b in range(SB):
                act.dma_start(wsb[b * ST:(b + 1) * ST, :, b * ST:(b + 1) * ST], wsT[0:ST, :, 0:ST])\
                    .then_inc(s["wsb_in"], 16)

            def sigmoid(p, c):
                name = f"cg{c}"
                wait_piece(act, p)
                parts = z_parts(name, *mix_parts(c))
                for n, (dst, src) in enumerate(parts):
                    do(A(dst, src, ACT.Sigmoid), s["zf_act"] if n == 2 else None)

            def empty(p, dst_prompt, dst_sample):
                name = PIECES[p][0]
                wait_piece(act, p)
                for n, (dst, src) in enumerate(z_parts(name, dst_prompt, dst_sample)):
                    do(A(dst, src, ACT.Copy), s["zf_act"] if n == 2 else None)

            stages = [0]

            def tail_copy(row, hist, keep):
                sm = row[:, hist + NP:hist + NP + SB * (hist + ST)].rearrange("p (b t) -> p b t", b=SB)
                dst = sptmp[:].rearrange("p c t -> p (c t)")[:, 0:SB * keep]
                do(A(dst.rearrange("p (b t) -> p b t", b=SB), sm[:, :, hist + ST - keep:hist + ST],
                     ACT.Copy), s["tail_ready"])

            def new_state(names, outs):
                if stages[0]:
                    act.wait_ge(s["stage_out"], stages[0])
                for c in range(2):
                    act.wait_ge(s["uc_ready"], c + 1)
                    tail_copy(uc[:, c, :], HC, HC)
                    b = ps[:, m_bank(names[c]), :]
                    m_out(names[c], [stage[0:n, m, c * P:(c + 1) * P] for m, (n, _, _) in enumerate(outs)],
                          [b[0:n, q:q + P] for n, q, _ in outs])
                for m, (n, _, dst) in enumerate(outs):
                    act.dma_start(dst, stage[0:n, m, :]).then_inc(s["stage_out"], 16)
                    stages[0] += 16

            sigmoid(0, 0)
            part_hi(2)
            part_hi(3)
            part_hi(4)
            sigmoid(2, 1)
            part_hi(5)
            for i in range(TILES):
                n = rows(i)
                name = f"v{i}"
                m_out(name, [vall[0:n, i, :]], [ps[0:n, m_bank(name), 0:W]])
            part_hi(6)
            part_hi(7)
            stc_out = a["new_conv_c_sample"][0].rearrange("(h b) r c -> h (b r) c", h=2)
            new_state(["cst0", "cst1"], [(HC, 0, a["new_conv_c_prompt"][0, 0]),
                                         (120, 128, stc_out[0]), (120, 256, stc_out[1])])
            part_hi(8)
            empty(6, *mix_parts(6))
            part_hi(9)
            empty(7, *mix_parts(7))
            act.wait_ge(s["v_ready"], 1)
            act.dma_start(a["chunk_v_sample"][0].rearrange("b t c -> (b t) c"), vall[0:NS, LAST, :])\
                .then_inc(s["v_out"], 16)
            part_hi(10)

            def pool_input(p, c):
                name = f"p{c}"
                sm = wk[:, 0, HP + NP:HP + NP + SB * (HP + ST)].rearrange("p (b t) -> p b t", b=SB)
                do(nc.scalar.mul(wk[:, 0, 0:HP], ones[:, 0:HP], 0.0))
                do(A(sm[:, :, 0:HP], hist_p[:, c, :].rearrange("p (b r) -> p b r", b=SB), ACT.Copy))
                empty(p, *work(wk[:, 0, :], HP))

            def pool_out(c):
                for r, (t0, t1) in enumerate(LN_RANGES):
                    name = f"pm{c}{r}"
                    m_wait(act, name)
                    do(A(mixT[:, 2 + c, t0:t1], ps[:, m_bank(name), 0:t1 - t0], ACT.Copy,
                         scale=par[:, c, 34:35]), s["mf_act"])

            m_wait(act, f"sp{LAST}")
            act.wait_ge(s["v_out"], 16)
            pool_input(8, 0)
            do(A(acts[:, 2:3], ones[:, 0:1], ACT.Copy), s["px_ready"])
            act.wait_ge(s["sp_done"], 1)
            tail_copy(wk[:, 0, :], HP, HP)
            pool_state = [(HP, 0, None), (SB * HP, 128, None)]

            def pool_state_part(c):
                name = f"pst{c}"
                if c == 0:
                    act.wait_ge(s["stage_out"], stages[0])
                b = ps[:, m_bank(name), :]
                m_out(name, [stage[0:n, m, c * P:(c + 1) * P] for m, (n, _, _) in enumerate(pool_state)],
                      [b[0:n, q:q + P] for n, q, _ in pool_state])
                if c == 1:
                    act.dma_start(a["new_pool_prompt"][0, 0], stage[0:HP, 0, :])\
                        .then_inc(s["stage_out"], 16)
                    act.dma_start(a["new_pool_sample"][0].rearrange("b r c -> (b r) c"),
                                  stage[0:SB * HP, 1, :]).then_inc(s["stage_out"], 16)
                    stages[0] += 32

            pool_state_part(0)
            part_hi(11)
            act.wait_ge(s["pd_ready"], 1)
            pool_input(9, 1)
            do(A(acts[:, 2:3], ones[:, 0:1], ACT.Copy), s["px_ready"])
            tail_copy(wk[:, 0, :], HP, HP)
            part_hi(12)
            pool_out(0)
            pool_state_part(1)
            part_hi(13)
            pool_out(1)

            def gate_c(p):
                ca = wk[:, 2, 0:NT]
                empty(p, ca[:, 0:NP], ca[:, NP:NT].rearrange("p (b t) -> p b t", b=SB))

            def a_hist(c):
                sm = wk[:, c, HA + NP:HA + NP + SB * (HA + ST)].rearrange("p (b t) -> p b t", b=SB)
                do(nc.scalar.mul(wk[:, c, 0:HA], ones[:, 0:HA], 0.0))
                do(A(sm[:, :, 0:HA], hist_a[:, c, :].rearrange("p (b r) -> p b r", b=SB), ACT.Copy))

            gate_c(10)
            act.wait_ge(s["pd_ready"], 2)
            a_hist(0)
            a_hist(1)
            do(A(acts[:, 2:3], ones[:, 0:1], ACT.Copy), s["ac_ready"])
            part_hi(14)

            def ln_square(r):
                t0, t1 = LN_RANGES[r]
                dst = lnsq2[:] if r == 2 else lnsq[:, r, :, :]
                act.wait_ge(s["c_mean"], r + 1)
                do(A(dst, mixT[:, 4:6, t0:t1], ACT.Square), s["c_sq"])

            def ln_sqrt(r):
                n = LN_RANGES[r][1] - LN_RANGES[r][0]
                name = f"var{r}"
                dst = lnsq2[:, 0, :] if r == 2 else lnsq[:, r, 0, :]
                m_wait(act, name)
                do(A(dst, ps[:, m_bank(name), 0:n], ACT.Sqrt, bias=epsc[:]), s["mf_act"])

            for r in range(3):
                ln_square(r)
            act.wait_ge(s["ua_ready"], 1)
            gate_c(13)
            do(A(acts[:, 2:3], ones[:, 0:1], ACT.Copy), s["ac_ready"])
            part_hi(15)
            act.wait_ge(s["stage_out"], stages[0])
            a_outs = [(HA, 0), (SB * HA, 128)]

            def a_state_part(c):
                name = f"ast{c}"
                b = ps[:, m_bank(name), :]
                m_out(name, [stage[0:n, m, c * P:(c + 1) * P] for m, (n, _) in enumerate(a_outs)],
                      [b[0:n, q:q + P] for n, q in a_outs])

            tail_copy(wk[:, 0, :], HA, HA)
            a_state_part(0)
            for r in range(3):
                ln_sqrt(r)
            for c in range(2):
                act.wait_ge(s["c_norm"], 1)
                do(A(mixT[:, 4 + c, :], mixT[:, 4 + c, :], ACT.Silu, bias=par[:, c, 37:38],
                     scale=par[:, c, 36:37]), s["c_ready"])
            act.wait_ge(s["ua_ready"], 2)
            tail_copy(wk[:, 1, :], HA, HA)
            a_state_part(1)
            act.dma_start(a["new_conv_a_prompt"][0, 0], stage[0:HA, 0, :]).then_inc(s["stage_out"], 16)
            act.dma_start(a["new_conv_a_sample"][0].rearrange("b r c -> (b r) c"),
                          stage[0:SB * HA, 1, :]).then_inc(s["stage_out"], 16)

            for p in range(NPIECE, NPIECE + KC):
                part_hi(p)

            def mix_hi(i):
                n = rows(i)
                if i == 0:
                    act.wait_ge(s["mix_ready"], 1)
                if i >= 2:
                    act.wait_ge(s["o_done"], i - 1)
                dst = ring[:, i % 2, 0, :].rearrange("p (k t) -> p k t", k=KC)
                do(A(dst[:, :, 0:n], mixT[:, :, i * P:i * P + n], ACT.Copy), s["mh_hi"])

            def h2T_out(i):
                n = rows(i)
                act.wait_ge(s["t2_done"], i + 1)
                if i >= 2:
                    m_wait(act, f"lg{i - 2}")
                src = ps[:, 4:6, :].rearrange("p b (k t) -> p (b k) t", t=P)
                do(A(h2T[:, i % 2, :, 0:n], src[:, :, 0:n], ACT.Copy), s["h2T_ready"])

            def router_exp(i):
                n = rows(i)
                act.wait_ge(s["lgmax"], i + 1)
                do(A(acts[0:n, 4:8], lg8[0:n, 0:NG], ACT.Exp, bias=sc[0:n, 0:1],
                     accum_out=acts[0:n, 0:1]), s["lgexp"])
                act.wait_ge(s["selmax"], i + 1)
                do(A(acts[0:n, 1:2], n8[0:n, 1:2], ACT.Exp, bias=sc[0:n, 1:2]), s["selexp"])

            mix_hi(0)
            for i in range(TILES + 2):
                if i + 1 < TILES:
                    mix_hi(i + 1)
                if i < TILES:
                    act.wait_ge(s["x1_ready"], i + 1)
                    square(i, 1)
                if i >= 2:
                    router_exp(i - 2)
                if 1 <= i <= TILES:
                    h2T_out(i - 1)

            def expert_hT(i, j):
                b = i * 4 + j
                act.wait_ge(s["xt_done"], b + 1)
                if not (isinstance(b, int) and b < 2):
                    act.wait_ge(s["gu_done"], b - 1)
                src = ps[:, 0:2, :].rearrange("p b (k t) -> p (b k) t", t=P)
                nc.scalar.activation(hTm[:, j % 2, :, :], src, ACT.Copy).then_inc(s["htm_ready"], 1)

            def expert_silu(i, j):
                b = i * 4 + j
                act.wait_ge(s["gu_done"], b + 1)
                if not (isinstance(b, int) and b < 2):
                    act.wait_ge(s["act_ready"], b - 1)
                nc.scalar.activation(sg[:, j % 2, :], ps[:, 2 + j % 2, 0:FF], ACT.Silu)\
                    .then_inc(s["sg_ready"], 1)

            def expert_actT(i, j):
                b = i * 4 + j
                act.wait_ge(s["at_done"], b + 1)
                if not (isinstance(b, int) and b < 2):
                    act.wait_ge(s["d_done"], b - 1)
                nc.scalar.activation(actT[:, j % 2, :], ps[:, 4, 0:P], ACT.Copy)\
                    .then_inc(s["att_ready"], 1)

            def expert_out(i, j):
                b = i * 4 + j
                act.wait_ge(s["d_done"], b + 1)
                if not (isinstance(b, int) and b < 2):
                    act.wait_ge(scat[j % 2], 16 * (i * 2 + j // 2))
                nc.scalar.activation(outb[:, j % 2, 0:512], ps[:, 5, :], ACT.Copy)\
                    .then_inc(s["ob_act"], 1)

            def step(i, j, first, last):
                if not last:
                    expert_hT(i, j + 1)
                expert_silu(i, j)
                if not first:
                    expert_actT(i, j - 1)
                    expert_out(i, j - 1)

            act.wait_ge(s["o_done"], TILES)
            expert_hT(0, 0)
            for j in range(4):
                step(0, j, first=j == 0, last=False)
            with act.Fori(1, NE // 4 - 1) as i:
                for j in range(4):
                    step(i, j, first=False, last=False)
            for j in range(4):
                step(NE // 4 - 1, j, first=False, last=j == 3)
            expert_actT(NE // 4 - 1, 3)
            expert_out(NE // 4 - 1, 3)
            act.wait_ge(s["ov_ready"], 1)
            total = act.value_load(ovt[0:1, 2 * OVER:2 * OVER + 1], min_val=0, max_val=OVER)
            with act.Fori(0, OVER // 4) as i:
                for j in range(4):
                    with act.If(i * 4 + j < total):
                        expert_hT(i + NE // 4, j)
                        expert_silu(i + NE // 4, j)
                        expert_actT(i + NE // 4, j)
                        expert_out(i + NE // 4, j)

            act.wait_ge(s["moe_done"], 1)
            for i in range(TILES):
                n = rows(i)
                act.wait_ge(s["y_sum"], i + 1)
                square(i, 2)
                if i >= 1:
                    result_out(act, i - 1)
            result_out(act, TILES - 1)

        @block.gpsimd
        def _(pool):
            do = Chain(pool, s["pool_chain"])
            g = nc.gpsimd
            do(g.memset(ident[:], 0.0))
            do(g.affine_select(out=ident[:], in_=ident[:], compare_op=ALU.not_equal, fill=1.0, base=0,
                               pattern=[[-1, P]], channel_multiplier=1))
            do(g.memset(mhalf[:], -0.5), s["ident_ready"])

            def inv_root(norm, i, n, scale):
                do(g.tensor_scalar(ss[0:n, norm, i:i + 1], ss[0:n, norm, i:i + 1], scale, EPS,
                                   ALU.mult, ALU.add))
                do(g.tensor_tensor(rs[0:n, norm, i:i + 1], ss[0:n, norm, i:i + 1], mhalf[0:n, 0:1],
                                   ALU.pow), s["rs_ready"])

            def rms(norm, i):
                pool.wait_ge(s["sq_done"], norm * TILES + i + 1)
                inv_root(norm, i, rows(i), 1.0 / D)

            rms(0, 0)
            rms(0, 1)
            do(g.memset(pw[:], 0.0), s["zero_ready"])
            rms(0, 2)
            do(g.memset(fill[:], NONE), s["fill_ready"])
            do(g.memset(wsb[:], 0.0))
            do(g.memset(ones[:], 1.0))
            do(g.memset(avg[:], 1.0 / W))
            do(g.affine_select(out=upper[:], in_=ones[:], compare_op=ALU.is_gt, fill=0.0, base=0,
                               pattern=[[1, P]], channel_multiplier=-1))
            rms(0, 3)
            for c in range(2):
                do(g.memset(uc[:, c, 0:HC], 0.0))
            do(g.memset(epsc[:], EPS))
            do(g.memset(lg8[:], -3.0e38))
            do(g.memset(mv[:], 1.0))
            do(g.memset(carry[:], 0.0))
            rms(0, 4)
            for c in range(2):
                for h in range(2):
                    do(g.memset(iwin[h * 64:h * 64 + 64, c:c + 1], 1.0 / (2 << (2 * c + h))))
                    do(g.memset(topm[h * 64:h * 64 + 64, :], float(h)))
            flt = dict(allow_small_or_imprecise_dtypes=True)
            do(g.iota(icnt[:], [[0, 2], [1, HP]], base=1, channel_multiplier=0, **flt))
            do(g.iota(io4[:], [[1, NG]], base=0, channel_multiplier=0, **flt))
            do(g.iota(io32[:], [[1, NE]], base=0, channel_multiplier=0, **flt))
            do(g.iota(iob[:], [[1, OVER]], base=0, channel_multiplier=0, **flt))
            do(g.iota(pid[:], [[2 * P, TILES], [1, 2]], base=0, channel_multiplier=2), s["const_ready"])
            rms(0, 5)
            mf_wait(pool, "ws")
            do(g.affine_select(out=wsT[:], in_=wsT[:], compare_op=ALU.is_ge, fill=0.0, base=0,
                               pattern=[[0, NG], [1, P]], channel_multiplier=-1), s["wsT_masked"])
            for i in range(6, TILES):
                rms(0, i)

            def part_lo(p):
                pool.wait_ge(s["hi_ready"], p + 1)
                if p >= 2:
                    wait_piece(pool, p - 2)
                do(g.tensor_tensor(ring[:, p % 2, 1, :], raw[:, p % 2, :],
                                   ring[:, p % 2, 0, :].bitcast(F32), ALU.subtract), s["lo_pool"])

            for p in range(8):
                part_lo(p)
            pool.wait_ge(s["v_stats"], 1)
            do(g.tensor_scalar(rsd[:], mv[:, :, 1], 1.0, EPS, ALU.mult, ALU.add))
            do(g.tensor_tensor(rsd[:], rsd[:], mhalf[:], ALU.pow), s["v_rsd"])
            pool.wait_ge(s["v_norm"], 1)
            pool.wait_ge(s["late_in"], 16 * 10)
            full = [P, LAST, W]
            do(g.tensor_tensor(vall[:, 0:LAST, :], vall[:, 0:LAST, :],
                               lng[:].unsqueeze(1).broadcast_to(full), ALU.mult))
            do(g.tensor_tensor(vall[:, 0:LAST, :], vall[:, 0:LAST, :],
                               lnb[:].unsqueeze(1).broadcast_to(full), ALU.add))
            do(g.tensor_tensor(vall[0:NS, LAST, :], vall[0:NS, LAST, :], lng[0:NS, :], ALU.mult))
            do(g.tensor_tensor(vall[0:NS, LAST, :], vall[0:NS, LAST, :], lnb[0:NS, :], ALU.add),
               s["v_ready"])
            for p in range(8, NPIECE):
                part_lo(p)

            pool.wait_ge(s["table_filled"], 16)
            for i in range(TILES + 3):
                if i < TILES:
                    rms(1, i)
                if i >= 3:
                    t = i - 3
                    n = rows(t)
                    pool.wait_ge(s["addr_ready"], t + 1)
                    for k in range(2):
                        g.indirect_dma_start(
                            table, bass.IndirectOffsetOnAxis(ap=addr[0:n, t, k:k + 1], axis=0),
                            pid[0:n, t, k:k + 1], None, bounds_check=P * TCOLS - 1, oob_is_err=False)\
                            .then_inc(s["placed"], 16)

            last_token, last_pair = pool.to_reg(NT - 1), pool.to_reg(2 * NT - 1)

            def gather(b, index):
                g.indirect_dma_start(xg[:, b % 4, :], None, hs,
                                     bass.IndirectOffsetOnAxis(ap=index, axis=0),
                                     bounds_check=last_token, oob_is_err=False)\
                    .then_inc(gath[b % 4], 16)

            def scatter(b, index):
                pool.wait_ge(s["ob_act"], b + 1)
                pool.wait_ge(s["ob_dve"], b + 1)
                g.indirect_dma_start(orow, bass.IndirectOffsetOnAxis(ap=index, axis=0),
                                     outb[:, b % 2, :], None, bounds_check=last_pair,
                                     oob_is_err=False).then_inc(scat[b % 2], 16)

            pool.wait_ge(s["o_done"], TILES)
            do(g.memset(xg[:].rearrange("p s d -> p (s d)"), 0.0), s["xg_zero"])
            for k in range(2):
                pool.wait_ge(h2_stored[k], 16 * ((TILES + 1 - k) // 2))
            pool.wait_ge(s["idx_ready"], 1)
            for b in range(-3, NE):
                if b + 3 < NE:
                    if b >= 1:
                        pool.wait_ge(s["xt_done"], b)
                    c = (b + 3) * CAPB
                    gather(b + 3, gidxs[:, c:c + 1])
                if b >= 1:
                    c = (b - 1) * CAPB
                    scatter(b - 1, tab[:, c:c + 1])
            c = (NE - 1) * CAPB
            scatter(NE - 1, tab[:, c:c + 1])
            pool.wait_ge(s["ov_ready"], 1)
            total = pool.value_load(ovt[0:1, 2 * OVER:2 * OVER + 1], min_val=0, max_val=OVER)
            for o in range(OVER):
                b = NE + o
                with pool.If(total > o):
                    col = pool.value_load(ovt[0:1, OVER + o:OVER + o + 1], min_val=0,
                                          max_val=TCOLS - 1)
                    do(g.tensor_copy(gcol[:, o:o + 1], gidxs[:, bass.ds(col, 1)]), s["gcol_ready"])
                    do(g.tensor_copy(scol[:, o:o + 1], tab[:, bass.ds(col, 1)]), s["scol_ready"])
                    pool.wait_ge(s["xt_done"], b - 3)
                    gather(b, gcol[:, o:o + 1])
                    scatter(b, scol[:, o:o + 1])
                    pool.wait_ge(scat[b % 2], 16 * (b // 2 + 1))
            for k in range(2):
                pool.wait_ge(scat[k], 16 * (NE // 2))
            do(g.memset(gcol[:, 0:1], 0), s["moe_done"])
            for i in range(TILES):
                rms(2, i)

        @block.vector
        def _(dve):
            do = Chain(dve, s["dve_chain"])
            v = nc.vector
            stt, tt, ts = v.scalar_tensor_tensor, v.tensor_tensor, v.tensor_scalar

            def normed(i, norm, done):
                n = rows(i)
                do(stt(wk[0:n, i % 2, 0:D].rearrange("p (k q) -> p q k", k=KC),
                       x1[0:n, i, :].rearrange("p (q k) -> p q k", k=KC), rs[0:n, norm, i:i + 1],
                       gain[0:n, :].rearrange("p (q k) -> p q k", k=KC), ALU.mult, ALU.mult), s[done])

            def hT_lo(i):
                n = rows(i)
                dve.wait_ge(s["ht_hi"], i + 1)
                src = ps[:, 2 * (i % 3):2 * (i % 3) + 2, :].rearrange("p b (k t) -> p (b k) t", t=P)
                do(tt(hT[:, 1, :, i * P:i * P + n], src[:, :, 0:n],
                      hT[:, 0, :, i * P:i * P + n].bitcast(F32), ALU.subtract), s["ht_lo"])

            dve.wait_ge(s["gain_mix_in"], 16)
            for i in range(TILES + 2):
                if i < TILES:
                    dve.wait_ge(s["rs_ready"], i + 1)
                    if i >= 2:
                        dve.wait_ge(s["ht_T"], i - 1)
                    normed(i, 0, "h_ready")
                if i >= 2:
                    hT_lo(i - 2)
            dve.wait_ge(s["const_ready"], 1)
            for c in range(2):
                for h in range(2):
                    q = slice(h * 64, h * 64 + 64)
                    do(ts(icnt[q, c, :], icnt[q, c, :], float(2 << (2 * c + h)), None, ALU.min))
            do(v.reciprocal(icnt[:], icnt[:]))

            def glu(c, p):
                name = f"ca{c}"
                wait_piece(dve, p)
                mf_wait(dve, "stc")
                zf_wait(dve, f"cg{c}")
                gp = z_parts(name, *mix_parts(c))
                for n, (dst, src) in enumerate(z_parts(name, *work(uc[:, c, :], HC))):
                    do(tt(dst, src, gp[n][0], ALU.mult), s["zf_dve"] if n == 2 else None)
                do(v.tensor_copy(sc[:, 7:8], ones[:, 0:1]), s["uc_ready"])

            def taps_c(c, k0, k1):
                for k in range(k0, k1):
                    xs = work(uc[:, c, :], HC, HC - k)
                    for y, x in zip(mix_parts(4 + c), xs):
                        if k == 0:
                            do(ts(y, x, par[:, c, 0:1], par[:, c, 35:36], ALU.mult, ALU.add))
                        else:
                            do(stt(y, x, par[:, c, k:k + 1], y, ALU.mult, ALU.add))

            glu(0, 1)
            dve.wait_ge(s["table_filled"], 16)
            mf_wait(dve, "par")
            taps_c(0, 0, 16)
            glu(1, 3)
            taps_c(0, 16, 31)
            mf_wait(dve, f"v{LAST}")
            for i in range(TILES):
                n = rows(i)
                do(v.bn_stats(st6[0:n, i, :], vall[0:n, i, :]))
            for i in range(TILES):
                n = rows(i)
                do(v.bn_aggr(mv[0:n, i, :], st6[0:n, i, :]), s["v_stats"] if i == LAST else None)
            dve.wait_ge(s["v_rsd"], 1)
            for i in range(TILES):
                n = rows(i)
                do(ts(vall[0:n, i, :], vall[0:n, i, :], mv[0:n, i, 0:1], rsd[0:n, i:i + 1],
                      ALU.subtract, ALU.mult), s["v_norm"] if i == LAST else None)
            taps_c(1, 0, 20)
            wait_piece(dve, 7)
            dve.wait_ge(s["late_in"], 16 * 10)
            zf_wait(dve, "du1")
            for i in range(TILES):
                name = f"sp{i}"
                m_wait(dve, name)
                b = ps[:, m_bank(name), :]
                if i < LAST:
                    do(tt(sptmp[:], b[:, 0:W].rearrange("p (c t) -> p c t", c=2), biasd[:], ALU.add),
                       s["mf_dve"])
                else:
                    for c in range(2):
                        do(tt(sptmp[:, c, 0:NS].rearrange("p (b t) -> p b t", b=SB),
                              b[:, c * P:c * P + NS].rearrange("p (b t) -> p b t", b=SB),
                              biasd[:, c, 0:ST].unsqueeze(1).broadcast_to([P, SB, ST]), ALU.add),
                           s["mf_dve"] if c == 1 else None)
                m = mixT[:, 6:8, i * P:i * P + rows(i)]
                do(tt(m, m, sptmp[:, :, 0:rows(i)], ALU.mult), s["sp_done"] if i == LAST else None)
            taps_c(1, 20, 31)
            do(v.tensor_copy(sc[:, 7:8], ones[:, 0:1]), s["conv_ready"])

            def pooled(c):
                n = HP + NP + SB * (HP + ST)
                row = [wk[:, r, :] for r in range(3)]
                dve.wait_ge(s["px_ready"], c + 1)
                if c == 1:
                    m_wait(dve, "pm02")
                steps = [(0, 1)] if c == 0 else [(0, 1), (1, 2), (2, 4)]
                src, lo_, at_ = row[0], 0, 0
                turn = [row[1], row[2]] if c == 0 else [row[2], row[1], row[2], row[1]]
                for k, shift in steps:
                    dst = turn[at_]
                    at_ += 1
                    lo_ += shift
                    do(tt(dst[:, lo_:n], src[:, lo_:n], src[:, lo_ - shift:n - shift], ALU.add))
                    src = dst
                shift = 2 if c == 0 else 8
                dst = turn[at_]
                do(stt(dst[:, HP:n], src[:, HP - shift:n - shift], topm[:, 0:1], src[:, HP:n],
                       ALU.mult, ALU.add))
                d = row[1 + c]
                for y, x, z in zip(work(d, HP), work(dst, HP), work(row[0], HP)):
                    if y.shape == [P, NP] or len(y.shape) == 2:
                        do(tt(y[:, 0:HP], x[:, 0:HP], icnt[:, c, :], ALU.mult))
                        do(tt(y[:, 0:HP], y[:, 0:HP], z[:, 0:HP], ALU.subtract))
                        y, x, z = y[:, HP:], x[:, HP:], z[:, HP:]
                    do(stt(y, x, iwin[:, c:c + 1], z, ALU.mult, ALU.subtract))
                do(v.tensor_copy(sc[:, 7:8], ones[:, 0:1]), s["pd_ready"])

            pooled(0)
            pooled(1)

            def a_input(c, p):
                name = f"ax{c}"
                wait_piece(dve, p)
                dve.wait_ge(s["ac_ready"], c + 1)
                ca = wk[:, 2, 0:NT]
                gp = z_parts(name, ca[:, 0:NP], ca[:, NP:NT].rearrange("p (b t) -> p b t", b=SB))
                for n, (dst, src) in enumerate(z_parts(name, *work(wk[:, c, :], HA))):
                    do(tt(dst, src, gp[n][0], ALU.mult), s["zf_dve"] if n == 2 else None)
                do(v.tensor_copy(sc[:, 7:8], ones[:, 0:1]), s["ua_ready"])

            def a_taps(c):
                for k in range(3):
                    w = par[:, c, 31 + k:32 + k]
                    for y, x in zip(mix_parts(c), work(wk[:, c, :], HA, HA - k)):
                        if k == 0:
                            do(ts(y, x, w, None, ALU.mult))
                        else:
                            do(stt(y, x, w, y, ALU.mult, ALU.add))

            def a_gate(c, p):
                name = f"ab{c}"
                wait_piece(dve, p)
                for n, (dst, src) in enumerate(z_parts(name, *mix_parts(c))):
                    do(tt(dst, dst, src, ALU.mult), s["zf_dve"] if n == 2 else None)

            def c_mean(r):
                t0, t1 = LN_RANGES[r]
                name = f"mean{r}"
                m_wait(dve, name)
                y = mixT[:, 4:6, t0:t1]
                mean = ps[:, m_bank(name), 0:t1 - t0].unsqueeze(1).broadcast_to([P, 2, t1 - t0])
                do(tt(y, y, mean, ALU.subtract), s["mf_dve"])
                do(v.tensor_copy(sc[:, 7:8], ones[:, 0:1]), s["c_mean"])

            def c_norm(r):
                t0, t1 = LN_RANGES[r]
                mf_wait(dve, f"var{r}")
                d = lnsq2[:, 0, :] if r == 2 else lnsq[:, r, 0, :]
                y = mixT[:, 4:6, t0:t1]
                do(v.reciprocal(d, d))
                do(tt(y, y, d.unsqueeze(1).broadcast_to([P, 2, t1 - t0]), ALU.mult),
                   s["c_norm"] if r == 2 else None)

            a_input(0, 11)
            a_taps(0)
            a_gate(0, 12)
            for r in range(3):
                c_mean(r)
            for r in range(3):
                c_norm(r)
            a_input(1, 14)
            a_taps(1)
            a_gate(1, 15)
            do(v.tensor_copy(sc[:, 7:8], ones[:, 0:1]), s["mix_ready"])

            for k in range(KC):
                dve.wait_ge(s["hi_ready"], NPIECE + k + 1)
                do(tt(wo[:, 1, k, :], raw[:, k % 2, :], wo[:, 0, k, :].bitcast(F32), ALU.subtract),
                   s["lo_dve"])

            def mix_lo(i):
                n = rows(i)
                dve.wait_ge(s["mh_hi"], i + 1)
                hi, low = (ring[:, i % 2, m, :].rearrange("p (k t) -> p k t", k=KC)[:, :, 0:n]
                           for m in range(2))
                do(tt(low, mixT[:, :, i * P:i * P + n], hi.bitcast(F32), ALU.subtract), s["mh_lo"])

            def residual(i):
                n = rows(i)
                dve.wait_ge(s["o_done"], i + 1)
                b = 2 * (i % 2)
                do(tt(x1[0:n, i, :].rearrange("p (r d) -> p r d", r=2),
                      x1[0:n, i, :].rearrange("p (r d) -> p r d", r=2), ps[0:n, b:b + 2, :], ALU.add),
                   s["x1_ready"])

            def route(i):
                n = rows(i)
                q = slice(0, n)
                name = f"lg{i}"
                z = i % 2
                m_wait(dve, name)
                b = ps[q, m_bank(name), :]
                do(tt(lg8[q, 0:NG], b[:, 0:NG], rb[q, 0:NG], ALU.add))
                do(tt(le[q, :], b[:, NG:NG + NE], rb[q, NG:NG + NE], ALU.add), s["mf_dve"])
                do(v.max(m8[q, :], lg8[q, :]))
                do(ts(sc[q, 0:1], m8[q, 0:1], -1.0, None, ALU.mult), s["lgmax"])
                do(v.max_index(i8[q, :], m8[q, :], lg8[q, :]))
                do(v.tensor_copy(gidx[q, :], i8[q, 0:1]))
                do(ts(goh[q, :], io4[q, :], gidx[q, :], None, ALU.is_equal))
                do(ts(sel8[q, :], le[q, 0:EG], goh[q, 0:1], None, ALU.mult))
                for m in range(1, NG):
                    do(stt(sel8[q, :], le[q, m * EG:(m + 1) * EG], goh[q, m:m + 1], sel8[q, :],
                           ALU.mult, ALU.add))
                do(v.max(n8[q, :], sel8[q, :]))
                do(ts(sc[q, 1:2], n8[q, 0:1], -1.0, None, ALU.mult), s["selmax"])
                do(v.max_index(j8[q, :], n8[q, :], sel8[q, :]))
                do(ts(sc[q, 2:3], gidx[q, :], float(EG), None, ALU.mult))
                do(ts(eidx[q, z, :], j8[q, 0:2], sc[q, 2:3], None, ALU.add))
                for k in range(2):
                    do(ts(oh[q, z, k, :], io32[q, :], eidx[q, z, k:k + 1], None, ALU.is_equal))
                do(tt(msum[q, z, :], oh[q, z, 0, :], oh[q, z, 1, :], ALU.add), s["m_onehot"])
                dve.wait_ge(s["lgexp"], i + 1)
                dve.wait_ge(s["selexp"], i + 1)
                do(ts(sc[q, 3:4], acts[q, 1:2], 1.0, None, ALU.add))
                do(ts(sc[q, 4:5], acts[q, 0:1], sc[q, 3:4], None, ALU.mult))
                do(v.reciprocal(gates[q, i, 0:1], sc[q, 4:5]))
                do(ts(gates[q, i, 1:2], acts[q, 1:2], gates[q, i, 0:1], None, ALU.mult))

            def places(i):
                n = rows(i)
                q = slice(0, n)
                name = f"cum{i}"
                z = i % 2
                m_wait(dve, name)
                b = ps[:, m_bank(name), :]
                do(tt(rank[q, :], b[q, 0:NE], carry[q, :], ALU.add))
                do(tt(carry[:], b[:, NE:2 * NE], carry[:], ALU.add), s["mf_dve"])
                for k in range(2):
                    do(stt(rjunk[q, :], rank[q, :], 0.0, oh[q, z, k, :], ALU.add, ALU.mult,
                           accum_out=rk[q, k:k + 1]))
                do(v.tensor_copy(rki[q, :], rk[q, :]))
                do(ts(rlo[q, :], rki[q, :], P - 1, None, ALU.bitwise_and))
                do(ts(rhi[q, :], rki[q, :], 7, None, ALU.logical_shift_right))
                do(stt(rhi[q, :], rlo[q, :], float(TCOLS), rhi[q, :], ALU.mult, ALU.add))
                do(stt(addr[q, i, :], eidx[q, z, :], float(CAPB), rhi[q, :], ALU.mult, ALU.add),
                   s["addr_ready"])

            mix_lo(0)
            dve.wait_ge(s["gain_ffn_in"], 16)
            for i in range(TILES + 3):
                if i + 1 < TILES:
                    mix_lo(i + 1)
                if i < TILES:
                    residual(i)
                    dve.wait_ge(s["rs_ready"], TILES + i + 1)
                    if i >= 2:
                        dve.wait_ge(s["t2_done"], i - 1)
                        dve.wait_ge(h2_stored[i % 2], 16 * (i // 2))
                    normed(i, 1, "h2_ready")
                if 2 <= i < TILES + 2:
                    route(i - 2)
                if i >= 3:
                    places(i - 3)

            dve.wait_ge(s["tab_in"], 16)
            do(ts(gidxs[:], tab[:], 1, None, ALU.logical_shift_right), s["idx_ready"])
            n_e, incl = ov[:, 0, :], ov[:, 1, :]
            do(ts(ovi[:], carry[0:1, :], float(P - 1), None, ALU.add))
            do(ts(ovi[:], ovi[:], 7, None, ALU.logical_shift_right))
            do(ts(n_e, ovi[:], 1.0, -1.0, ALU.max, ALU.add))
            do(v.tensor_tensor_scan(incl, ones[0:1, 0:NE], n_e, 0.0, ALU.mult, ALU.add))
            grid = [1, OVER, NE]
            for k in range(2):
                dve.wait_ge(h2_stored[k], 16 * ((TILES + 1 - k) // 2))
            do(tt(otmp[:], incl.unsqueeze(1).broadcast_to(grid), iob[:].unsqueeze(2).broadcast_to(grid),
                  ALU.is_le))
            do(v.tensor_reduce(ovb[:, 0, :], otmp[:], AX_X, ALU.add))
            do(tt(otmp2[:], otmp[:], n_e.unsqueeze(1).broadcast_to(grid), ALU.mult))
            do(v.tensor_reduce(ovb[:, 1, :], otmp2[:], AX_X, ALU.add))
            do(ts(ovb[:, 0, :], ovb[:, 0, :], float(NE - 1), None, ALU.min))
            do(v.tensor_copy(ovt[:, 0:OVER], ovb[:, 0, :]))
            do(tt(ovb[:, 2, :], iob[:], ovb[:, 1, :], ALU.subtract))
            do(stt(ovb[:, 2, :], ovb[:, 0, :], float(CAPB), ovb[:, 2, :], ALU.mult, ALU.add))
            do(ts(ovb[:, 2, :], ovb[:, 2, :], 1.0, float(TCOLS - 1), ALU.add, ALU.min))
            do(v.tensor_copy(ovt[:, OVER:2 * OVER], ovb[:, 2, :]))
            do(v.tensor_copy(ovt[:, 2 * OVER:2 * OVER + 1], incl[:, NE - 1:NE]), s["ov_ready"])

            def expert_act(i, j):
                b = i * 4 + j
                dve.wait_ge(s["sg_ready"], b + 1)
                if not (isinstance(b, int) and b < 2):
                    dve.wait_ge(s["at_done"], b - 1)
                v.tensor_tensor(actv[:, j % 2, :], sg[:, j % 2, :], ps[:, 2 + j % 2, FF:2 * FF],
                                ALU.mult).then_inc(s["act_ready"], 1)

            def expert_out(i, j):
                b = i * 4 + j
                dve.wait_ge(s["d_done"], b + 1)
                if not (isinstance(b, int) and b < 2):
                    dve.wait_ge(scat[j % 2], 16 * (i * 2 + j // 2))
                v.tensor_copy(outb[:, j % 2, 512:D], ps[:, 6, :]).then_inc(s["ob_dve"], 1)

            def step(i, j, first):
                expert_act(i, j)
                if not first:
                    expert_out(i, j - 1)

            for j in range(4):
                step(0, j, first=j == 0)
            with dve.Fori(1, NE // 4) as i:
                for j in range(4):
                    step(i, j, first=False)
            expert_out(NE // 4 - 1, 3)
            total = dve.value_load(ovt[0:1, 2 * OVER:2 * OVER + 1], min_val=0, max_val=OVER)
            with dve.Fori(0, OVER // 4) as i:
                for j in range(4):
                    with dve.If(i * 4 + j < total):
                        expert_act(i + NE // 4, j)
                        expert_out(i + NE // 4, j)

            dve.wait_ge(s["moe_done"], 1)
            dve.wait_ge(s["gain_fin_in"], 16)
            for i in range(TILES + 1):
                if i < TILES:
                    n = rows(i)
                    dve.wait_ge(pair_in[i % 2], 16 * (i // 2 + 1))
                    for k in range(2):
                        do(stt(x1[0:n, i, :], opair[0:n, i % 2, k * D:(k + 1) * D],
                               gates[0:n, i, k:k + 1], x1[0:n, i, :], ALU.mult, ALU.add),
                           s["y_sum"] if k == 1 else None)
                if i >= 1:
                    m = i - 1
                    n = rows(m)
                    dve.wait_ge(s["rs_ready"], 2 * TILES + m + 1)
                    do(stt(x1[0:n, m, :], x1[0:n, m, :], rs[0:n, 2, m:m + 1], gain[0:n, :], ALU.mult,
                           ALU.mult), s["y_done"])

        @block.tensor
        def _(pe):
            def m_open(name):
                n = M_AT[name]
                if n >= 2:
                    mf_wait(pe, M_USES[n - 2][0])
                return ps[:, m_bank(name), :]

            def transposes(i, banks):
                n = rows(i)
                for k in range(KC):
                    mm = pe.transpose(ps[:, banks + k // 4, k % 4 * P:k % 4 * P + n],
                                      wk[0:n, i % 2, k * P:(k + 1) * P], ident[0:n, 0:n])
                return mm

            pe.wait_ge(s["ident_ready"], 1)
            pe.wait_ge(s["small_in"], 16 * 10)
            b = m_open("par")
            for c in range(2):
                mm = pe.transpose(b[:, c * 64:c * 64 + NPAR], par_rows[0:NPAR, c * P:(c + 1) * P],
                                  ident[0:NPAR, 0:NPAR])
            mm.then_inc(s["m_ready"], 1)
            b = m_open("stc")
            for c in range(2):
                for h in range(2):
                    q = (2 * c + h) * 120
                    mm = pe.transpose(b[:, q:q + 120], st_rows[0:120, h, c * P:(c + 1) * P],
                                      ident[0:120, 0:120])
            mm.then_inc(s["m_ready"], 1)
            b = m_open("stpa")
            for r, n, q in ((2, SB * HP, 0), (3, SB * HA, 240)):
                for c in range(2):
                    mm = pe.transpose(b[:, q + c * n:q + (c + 1) * n], st_rows[0:n, r, c * P:(c + 1) * P],
                                      ident[0:n, 0:n])
            mm.then_inc(s["m_ready"], 1)
            b = m_open("ws")
            pe.wait_ge(s["ws_in"], 16)
            for h in range(NG):
                mm = pe.transpose(b[:, h * P:(h + 1) * P], ws_rows[:, h, :], ident[:])
            mm.then_inc(s["m_ready"], 1)

            for i in range(TILES):
                pe.wait_ge(s["h_ready"], i + 1)
                if i >= 3:
                    pe.wait_ge(s["ht_lo"], i - 2)
                transposes(i, 2 * (i % 3)).then_inc(s["ht_T"], 1)

            def z(p):
                name = PIECES[p][0]
                n = ZS.index(name)
                pe.wait_ge(s["lo_pool"], p + 1)
                if p == 0:
                    pe.wait_ge(s["ht_lo"], TILES)
                if n >= 2:
                    user = Z_USER[n - 2]
                    pe.wait_ge(s["zf_" + user], nth(Z_USER, n - 2))
                piece_matmuls(pe, ps, ring, hT, p % 2, z_bank(name)).then_inc(s["piece_done"], 1)

            for p in range(4):
                z(p)
            pe.wait_ge(s["lo_pool"], 6)
            for i in range(TILES):
                n = rows(i)
                b = m_open(f"v{i}")
                for k in range(KC):
                    for hpart, wpart in ((0, 0), (0, 1), (1, 0)):
                        mm = pe.matmul(b[0:n, 0:W].rearrange("p (s c) -> p s c", s=2),
                                       hT[:, hpart, k, i * P:i * P + n],
                                       ring[:, :, wpart, k * P:(k + 1) * P],
                                       start=(k, hpart, wpart) == (0, 0, 0),
                                       stop=(k, hpart, wpart) == (KC - 1, 1, 0))
                mm.then_inc(s["m_ready"], 1)

            def tails(name, row, hist, keep, halves=1):
                b = m_open(name)
                pe.transpose(b[0:keep, 0:P], row[:, hist + NP - keep:hist + NP], ident[:])
                tail = sptmp[:].rearrange("p c t -> p (c t)")
                pe.wait_ge(s["tail_ready"], [n for n, _ in M_USES if "st" in n and n[-1] in "01"]
                           .index(name) + 1)
                n = SB * keep // halves
                for h in range(halves):
                    mm = pe.transpose(b[0:n, P * (h + 1):P * (h + 2)], tail[:, h * n:(h + 1) * n],
                                      ident[:])
                mm.then_inc(s["m_ready"], 1)

            for c in range(2):
                pe.wait_ge(s["uc_ready"], c + 1)
                tails(f"cst{c}", uc[:, c, :], HC, HC, halves=2)
            z(6)
            z(7)
            pe.wait_ge(s["v_ready"], 1)
            pe.wait_ge(s["wsb_in"], 16 * SB)
            for i in range(TILES):
                n = rows(i)
                b = m_open(f"sp{i}")
                for h in range(NG):
                    mm = pe.matmul(b[h % 2 * 64:h % 2 * 64 + 64, h // 2 * P:h // 2 * P + n],
                                   vall[0:n, i, h * 64:(h + 1) * 64],
                                   wsT[:, h, :] if i < LAST else wsb[:, h, :], start=True, stop=True)
                mm.then_inc(s["m_ready"], 1)
            z(8)
            z(9)
            pe.wait_ge(s["px_ready"], 1)
            tails("pst0", wk[:, 0, :], HP, HP)
            z(10)

            def pool_product(c):
                pe.wait_ge(s["pd_ready"], c + 1)
                pe.wait_ge(s["pw_in"], 16 * 4)
                prompt, sample = work(wk[:, 1 + c, :], HP)
                for r, (t0, t1) in enumerate(LN_RANGES):
                    b = m_open(f"pm{c}{r}")
                    x = sample if r == 2 else prompt[:, t0:t1]
                    y = b[:, 0:NS].rearrange("p (b t) -> p b t", b=SB) if r == 2 else b
                    pe.matmul(y, pw[:, c, :], x, start=True, stop=True).then_inc(s["m_ready"], 1)

            pool_product(0)
            pe.wait_ge(s["px_ready"], 2)
            tails("pst1", wk[:, 0, :], HP, HP)
            z(11)
            pool_product(1)
            z(12)

            def over_channels(what, r, src):
                n = LN_RANGES[r][1] - LN_RANGES[r][0]
                b = m_open(f"{what}{r}")
                for c in range(2):
                    mm = pe.matmul(b[:, 0:n], avg[:], src[:, c, :], start=c == 0, stop=c == 1)
                mm.then_inc(s["m_ready"], 1)

            pe.wait_ge(s["conv_ready"], 1)
            for r, (t0, t1) in enumerate(LN_RANGES):
                over_channels("mean", r, mixT[:, 4:6, t0:t1])
            z(13)
            pe.wait_ge(s["ua_ready"], 1)
            tails("ast0", wk[:, 0, :], HA, HA)
            for r in range(3):
                pe.wait_ge(s["c_sq"], r + 1)
                over_channels("var", r, lnsq2[:] if r == 2 else lnsq[:, r, :, :])
            z(14)
            z(15)
            pe.wait_ge(s["ua_ready"], 2)
            tails("ast1", wk[:, 1, :], HA, HA)

            def project(i):
                n = rows(i)
                b = 2 * (i % 2)
                pe.wait_ge(s["mh_lo"], i + 1)
                if i >= 2:
                    pe.wait_ge(s["x1_ready"], i - 1)
                for k in range(KC):
                    if i == 0:
                        pe.wait_ge(s["lo_dve"], k + 1)
                    for mpart, wpart in ((0, 0), (0, 1), (1, 0)):
                        for r in range(2):
                            mm = pe.matmul(ps[0:n, b + r, :], ring[:, i % 2, mpart, k * P:k * P + n],
                                           wo[:, wpart, k, r * 512:(r + 1) * 512],
                                           start=(k, mpart, wpart) == (0, 0, 0),
                                           stop=(k, mpart, wpart) == (KC - 1, 1, 0))
                mm.then_inc(s["o_done"], 1)

            pe.wait_ge(s["mix_ready"], 1)
            for i in range(TILES + 3):
                if i < TILES:
                    project(i)
                if 2 <= i < TILES + 2:
                    t = i - 2
                    n = rows(t)
                    b = m_open(f"lg{t}")
                    pe.wait_ge(s["h2T_ready"], t + 1)
                    pe.wait_ge(s["late_in"], 16 * 10)
                    for k in range(KC):
                        mm = pe.matmul(b[0:n, 0:NG + NE], h2T[:, t % 2, k, 0:n], rw[:, k, :],
                                       start=k == 0, stop=k == KC - 1)
                    mm.then_inc(s["m_ready"], 1)
                if i >= 3:
                    t = i - 3
                    n = rows(t)
                    b = m_open(f"cum{t}")
                    pe.wait_ge(s["m_onehot"], t + 1)
                    pe.matmul(b[0:n, 0:NE], upper[0:n, 0:n], msum[0:n, t % 2, :], start=True, stop=True)
                    pe.matmul(b[:, NE:2 * NE], ones[0:n, :], msum[0:n, t % 2, :], start=True, stop=True)\
                        .then_inc(s["m_ready"], 1)
                if 1 <= i <= TILES:
                    pe.wait_ge(s["h2_ready"], i)
                    if i >= 2:
                        pe.wait_ge(s["h2T_ready"], i - 1)
                    transposes(i - 1, 4).then_inc(s["t2_done"], 1)

            def early(b, n):
                return isinstance(b, int) and b < n

            def expert_T(i, j):
                b = i * 4 + j
                if not early(b, 1):
                    pe.wait_ge(s["htm_ready"], b)
                pe.wait_ge(gath[j % 4], 16 * lap(i, j) + 16)
                for k in range(KC):
                    mm = pe.transpose(ps[:, k // 4, k % 4 * P:(k % 4 + 1) * P],
                                      xg[:, j % 4, k * P:(k + 1) * P], ident[:])
                mm.then_inc(s["xt_done"], 1)

            def expert_GU(i, j):
                b = i * 4 + j
                pe.wait_ge(s["htm_ready"], b + 1)
                if not early(b, 2):
                    pe.wait_ge(s["act_ready"], b - 1)
                pe.wait_ge(w_in_sem[j % 4], 48 * lap(i, j) + 48)
                w = wexp[:, j % 4, 0:2 * D].rearrange("p (g k f) -> p g k f", g=2, k=KC)
                for k in range(KC):
                    mm = pe.matmul(ps[:, 2 + j % 2, 0:2 * FF].rearrange("p (g f) -> p g f", g=2),
                                   hTm[:, j % 2, k, :], w[:, :, k, :], start=k == 0, stop=k == KC - 1)
                mm.then_inc(s["gu_done"], 1)

            def expert_AT(i, j):
                b = i * 4 + j
                if not early(b, 1):
                    pe.wait_ge(s["att_ready"], b)
                pe.wait_ge(s["act_ready"], b + 1)
                pe.transpose(ps[:, 4, 0:P], actv[:, j % 2, :], ident[:]).then_inc(s["at_done"], 1)

            def expert_D(i, j):
                b = i * 4 + j
                if not early(b, 1):
                    pe.wait_ge(s["ob_act"], b)
                    pe.wait_ge(s["ob_dve"], b)
                pe.wait_ge(s["att_ready"], b + 1)
                for r in range(2):
                    q = 2 * D + r * 512
                    mm = pe.matmul(ps[:, 5 + r, :], actT[:, j % 2, :], wexp[:, j % 4, q:q + 512],
                                   start=True, stop=True)
                mm.then_inc(s["d_done"], 1)

            def step(i, j, first, last):
                if not last:
                    expert_T(i, j + 1)
                expert_GU(i, j)
                if not first:
                    expert_AT(i, j - 1)
                    expert_D(i, j - 1)

            pe.wait_ge(s["xg_zero"], 1)
            pe.wait_ge(s["addr_ready"], TILES)
            expert_T(0, 0)
            for j in range(4):
                step(0, j, first=j == 0, last=False)
            with pe.Fori(1, NE // 4 - 1) as i:
                for j in range(4):
                    step(i, j, first=False, last=False)
            for j in range(4):
                step(NE // 4 - 1, j, first=False, last=j == 3)
            expert_AT(NE // 4 - 1, 3)
            expert_D(NE // 4 - 1, 3)
            pe.wait_ge(s["ov_ready"], 1)
            total = pe.value_load(ovt[0:1, 2 * OVER:2 * OVER + 1], min_val=0, max_val=OVER)
            with pe.Fori(0, OVER // 4) as i:
                for j in range(4):
                    with pe.If(i * 4 + j < total):
                        for part in (expert_T, expert_GU, expert_AT, expert_D):
                            part(i + NE // 4, j)


_INS = ["x_prompt", "x_sample", "state_conv_a", "state_pool", "state_conv_c", "g_mix", "w_in",
        "conv_a_w", "pool_w", "pool_scale", "conv_c_w", "conv_c_b", "ln_c_g", "ln_c_b", "ln_d_g",
        "ln_d_b", "sgu_w", "sgu_b", "w_out", "g_ffn", "router_group_w", "router_group_b",
        "router_expert_w", "router_expert_b", "expert_w_gate", "expert_w_up", "expert_w_down",
        "g_final"]
_OUTS = [("y_prompt", (1, NP, D)), ("y_sample", (SB, ST, D)), ("new_conv_a_prompt", (1, 1, HA, W)),
         ("new_pool_prompt", (1, 1, HP, W)), ("new_conv_c_prompt", (1, 1, HC, W)),
         ("new_conv_a_sample", (1, SB, HA, W)), ("new_pool_sample", (1, SB, HP, W)),
         ("new_conv_c_sample", (1, SB, HC, W)), ("chunk_v_sample", (1, SB, ST, W))]


def kernel(**inputs):
    import numpy as np
    import concourse.bacc as bacc
    from concourse.bass_utils import run_bass_kernel_spmd

    nc = bacc.Bacc("TRN2", target_bir_lowering=False, num_devices=1)
    arrays, args = {}, {}
    for name in _INS:
        x = np.ascontiguousarray(inputs[name])
        arrays[f"in_{name}"] = x
        args[name] = nc.dram_tensor(f"in_{name}", x.shape, mybir.dt.from_np(x.dtype),
                                    kind="ExternalInput").ap()
    for name, shape in _OUTS:
        args[name] = nc.dram_tensor(f"out_{name}", shape, F32, kind="ExternalOutput").ap()
    build_layer(nc, args)
    r = run_bass_kernel_spmd(nc, [arrays], core_ids=[0])
    return tuple(r.results[0][f"out_{name}"] for name, _ in _OUTS)
```

```python
from contextlib import ExitStack

import concourse.bass as bass
from concourse import mybir

F32 = mybir.dt.float32
F32R = mybir.dt.float32r
I32 = mybir.dt.int32
U32 = mybir.dt.uint32
ALU = mybir.AluOpType
ACT = mybir.ActivationFunctionType
AX_X = mybir.AxisListType.X

P = 128
D = 1024
KC = D // P
NP = 1024
SB, ST = 8, 8
NS = SB * ST
NT = NP + NS
TILES = NT // P + 1
LAST = TILES - 1
W = 256
HA, HP, HC = 2, 15, 30
EPS = 1e-6
NE, NG, EG, FF = 32, 4, 8, 128
CAPB = -(-NT // P)
TCOLS = NE * CAPB
OVER = (2 * NT - 1) // P
NONE = 1 << 20
NPAR = 31 + 3 + 4

PIECES = [("cg0", 1280), ("ca0", 1024), ("cg1", 1408), ("ca1", 1152), ("v0", 1792), ("v1", 1920),
          ("du0", 1536), ("du1", 1664), ("p0", 768), ("p1", 896),
          ("ac0", 256), ("ax0", 512), ("ac1", 384), ("ax1", 640), ("ab0", 0), ("ab1", 128)]
NPIECE = len(PIECES)
SPLITS = [0, 1, 2, 3, 5, 4] + list(range(6, NPIECE))
SLOT = [0, 1, 0, 1, 0, 2] + [(p + 1) % 2 for p in range(6, NPIECE)]
POOL_LO = (3, 6)
ZS = [n for n, _ in PIECES if n[0] != "v"]
Z_BY = {"cg": "act", "ca": "dve", "du": "act", "p": "act", "ac": "act", "ax": "dve", "ab": "dve"}
Z_USER = [Z_BY[n[:-1]] for n in ZS]
RANGES = [(0, 384), (384, 768), (768, NT)]
LN_RANGES = [(0, 512), (512, 1024), (1024, NT)]

M_USES = [("par", "act"), ("stc", "act"), ("stpa", "act"), ("ws", "act")]
M_USES += [(f"v{i}", "act") for i in range(TILES)]
M_USES += [("cst0", "act"), ("cst1", "act")]
M_USES += [(f"sp{i}", "dve") for i in range(TILES)]
M_USES += [("pst0", "act")] + [(f"pm0{r}", "act") for r in range(3)] + [("pst1", "act")]
M_USES += [(f"pm1{r}", "act") for r in range(3)]
M_USES += [(f"mean{r}", "dve") for r in range(3)] + [("ast0", "act")]
M_USES += [(f"var{r}", "act") for r in range(3)] + [("ast1", "act")]


def _router_uses():
    out = []
    for i in range(TILES + 3):
        if 2 <= i < TILES + 2:
            out.append((f"lg{i - 2}", "dve"))
        if i >= 3:
            out.append((f"cum{i - 3}", "dve"))
    return out


M_USES += _router_uses()
M_AT = {n: i for i, (n, _) in enumerate(M_USES)}


def nth(users, n):
    return sum(u == users[n] for u in users[:n + 1])


class Chain:

    def __init__(self, eng, sem):
        self.eng, self.sem, self.n = eng, sem, {}

    def __call__(self, ins, sem=None):
        sem, key = (self.sem, "chain") if sem is None else (sem, id(sem))
        self.n[key] = self.n.get(key, 0) + 1
        ins.then_inc(sem, 1)
        self.eng.wait_ge(sem, self.n[key])


def rows(i):
    return NS if i == LAST else P


def piece_matmuls(pe, ps, w, hT, bank):
    first, last = (0, 0, 0), (KC - 1, 1, 0)
    for k in range(KC):
        for wpart, hpart in ((0, 0), (0, 1), (1, 0)):
            for r, (t0, t1) in enumerate(RANGES):
                mm = pe.matmul(ps[:, bank + r, 0:t1 - t0], w[:, wpart, k * P:(k + 1) * P],
                               hT[:, hpart, k, t0:t1], start=(k, wpart, hpart) == first,
                               stop=(k, wpart, hpart) == last)
    return mm


def build_layer(nc, a):
    with ExitStack() as ctx:
        def sb(name, shape, dt=F32):
            return ctx.enter_context(nc.sbuf_tensor("sb_" + name, shape, dt))

        def sem(name):
            return ctx.enter_context(nc.semaphore(name))

        WL, CL = 1232, HC + NP + SB * (HC + ST)
        o_hT = 0
        o_mix = o_hT + 2 * KC * NT * 4
        o_raw = o_mix + KC * NT * 4
        o_ring = o_raw + 2 * D * 4
        o_x1 = o_ring + 4 * D * 4
        o_w = o_x1 + TILES * D * 4
        o_uc = o_w + 3 * WL * 4
        o_end = o_uc + 2 * CL * 4
        lo, _ = nc.bump_sbuf(o_end)

        def at(name, shape, offset, dt=F32):
            return nc.alloc_sbuf_tensor_at("at_" + name, shape, dt, offset=lo + offset)

        hT = at("hT", [P, 2, KC, NT], o_hT, F32R)
        wo = at("wo", [P, 2, KC, D], o_hT, F32R)
        wexp = at("wexp", [P, 4, 3 * D], o_hT)
        xg = at("xg", [P, 4, D], o_hT + 4 * 3 * D * 4)
        mixT = at("mixT", [P, KC, NT], o_mix)
        hTm = at("hTm", [P, 2, KC, P], o_mix)
        outb = at("outb", [P, 2, D], o_mix + 8192)
        opair = at("opair", [P, 2, 2 * D], o_mix + 16384)
        raw = at("raw", [P, 2, D], o_raw)
        far = (o_ring - o_mix) // 4 - 2 * NT
        rings = at("rings", [P, 2 * far], o_mix + 2 * NT * 4, F32R)
        ring = rings[:, far:far + 4 * D].rearrange("p (s m n) -> p s m n", s=2, m=2)
        ring2 = rings[:, 0:2 * D].rearrange("p (m n) -> p m n", m=2)
        vpair = rings[:].rearrange("p (s n) -> p s n", s=2)
        ovt = at("ovt", [1, 2 * OVER + 1], o_raw + 3712, I32)
        gcol = at("gcol", [P, OVER], o_raw + 3904, I32)
        scol = at("scol", [P, OVER], o_raw + 3968, I32)
        sg = at("sg", [P, 2, FF], o_raw)
        actv = at("actv", [P, 2, FF], o_raw + 1024)
        actT = at("actT", [P, 2, P], o_raw + 2048)
        ov = at("ov", [1, 2, NE], o_raw + 3072)
        ovi = at("ovi", [1, NE], o_raw + 3328, I32)
        ovb = at("ovb", [1, 3, OVER], o_raw + 3456)
        x1 = at("x1", [P, TILES, D], o_x1)
        wk = at("wk", [P, 3, WL], o_w)
        vall = at("vall", [P, TILES, W], o_w)
        uc = at("uc", [P, 2, CL], o_uc)
        lnsq = at("lnsq", [P, 2, 2, 512], o_uc)
        lnsq2 = at("lnsq2", [P, 2, NS], o_uc + 8192)
        h2T = at("h2T", [P, 2, KC, P], o_uc)
        wo_wk = at("wo_wk", [P, D], o_w + 2 * WL * 4)
        wo_ring = at("wo_ring", [P, 2, D], o_ring + 2 * D * 4)
        wo_uc = at("wo_uc", [P, 2, D], o_uc)
        st_rows = at("st_rows", [P, 4, W], o_mix + 6 * NT * 4)
        par_rows = at("par_rows", [P, W], o_mix + 7 * NT * 4)
        ws_rows = at("ws_rows", [P, NG, P], o_mix + 7 * NT * 4 + 1024)
        fill = at("fill", [P, TCOLS], o_mix + 5 * NT * 4, I32)
        lng = at("lng", [P, W], o_mix)
        lnb = at("lnb", [P, W], o_mix + W * 4)
        tab = at("tab", [P, TCOLS], o_mix + 32768, I32)
        gidxs = at("gidxs", [P, TCOLS], o_uc + 8192, I32)
        otmp = at("otmp", [1, OVER, NE], o_w)
        otmp2 = at("otmp2", [1, OVER, NE], o_w + 2048)

        ident = sb("ident", [P, P])
        ones = sb("ones", [P, P])
        avg = sb("avg", [P, P])
        upper = sb("upper", [P, P])
        gain = sb("gain", [P, D])
        wsT = sb("wsT", [P, NG, P])
        wsb = sb("wsb", [NS, NG, NS])
        pw = sb("pw", [P, 2, P])
        rw = sb("rw", [P, KC, NG + NE])
        rb = sb("rb", [P, NG + NE])
        biasd = sb("biasd", [P, 2, P])
        par = sb("par", [P, 2, NPAR])
        hist_p = sb("hist_p", [P, 2, SB * HP])
        hist_a = sb("hist_a", [P, 2, SB * HA])
        iwin = sb("iwin", [P, 2])
        topm = sb("topm", [P, 1])
        icnt = sb("icnt", [P, 2, HP])
        sptmp = sb("sptmp", [P, 2, P])
        st6 = sb("st6", [P, TILES, 6])
        mv = sb("mv", [P, TILES, 2])
        rsd = sb("rsd", [P, TILES])
        ss = sb("ss", [P, 3, TILES])
        rs = sb("rs", [P, 3, TILES])
        mhalf = sb("mhalf", [P, TILES])
        epsc = sb("epsc", [P, 1])
        io4 = sb("io4", [P, NG])
        io32 = sb("io32", [P, NE])
        iob = sb("iob", [1, OVER])
        pid = sb("pid", [P, TILES, 2], I32)
        lg8 = sb("lg8", [P, 8])
        le = sb("le", [P, NE])
        m8 = sb("m8", [P, 8])
        i8 = sb("i8", [P, 8], U32)
        sel8 = sb("sel8", [P, 8])
        n8 = sb("n8", [P, 8])
        j8 = sb("j8", [P, 8], U32)
        goh = sb("goh", [P, NG])
        sc = sb("sc", [P, 8])
        acts = sb("acts", [P, 8])
        gidx = sb("gidx", [P, 1])
        gates = sb("gates", [P, TILES, 2])
        eidx = sb("eidx", [P, 2, 2])
        oh = sb("oh", [P, 2, 2, NE])
        msum = sb("msum", [P, 2, NE])
        carry = sb("carry", [P, NE])
        rank = sb("rank", [P, NE])
        rjunk = sb("rjunk", [P, NE])
        rk = sb("rk", [P, 2])
        stage = sb("stage", [P, 3, W])
        rki = sb("rki", [P, 2], I32)
        rlo = sb("rlo", [P, 2], I32)
        rhi = sb("rhi", [P, 2], I32)
        addr = sb("addr", [P, TILES, 2], I32)

        ps = ctx.enter_context(nc.psum_tensor("ps", [P, 8, 512], F32))

        hs = nc.dram_tensor("scratch_h", [NT, D], F32, kind="Internal").ap()
        table = nc.dram_tensor("scratch_table", [P * TCOLS, 1], I32, kind="Internal").ap()
        orow = nc.dram_tensor("scratch_out", [2 * NT, D], F32, kind="Internal").ap()

        s = {n: sem(n) for n in (
            "dve_chain", "act_chain", "pool_chain",
            "const_ready", "ident_ready", "gcol_ready", "scol_ready", "fill_ready", "zero_ready",
            "small_in", "ws_in", "late_in", "gain_mix_in", "ln_d_in",
            "gain_ffn_in", "gain_fin_in", "pw_in", "wsT_masked", "wsb_in", "table_filled",
            "sq_done", "rs_ready", "h_ready", "ht_T", "ht_hi", "ht_lo",
            "hi_ready", "lo_pool", "lo_dve", "piece_done", "zf_act", "zf_dve",
            "m_ready", "mf_act", "mf_dve", "uc_ready", "v_stats", "v_rsd", "v_norm",
            "v_ready", "v_out", "px_ready", "pd_ready", "ac_ready", "ua_ready",
            "tail_ready", "sp_done", "c_mean", "c_sq", "c_norm", "c_ready", "conv_ready", "mix_ready",
            "stage_out", "mh_hi", "mh_lo", "o_done", "x1_ready", "h2_ready",
            "t2_done", "h2T_ready", "lgmax", "lgexp", "selmax", "selexp", "m_onehot",
            "addr_ready", "placed", "tab_in", "idx_ready", "ov_ready", "xg_zero",
            "xt_done", "htm_ready", "gu_done", "sg_ready", "act_ready", "at_done", "att_ready",
            "d_done", "ob_act", "ob_dve", "moe_done", "y_sum", "y_done", "y_out")}
        x_in = [sem(f"x_in{i}") for i in range(TILES)]
        raw_in = [sem(f"raw_in{i}") for i in range(2)]
        wo_in = [sem(f"w_out_in{k}") for k in range(2, 7)]
        w_in_sem = [sem(f"expert_in{i}") for i in range(4)]
        gath = [sem(f"gathered{i}") for i in range(4)]
        scat = [sem(f"scattered{i}") for i in range(2)]
        h2_stored = [sem(f"h2_stored{i}") for i in range(2)]
        pair_in = [sem(f"pair_in{i}") for i in range(2)]

        def wait_piece(eng, p):
            if PIECES[p][0][0] == "v":
                eng.wait_ge(s["m_ready"], M_AT[f"v{LAST}"] + 1)
            else:
                eng.wait_ge(s["piece_done"], p + 1 if p < 4 else p - 1)

        def slot_wait(eng, p):
            last = [q for q in range(p) if SLOT[q] == SLOT[p]]
            if last:
                wait_piece(eng, last[-1])

        def piece_slot(p):
            return ring2 if SLOT[p] == 2 else ring[:, SLOT[p]]

        def hi_wait(eng, p):
            eng.wait_ge(s["hi_ready"], (SPLITS.index(p) if p < NPIECE else p) + 1)

        def lo_wait(eng, p):
            k = p - NPIECE
            if k < 0:
                eng.wait_ge(s["lo_pool"], SPLITS.index(p) + 1)
            elif k in POOL_LO:
                eng.wait_ge(s["lo_pool"], NPIECE + POOL_LO.index(k) + 1)
            else:
                eng.wait_ge(s["lo_dve"], sum(m not in POOL_LO for m in range(k + 1)))

        def landing(p):
            k = p - NPIECE
            if k < 2:
                return raw[:, p % 2, :], raw_in[p % 2], p // 2 + 1
            if k == 7:
                return raw[:, 0, :], raw_in[0], NPIECE // 2 + 2
            dst = wo_wk[:] if k == 2 else wo_ring[:, k - 3] if k < 5 else wo_uc[:, k - 5]
            return dst, wo_in[k - 2], 1

        def m_bank(name):
            return 6 + M_AT[name] % 2

        def m_wait(eng, name):
            eng.wait_ge(s["m_ready"], M_AT[name] + 1)

        def z_bank(name):
            return 3 * (ZS.index(name) % 2)

        def z_parts(name, prompt, sample):
            b = z_bank(name)
            return [(prompt[:, 0:768].rearrange("p (r t) -> p r t", r=2), ps[:, b:b + 2, 0:384]),
                    (prompt[:, 768:1024], ps[:, b + 2, 0:256]),
                    (sample, ps[:, b + 2, 256:320].rearrange("p (b t) -> p b t", b=SB))]

        def mix_parts(c):
            return mixT[:, c, 0:NP], mixT[:, c, NP:NT].rearrange("p (b t) -> p b t", b=SB)

        def work(row, hist, shift=0):
            sm = row[:, hist + NP:hist + NP + SB * (hist + ST)].rearrange("p (b t) -> p b t", b=SB)
            return (row[:, hist - shift:hist - shift + NP], sm[:, :, hist - shift:hist - shift + ST])

        def mf_wait(eng, name):
            n = M_AT[name]
            eng.wait_ge(s["mf_" + M_USES[n][1]], nth([u for _, u in M_USES], n))

        def zf_wait(eng, name):
            n = ZS.index(name)
            eng.wait_ge(s["zf_" + Z_USER[n]], nth(Z_USER, n))

        def lap(i, j):
            return i + j // 4

        def result_out(eng, i):
            n = rows(i)
            eng.wait_ge(s["y_done"], i + 1)
            dst = a["y_sample"].rearrange("b t d -> (b t) d") if i == LAST \
                else a["y_prompt"][0, i * P:(i + 1) * P, :]
            eng.dma_start(dst, x1[0:n, i, :]).then_inc(s["y_out"], 16)

        block = ctx.enter_context(nc.Block())

        @block.sync
        def _(sp):
            def load_piece(p):
                k = p - NPIECE
                dst, arrived, _ = landing(p)
                if 2 <= p < NPIECE + 2 or k == 7:
                    last = p - 2 if k < 2 else NPIECE
                    hi_wait(sp, last)
                    lo_wait(sp, last)
                if p < NPIECE:
                    c = PIECES[p][1]
                    src = a["w_in"][0, :, c:c + P].rearrange("(q k) n -> q k n", k=KC)
                    dst = dst.rearrange("q (k n) -> q k n", k=KC)
                else:
                    src = a["w_out"][0, k * P:(k + 1) * P, :]
                if k == 2:
                    m_wait(sp, "pm12")
                if k == 3:
                    wait_piece(sp, NPIECE - 2)
                if k == 5:
                    sp.wait_ge(s["c_norm"], 1)
                sp.dma_start(dst, src).then_inc(arrived, 16)

            for i in range(TILES):
                src = a["x_sample"].rearrange("b t d -> (b t) d") if i == LAST \
                    else a["x_prompt"][0, i * P:(i + 1) * P, :]
                sp.dma_start(x1[0:rows(i), i, :], src).then_inc(x_in[i], 16)
                if i == 0:
                    sp.dma_start(gain[:], a["g_mix"].to_broadcast([P, D]))\
                        .then_inc(s["gain_mix_in"], 16)
            load_piece(0)
            load_piece(1)
            sp.wait_ge(s["fill_ready"], 1)
            sp.dma_start(table.rearrange("(p c) o -> p (c o)", p=P), fill[:])\
                .then_inc(s["table_filled"], 16)
            for h in range(NG):
                sp.dma_start(biasd[h % 2 * 64:h % 2 * 64 + 64, h // 2, :],
                             a["sgu_b"][0, h:h + 1, :].to_broadcast([64, P]))\
                    .then_inc(s["late_in"], 16)
            for n0, n, w, b in ((0, NG, "router_group_w", "router_group_b"),
                                (NG, NE, "router_expert_w", "router_expert_b")):
                sp.dma_start(rw[:, :, n0:n0 + n], a[w][0].rearrange("(q k) n -> q k n", k=KC))\
                    .then_inc(s["late_in"], 16)
                sp.dma_start(rb[:, n0:n0 + n], a[b].to_broadcast([P, n])).then_inc(s["late_in"], 16)
            sp.wait_ge(s["zero_ready"], 1)
            for g in range(4):
                q = g % 2 * 64
                sp.dma_start(pw[q:q + 64, g // 2, q:q + 64], a["pool_w"][0, g])\
                    .then_inc(s["pw_in"], 16)
            for p in range(2, NPIECE + KC):
                load_piece(p)
                if p == 3:
                    sp.wait_ge(s["wsT_masked"], 1)
                    for b in range(SB):
                        sp.dma_start(wsb[b * ST:(b + 1) * ST, :, b * ST:(b + 1) * ST],
                                     wsT[0:ST, :, 0:ST]).then_inc(s["wsb_in"], 16)
                if p == 4:
                    sp.wait_ge(s["h_ready"], TILES)
                    sp.dma_start(gain[:], a["g_ffn"].to_broadcast([P, D]))\
                        .then_inc(s["gain_ffn_in"], 16)
                    sp.wait_ge(s["uc_ready"], 1)
                    sp.dma_start(lng[:], a["ln_d_g"].to_broadcast([P, W])).then_inc(s["ln_d_in"], 16)
                    sp.dma_start(lnb[:], a["ln_d_b"].to_broadcast([P, W])).then_inc(s["ln_d_in"], 16)
            for i in range(TILES):
                sp.wait_ge(s["h2_ready"], i + 1)
                sp.dma_start(hs[i * P:i * P + rows(i), :], wk[0:rows(i), i % 2, 0:D])\
                    .then_inc(h2_stored[i % 2], 16)
            sp.dma_start(gain[:], a["g_final"].rearrange("(o d) -> o d", o=1).to_broadcast([P, D]))\
                .then_inc(s["gain_fin_in"], 16)

            def load_expert(i, j, e):
                lap = i + j // 4
                for m, w in enumerate(("expert_w_gate", "expert_w_up", "expert_w_down")):
                    src = a[w][0, bass.ds(e, 1), :, :].rearrange("o (q k) f -> q (o k f)", q=P)
                    sp.dma_start(wexp[:, j % 4, m * D:(m + 1) * D], src)\
                        .then_inc(w_in_sem[j % 4], 16)

            def expert_block(i, j, e, first=False):
                if not first:
                    sp.wait_ge(s["d_done"], i * 4 + j - 3)
                load_expert(i, j, e)

            sp.wait_ge(s["o_done"], TILES)
            for j in range(4):
                expert_block(0, j, j, first=True)
            sp.wait_ge(s["placed"], 16 * 2 * TILES)
            sp.dma_start(tab[:], table.rearrange("(p c) o -> p (c o)", p=P)).then_inc(s["tab_in"], 16)
            with sp.Fori(1, NE // 4) as i:
                for j in range(4):
                    expert_block(i, j, i * 4 + j)
            sp.wait_ge(s["ov_ready"], 1)
            total = sp.value_load(ovt[0:1, 2 * OVER:2 * OVER + 1], min_val=0, max_val=OVER)
            with sp.Fori(0, OVER // 4) as i:
                with sp.If(i * 4 < total):
                    for j in range(4):
                        with sp.If(i * 4 + j < total):
                            e = sp.value_load(ovt[0:1, bass.ds(i * 4 + j, 1)], min_val=0,
                                              max_val=NE - 1)
                            expert_block(i + NE // 4, j, e)
            sp.wait_ge(s["moe_done"], 1)
            for i in range(TILES):
                if i >= 2:
                    sp.wait_ge(s["y_sum"], i - 1)
                n = rows(i)
                src = orow[2 * i * P:2 * (i * P + n), :].rearrange("(t k) d -> t (k d)", k=2)
                sp.dma_start(opair[0:n, i % 2, :], src).then_inc(pair_in[i % 2], 16)
            sp.wait_ge(s["stage_out"], 16 * 7)
            sp.wait_ge(s["v_out"], 16)
            sp.wait_ge(s["y_out"], 16 * TILES)

        @block.scalar
        def _(act):
            do = Chain(act, s["act_chain"])
            A = nc.scalar.activation
            pools = a["state_pool"][0].rearrange("b r c -> (b r) c")
            half = SB // 2
            for h in range(2):
                act.dma_start(st_rows[0:half * HC, h, :],
                              a["state_conv_c"][0, h * half:(h + 1) * half].rearrange("b r c -> (b r) c"))\
                    .then_inc(s["small_in"], 16)
            act.dma_start(st_rows[0:SB * HP, 2, :], pools).then_inc(s["small_in"], 16)
            act.dma_start(st_rows[0:SB * HA, 3, :], a["state_conv_a"][0].rearrange("b r c -> (b r) c"))\
                .then_inc(s["small_in"], 16)
            for name, r0, n in (("conv_c_w", 0, 31), ("conv_a_w", 31, 3)):
                act.dma_start(par_rows[r0:r0 + n, :], a[name][0]).then_inc(s["small_in"], 16)
            for name, r0 in (("pool_scale", 34), ("conv_c_b", 35), ("ln_c_g", 36), ("ln_c_b", 37)):
                act.dma_start(par_rows[r0:r0 + 1, :], a[name]).then_inc(s["small_in"], 16)
            act.dma_start(ws_rows[:], a["sgu_w"][0].rearrange("h i j -> i h j")).then_inc(s["ws_in"], 16)

            def square(i, norm):
                n = rows(i)
                do(A(wk[0:n, 2, 0:D], x1[0:n, i, :], ACT.Square, accum_out=ss[0:n, norm, i:i + 1]),
                   s["sq_done"])

            def hT_hi(i):
                n = rows(i)
                act.wait_ge(s["ht_T"], i + 1)
                src = ps[:, 2 * (i % 3):2 * (i % 3) + 2, :].rearrange("p b (k t) -> p (b k) t", t=P)
                do(A(hT[:, 0, :, i * P:i * P + n], src[:, :, 0:n], ACT.Copy), s["ht_hi"])

            def m_out(name, dst, src):
                m_wait(act, name)
                for n, (x, y) in enumerate(zip(dst, src)):
                    do(A(x, y, ACT.Copy), s["mf_act"] if n == len(dst) - 1 else None)

            def part_hi(p):
                src, arrived, n = landing(p)
                act.wait_ge(arrived, 16 * n)
                if p < NPIECE:
                    slot_wait(act, p)
                    dst = piece_slot(p)[:, 0, :]
                else:
                    if p == NPIECE:
                        wait_piece(act, NPIECE - 1)
                    dst = wo[:, 0, p - NPIECE, :]
                do(A(dst, src, ACT.Copy), s["hi_ready"])

            for i in range(TILES + 2):
                if i < TILES:
                    act.wait_ge(x_in[i], 16)
                    square(i, 0)
                if i >= 2:
                    hT_hi(i - 2)
                if i in (5, 7):
                    part_hi((i - 5) // 2)

            def sigmoid(p, c):
                name = f"cg{c}"
                wait_piece(act, p)
                parts = z_parts(name, *mix_parts(c))
                for n, (dst, src) in enumerate(parts):
                    do(A(dst, src, ACT.Sigmoid), s["zf_act"] if n == 2 else None)

            def empty(p, dst_prompt, dst_sample):
                name = PIECES[p][0]
                wait_piece(act, p)
                for n, (dst, src) in enumerate(z_parts(name, dst_prompt, dst_sample)):
                    do(A(dst, src, ACT.Copy), s["zf_act"] if n == 2 else None)

            stages = [0]

            def tail_copy(row, hist, keep):
                sm = row[:, hist + NP:hist + NP + SB * (hist + ST)].rearrange("p (b t) -> p b t", b=SB)
                dst = sptmp[:].rearrange("p c t -> p (c t)")[:, 0:SB * keep]
                do(A(dst.rearrange("p (b t) -> p b t", b=SB), sm[:, :, hist + ST - keep:hist + ST],
                     ACT.Copy), s["tail_ready"])

            wait_piece(act, 0)
            part_hi(2)
            sigmoid(0, 0)
            b6, b7 = ps[:, 6, :], ps[:, 7, :]
            m_out("par", [par[:]],
                  [b6[:, 0:2 * 64].rearrange("p (c n) -> p c n", c=2)[:, :, 0:NPAR]])
            smp = [uc[:, c, HC + NP:CL].rearrange("p (b r) -> p b r", b=SB)[:, :, 0:HC]
                   for c in range(2)]
            m_out("stc", smp, [b7[:, c * 240:c * 240 + 240].rearrange("p (b r) -> p b r", b=SB)
                               for c in range(2)])
            m_out("stpa", [hist_p[:], hist_a[:]],
                  [b6[:, 0:240].rearrange("p (c n) -> p c n", c=2),
                   b6[:, 240:272].rearrange("p (c n) -> p c n", c=2)])
            m_out("ws", [wsT[:]], [b7.rearrange("p (h i) -> p h i", h=NG)])
            part_hi(3)
            part_hi(5)
            part_hi(4)
            sigmoid(2, 1)
            part_hi(6)
            for i in range(TILES):
                n = rows(i)
                name = f"v{i}"
                m_out(name, [vall[0:n, i, :]], [ps[0:n, m_bank(name), 0:W]])
            part_hi(7)
            stc_out = a["new_conv_c_sample"][0].rearrange("(h b) r c -> h (b r) c", h=2)
            c_outs = [(HC, 0, a["new_conv_c_prompt"][0, 0]), (120, 128, stc_out[0]),
                      (120, 256, stc_out[1])]

            def conv_state_part(c):
                name = f"cst{c}"
                b = ps[:, m_bank(name), :]
                m_out(name, [stage[0:n, m, c * P:(c + 1) * P] for m, (n, _, _) in enumerate(c_outs)],
                      [b[0:n, q:q + P] for n, q, _ in c_outs])
                if c == 1:
                    for m, (n, _, dst) in enumerate(c_outs):
                        act.dma_start(dst, stage[0:n, m, :]).then_inc(s["stage_out"], 16)
                        stages[0] += 16

            act.wait_ge(s["uc_ready"], 1)
            tail_copy(uc[:, 0, :], HC, HC)
            part_hi(8)
            empty(6, *mix_parts(6))
            conv_state_part(0)
            act.wait_ge(s["uc_ready"], 2)
            tail_copy(uc[:, 1, :], HC, HC)
            part_hi(9)
            empty(7, *mix_parts(7))
            conv_state_part(1)
            act.wait_ge(s["v_ready"], 1)
            act.dma_start(a["chunk_v_sample"][0].rearrange("b t c -> (b t) c"), vall[0:NS, LAST, :])\
                .then_inc(s["v_out"], 16)
            part_hi(10)

            def pool_input(p, c):
                name = f"p{c}"
                sm = wk[:, 0, HP + NP:HP + NP + SB * (HP + ST)].rearrange("p (b t) -> p b t", b=SB)
                do(nc.scalar.mul(wk[:, 0, 0:HP], ones[:, 0:HP], 0.0))
                do(A(sm[:, :, 0:HP], hist_p[:, c, :].rearrange("p (b r) -> p b r", b=SB), ACT.Copy))
                empty(p, *work(wk[:, 0, :], HP))

            def pool_out(c):
                for r, (t0, t1) in enumerate(LN_RANGES):
                    name = f"pm{c}{r}"
                    m_wait(act, name)
                    do(A(mixT[:, 2 + c, t0:t1], ps[:, m_bank(name), 0:t1 - t0], ACT.Copy,
                         scale=par[:, c, 34:35]), s["mf_act"])

            m_wait(act, f"sp{LAST}")
            act.wait_ge(s["v_out"], 16)
            pool_input(8, 0)
            do(A(acts[:, 2:3], ones[:, 0:1], ACT.Copy), s["px_ready"])
            act.wait_ge(s["sp_done"], 1)
            tail_copy(wk[:, 0, :], HP, HP)
            pool_state = [(HP, 0, None), (SB * HP, 128, None)]

            def pool_state_part(c):
                name = f"pst{c}"
                if c == 0:
                    act.wait_ge(s["stage_out"], stages[0])
                b = ps[:, m_bank(name), :]
                m_out(name, [stage[0:n, m, c * P:(c + 1) * P] for m, (n, _, _) in enumerate(pool_state)],
                      [b[0:n, q:q + P] for n, q, _ in pool_state])
                if c == 1:
                    act.dma_start(a["new_pool_prompt"][0, 0], stage[0:HP, 0, :])\
                        .then_inc(s["stage_out"], 16)
                    act.dma_start(a["new_pool_sample"][0].rearrange("b r c -> (b r) c"),
                                  stage[0:SB * HP, 1, :]).then_inc(s["stage_out"], 16)
                    stages[0] += 32

            part_hi(11)
            pool_state_part(0)
            act.wait_ge(s["pd_ready"], 1)
            pool_input(9, 1)
            do(A(acts[:, 2:3], ones[:, 0:1], ACT.Copy), s["px_ready"])
            tail_copy(wk[:, 0, :], HP, HP)
            pool_out(0)
            part_hi(12)

            def a_hist(c):
                sm = wk[:, c, HA + NP:HA + NP + SB * (HA + ST)].rearrange("p (b t) -> p b t", b=SB)
                do(nc.scalar.mul(wk[:, c, 0:HA], ones[:, 0:HA], 0.0))
                do(A(sm[:, :, 0:HA], hist_a[:, c, :].rearrange("p (b r) -> p b r", b=SB), ACT.Copy))

            empty(10, *mix_parts(0))
            pool_state_part(1)
            act.wait_ge(s["pd_ready"], 2)
            a_hist(0)
            a_hist(1)
            do(A(acts[:, 2:3], ones[:, 0:1], ACT.Copy), s["ac_ready"])
            part_hi(13)
            pool_out(1)
            part_hi(14)
            empty(12, *mix_parts(1))
            do(A(acts[:, 2:3], ones[:, 0:1], ACT.Copy), s["ac_ready"])

            def ln_square(r):
                t0, t1 = LN_RANGES[r]
                dst = lnsq2[:] if r == 2 else lnsq[:, r, :, :]
                act.wait_ge(s["c_mean"], r + 1)
                do(A(dst, mixT[:, 4:6, t0:t1], ACT.Square), s["c_sq"])

            def deviation(r):
                n = LN_RANGES[r][1] - LN_RANGES[r][0]
                name = f"var{r}"
                dst = lnsq2[:, 0, :] if r == 2 else lnsq[:, r, 0, :]
                m_wait(act, name)
                do(A(dst, ps[:, m_bank(name), 0:n], ACT.Sqrt, bias=epsc[:]), s["mf_act"])

            for r in range(3):
                ln_square(r)
            a_outs = [(HA, 0), (SB * HA, 128)]

            def a_state_part(c):
                name = f"ast{c}"
                b = ps[:, m_bank(name), :]
                m_out(name, [stage[0:n, m, c * P:(c + 1) * P] for m, (n, _) in enumerate(a_outs)],
                      [b[0:n, q:q + P] for n, q in a_outs])

            act.wait_ge(s["ua_ready"], 1)
            tail_copy(wk[:, 0, :], HA, HA)
            part_hi(15)
            act.wait_ge(s["stage_out"], stages[0])
            a_state_part(0)
            for r in range(3):
                deviation(r)
            act.wait_ge(s["ua_ready"], 2)
            tail_copy(wk[:, 1, :], HA, HA)
            for c in range(2):
                act.wait_ge(s["c_norm"], 1)
                do(A(mixT[:, 4 + c, :], mixT[:, 4 + c, :], ACT.Silu, bias=par[:, c, 37:38],
                     scale=par[:, c, 36:37]), s["c_ready"])
            a_state_part(1)
            act.dma_start(a["new_conv_a_prompt"][0, 0], stage[0:HA, 0, :]).then_inc(s["stage_out"], 16)
            act.dma_start(a["new_conv_a_sample"][0].rearrange("b r c -> (b r) c"),
                          stage[0:SB * HA, 1, :]).then_inc(s["stage_out"], 16)

            def mix_hi(i):
                n = rows(i)
                if i == 0:
                    act.wait_ge(s["mix_ready"], 1)
                if i == 1:
                    lo_wait(act, NPIECE + 3)
                if i >= 2:
                    act.wait_ge(s["o_done"], i - 1)
                dst = ring[:, i % 2, 0, :].rearrange("p (k t) -> p k t", k=KC)
                do(A(dst[:, :, 0:n], mixT[:, :, i * P:i * P + n], ACT.Copy), s["mh_hi"])

            def h2T_out(i):
                n = rows(i)
                act.wait_ge(s["t2_done"], i + 1)
                if i >= 2:
                    m_wait(act, f"lg{i - 2}")
                src = ps[:, 4:6, :].rearrange("p b (k t) -> p (b k) t", t=P)
                do(A(h2T[:, i % 2, :, 0:n], src[:, :, 0:n], ACT.Copy), s["h2T_ready"])

            def router_exp(i):
                n = rows(i)
                act.wait_ge(s["lgmax"], i + 1)
                do(A(acts[0:n, 4:8], lg8[0:n, 0:NG], ACT.Exp, bias=sc[0:n, 0:1],
                     accum_out=acts[0:n, 0:1]), s["lgexp"])
                act.wait_ge(s["selmax"], i + 1)
                do(A(acts[0:n, 1:2], n8[0:n, 1:2], ACT.Exp, bias=sc[0:n, 1:2]), s["selexp"])

            part_hi(NPIECE)
            part_hi(NPIECE + 1)
            mix_hi(0)
            for k in range(2, KC):
                part_hi(NPIECE + k)
            for i in range(TILES + 2):
                if i + 1 < TILES:
                    mix_hi(i + 1)
                if i < TILES:
                    act.wait_ge(s["x1_ready"], i + 1)
                    square(i, 1)
                if i >= 2:
                    router_exp(i - 2)
                if 1 <= i <= TILES:
                    h2T_out(i - 1)

            def expert_hT(i, j):
                b = i * 4 + j
                act.wait_ge(s["xt_done"], b + 1)
                if not (isinstance(b, int) and b < 2):
                    act.wait_ge(s["gu_done"], b - 1)
                src = ps[:, 0:2, :].rearrange("p b (k t) -> p (b k) t", t=P)
                nc.scalar.activation(hTm[:, j % 2, :, :], src, ACT.Copy).then_inc(s["htm_ready"], 1)

            def expert_silu(i, j):
                b = i * 4 + j
                act.wait_ge(s["gu_done"], b + 1)
                if not (isinstance(b, int) and b < 2):
                    act.wait_ge(s["act_ready"], b - 1)
                nc.scalar.activation(sg[:, j % 2, :], ps[:, 2 + j % 2, 0:FF], ACT.Silu)\
                    .then_inc(s["sg_ready"], 1)

            def expert_actT(i, j):
                b = i * 4 + j
                act.wait_ge(s["at_done"], b + 1)
                if not (isinstance(b, int) and b < 2):
                    act.wait_ge(s["d_done"], b - 1)
                nc.scalar.activation(actT[:, j % 2, :], ps[:, 4, 0:P], ACT.Copy)\
                    .then_inc(s["att_ready"], 1)

            def expert_out(i, j):
                b = i * 4 + j
                act.wait_ge(s["d_done"], b + 1)
                if not (isinstance(b, int) and b < 2):
                    act.wait_ge(scat[j % 2], 16 * (i * 2 + j // 2))
                nc.scalar.activation(outb[:, j % 2, 0:512], ps[:, 5, :], ACT.Copy)\
                    .then_inc(s["ob_act"], 1)

            def step(i, j, first, last):
                if not last:
                    expert_hT(i, j + 1)
                else:
                    with act.If(total > 0):
                        expert_hT(i, j + 1)
                expert_silu(i, j)
                if not first:
                    expert_actT(i, j - 1)
                    expert_out(i, j - 1)

            act.wait_ge(s["o_done"], TILES)
            expert_hT(0, 0)
            for j in range(4):
                step(0, j, first=j == 0, last=False)
            with act.Fori(1, NE // 4 - 1) as i:
                for j in range(4):
                    step(i, j, first=False, last=False)
            act.wait_ge(s["ov_ready"], 1)
            total = act.value_load(ovt[0:1, 2 * OVER:2 * OVER + 1], min_val=0, max_val=OVER)
            for j in range(4):
                step(NE // 4 - 1, j, first=False, last=j == 3)
            expert_actT(NE // 4 - 1, 3)
            expert_out(NE // 4 - 1, 3)
            with act.Fori(0, OVER // 4) as i:
                with act.If(i * 4 < total):
                    for j in range(4):
                        with act.If(i * 4 + j < total):
                            with act.If(i * 4 + j + 1 < total):
                                expert_hT(i + NE // 4, j + 1)
                            expert_silu(i + NE // 4, j)
                            expert_actT(i + NE // 4, j)
                            expert_out(i + NE // 4, j)

            act.wait_ge(s["moe_done"], 1)
            for i in range(TILES):
                n = rows(i)
                act.wait_ge(s["y_sum"], i + 1)
                square(i, 2)
                if i >= 1:
                    result_out(act, i - 1)
            result_out(act, TILES - 1)

        @block.gpsimd
        def _(pool):
            do = Chain(pool, s["pool_chain"])
            g = nc.gpsimd
            do(g.memset(ident[:], 0.0))
            do(g.affine_select(out=ident[:], in_=ident[:], compare_op=ALU.not_equal, fill=1.0, base=0,
                               pattern=[[-1, P]], channel_multiplier=1))
            do(g.memset(mhalf[:], -0.5), s["ident_ready"])

            def inv_root(norm, i, n, scale):
                do(g.tensor_scalar(ss[0:n, norm, i:i + 1], ss[0:n, norm, i:i + 1], scale, EPS,
                                   ALU.mult, ALU.add))
                do(g.tensor_tensor(rs[0:n, norm, i:i + 1], ss[0:n, norm, i:i + 1], mhalf[0:n, 0:1],
                                   ALU.pow), s["rs_ready"])

            def rms(norm, i):
                pool.wait_ge(s["sq_done"], norm * TILES + i + 1)
                inv_root(norm, i, rows(i), 1.0 / D)

            rms(0, 0)
            rms(0, 1)
            do(g.memset(pw[:], 0.0), s["zero_ready"])
            rms(0, 2)
            do(g.memset(fill[:], NONE), s["fill_ready"])
            do(g.memset(wsb[:], 0.0))
            do(g.memset(ones[:], 1.0))
            do(g.memset(avg[:], 1.0 / W))
            do(g.affine_select(out=upper[:], in_=ones[:], compare_op=ALU.is_gt, fill=0.0, base=0,
                               pattern=[[1, P]], channel_multiplier=-1))
            rms(0, 3)
            for c in range(2):
                do(g.memset(uc[:, c, 0:HC], 0.0))
            do(g.memset(epsc[:], EPS))
            do(g.memset(lg8[:], -3.0e38))
            do(g.memset(mv[:], 1.0))
            do(g.memset(carry[:], 0.0))
            rms(0, 4)
            for c in range(2):
                for h in range(2):
                    do(g.memset(iwin[h * 64:h * 64 + 64, c:c + 1], 1.0 / (2 << (2 * c + h))))
                    do(g.memset(topm[h * 64:h * 64 + 64, :], float(h)))
            flt = dict(allow_small_or_imprecise_dtypes=True)
            do(g.iota(icnt[:], [[0, 2], [1, HP]], base=1, channel_multiplier=0, **flt))
            do(g.iota(io4[:], [[1, NG]], base=0, channel_multiplier=0, **flt))
            do(g.iota(io32[:], [[1, NE]], base=0, channel_multiplier=0, **flt))
            do(g.iota(iob[:], [[1, OVER]], base=0, channel_multiplier=0, **flt))
            do(g.iota(pid[:], [[2 * P, TILES], [1, 2]], base=0, channel_multiplier=2), s["const_ready"])
            rms(0, 5)
            for i in range(6, TILES):
                rms(0, i)

            def part_lo(p):
                hi_wait(pool, p)
                if p < NPIECE:
                    slot_wait(pool, p)
                    hi, lo = piece_slot(p)[:, 0, :], piece_slot(p)[:, 1, :]
                else:
                    hi, lo = wo[:, 0, p - NPIECE, :], wo[:, 1, p - NPIECE, :]
                do(g.tensor_tensor(lo, landing(p)[0], hi.bitcast(F32), ALU.subtract), s["lo_pool"])

            for n, p in enumerate(SPLITS[:8]):
                part_lo(p)
                if n == 2:
                    mf_wait(pool, "ws")
                    do(g.affine_select(out=wsT[:], in_=wsT[:], compare_op=ALU.is_ge, fill=0.0, base=0,
                                       pattern=[[0, NG], [1, P]], channel_multiplier=-1), s["wsT_masked"])
            pool.wait_ge(s["v_stats"], 1)
            do(g.tensor_scalar(rsd[:], mv[:, :, 1], 1.0, EPS, ALU.mult, ALU.add))
            do(g.tensor_tensor(rsd[:], rsd[:], mhalf[:], ALU.pow), s["v_rsd"])
            part_lo(8)
            pool.wait_ge(s["v_norm"], 1)
            pool.wait_ge(s["ln_d_in"], 16 * 2)
            full = [P, LAST, W]
            do(g.tensor_tensor(vall[:, 0:LAST, :], vall[:, 0:LAST, :],
                               lng[:].unsqueeze(1).broadcast_to(full), ALU.mult))
            do(g.tensor_tensor(vall[:, 0:LAST, :], vall[:, 0:LAST, :],
                               lnb[:].unsqueeze(1).broadcast_to(full), ALU.add))
            do(g.tensor_tensor(vall[0:NS, LAST, :], vall[0:NS, LAST, :], lng[0:NS, :], ALU.mult))
            do(g.tensor_tensor(vall[0:NS, LAST, :], vall[0:NS, LAST, :], lnb[0:NS, :], ALU.add),
               s["v_ready"])
            for p in range(9, NPIECE):
                part_lo(p)
            for k in POOL_LO:
                part_lo(NPIECE + k)

            pool.wait_ge(s["table_filled"], 16)
            for i in range(TILES + 3):
                if i < TILES:
                    rms(1, i)
                if i >= 3:
                    t = i - 3
                    n = rows(t)
                    pool.wait_ge(s["addr_ready"], t + 1)
                    for k in range(2):
                        g.indirect_dma_start(
                            table, bass.IndirectOffsetOnAxis(ap=addr[0:n, t, k:k + 1], axis=0),
                            pid[0:n, t, k:k + 1], None, bounds_check=P * TCOLS - 1, oob_is_err=False)\
                            .then_inc(s["placed"], 16)

            last_token, last_pair = pool.to_reg(NT - 1), pool.to_reg(2 * NT - 1)

            def gather(b, index):
                g.indirect_dma_start(xg[:, b % 4, :], None, hs,
                                     bass.IndirectOffsetOnAxis(ap=index, axis=0),
                                     bounds_check=last_token, oob_is_err=False)\
                    .then_inc(gath[b % 4], 16)

            def scatter(b, index):
                pool.wait_ge(s["ob_act"], b + 1)
                pool.wait_ge(s["ob_dve"], b + 1)
                g.indirect_dma_start(orow, bass.IndirectOffsetOnAxis(ap=index, axis=0),
                                     outb[:, b % 2, :], None, bounds_check=last_pair,
                                     oob_is_err=False).then_inc(scat[b % 2], 16)

            pool.wait_ge(s["o_done"], TILES)
            do(g.memset(xg[:].rearrange("p s d -> p (s d)"), 0.0), s["xg_zero"])
            for k in range(2):
                pool.wait_ge(h2_stored[k], 16 * ((TILES + 1 - k) // 2))
            pool.wait_ge(s["idx_ready"], 1)
            def gather_over(o):
                with pool.If(total > o):
                    col = pool.value_load(ovt[0:1, OVER + o:OVER + o + 1], min_val=0,
                                          max_val=TCOLS - 1)
                    do(g.tensor_copy(gcol[:, o:o + 1], gidxs[:, bass.ds(col, 1)]), s["gcol_ready"])
                    do(g.tensor_copy(scol[:, o:o + 1], tab[:, bass.ds(col, 1)]), s["scol_ready"])
                    pool.wait_ge(s["xt_done"], NE + o - 3)
                    gather(NE + o, gcol[:, o:o + 1])

            for b in range(-3, NE + 1):
                if b >= 1 and b + 3 < NE:
                    pool.wait_ge(s["xt_done"], b)
                if b + 3 < NE:
                    c = (b + 3) * CAPB
                    gather(b + 3, gidxs[:, c:c + 1])
                else:
                    if b + 3 == NE:
                        pool.wait_ge(s["ov_ready"], 1)
                        total = pool.value_load(ovt[0:1, 2 * OVER:2 * OVER + 1], min_val=0,
                                                max_val=OVER)
                    gather_over(b + 3 - NE)
                if b >= 1:
                    c = (b - 1) * CAPB
                    scatter(b - 1, tab[:, c:c + 1])

            def all_scattered(n):
                for k in range(2):
                    pool.wait_ge(scat[k], 16 * ((n + 1 - k) // 2))

            def over_from(o):
                if o == OVER:
                    return
                with pool.If(total > o):
                    if o + 4 < OVER:
                        gather_over(o + 4)
                    scatter(NE + o, scol[:, o:o + 1])
                    with pool.If(total < o + 2):
                        all_scattered(NE + o + 1)
                    over_from(o + 1)

            with pool.If(total < 1):
                all_scattered(NE)
            over_from(0)
            do(g.memset(gcol[:, 0:1], 0), s["moe_done"])
            for i in range(TILES):
                rms(2, i)

        @block.vector
        def _(dve):
            do = Chain(dve, s["dve_chain"])
            v = nc.vector
            stt, tt, ts = v.scalar_tensor_tensor, v.tensor_tensor, v.tensor_scalar

            def normed(i, norm, done):
                n = rows(i)
                do(stt(wk[0:n, i % 2, 0:D].rearrange("p (k q) -> p q k", k=KC),
                       x1[0:n, i, :].rearrange("p (q k) -> p q k", k=KC), rs[0:n, norm, i:i + 1],
                       gain[0:n, :].rearrange("p (q k) -> p q k", k=KC), ALU.mult, ALU.mult), s[done])

            def hT_lo(i):
                n = rows(i)
                dve.wait_ge(s["ht_hi"], i + 1)
                src = ps[:, 2 * (i % 3):2 * (i % 3) + 2, :].rearrange("p b (k t) -> p (b k) t", t=P)
                do(tt(hT[:, 1, :, i * P:i * P + n], src[:, :, 0:n],
                      hT[:, 0, :, i * P:i * P + n].bitcast(F32), ALU.subtract), s["ht_lo"])

            dve.wait_ge(s["gain_mix_in"], 16)
            for i in range(TILES + 2):
                if i < TILES:
                    dve.wait_ge(s["rs_ready"], i + 1)
                    if i >= 2:
                        dve.wait_ge(s["ht_T"], i - 1)
                    normed(i, 0, "h_ready")
                if i >= 2:
                    hT_lo(i - 2)
            dve.wait_ge(s["const_ready"], 1)
            for c in range(2):
                for h in range(2):
                    q = slice(h * 64, h * 64 + 64)
                    do(ts(icnt[q, c, :], icnt[q, c, :], float(2 << (2 * c + h)), None, ALU.min))
            do(v.reciprocal(icnt[:], icnt[:]))

            def glu(c, p):
                name = f"ca{c}"
                wait_piece(dve, p)
                mf_wait(dve, "stc")
                zf_wait(dve, f"cg{c}")
                gp = z_parts(name, *mix_parts(c))
                for n, (dst, src) in enumerate(z_parts(name, *work(uc[:, c, :], HC))):
                    do(tt(dst, src, gp[n][0], ALU.mult), s["zf_dve"] if n == 2 else None)
                do(v.tensor_copy(sc[:, 7:8], ones[:, 0:1]), s["uc_ready"])

            def taps_c(c, k0, k1):
                for k in range(k0, k1):
                    xs = work(uc[:, c, :], HC, HC - k)
                    for y, x in zip(mix_parts(4 + c), xs):
                        if k == 0:
                            do(ts(y, x, par[:, c, 0:1], par[:, c, 35:36], ALU.mult, ALU.add))
                        else:
                            do(stt(y, x, par[:, c, k:k + 1], y, ALU.mult, ALU.add))

            glu(0, 1)
            dve.wait_ge(s["table_filled"], 16)
            mf_wait(dve, "par")
            taps_c(0, 0, 14)
            glu(1, 3)
            taps_c(0, 14, 31)
            mf_wait(dve, f"v{LAST}")
            for i in range(TILES):
                n = rows(i)
                do(v.bn_stats(st6[0:n, i, :], vall[0:n, i, :]))
            for i in range(TILES):
                n = rows(i)
                do(v.bn_aggr(mv[0:n, i, :], st6[0:n, i, :]), s["v_stats"] if i == LAST else None)
            dve.wait_ge(s["v_rsd"], 1)
            for i in range(TILES):
                n = rows(i)
                do(ts(vall[0:n, i, :], vall[0:n, i, :], mv[0:n, i, 0:1], rsd[0:n, i:i + 1],
                      ALU.subtract, ALU.mult), s["v_norm"] if i == LAST else None)
            taps_c(1, 0, 16)
            wait_piece(dve, 7)
            dve.wait_ge(s["late_in"], 16 * 8)
            zf_wait(dve, "du1")
            for i in range(TILES):
                name = f"sp{i}"
                m_wait(dve, name)
                b = ps[:, m_bank(name), :]
                if i < LAST:
                    do(tt(sptmp[:], b[:, 0:W].rearrange("p (c t) -> p c t", c=2), biasd[:], ALU.add),
                       s["mf_dve"])
                else:
                    for c in range(2):
                        do(tt(sptmp[:, c, 0:NS].rearrange("p (b t) -> p b t", b=SB),
                              b[:, c * P:c * P + NS].rearrange("p (b t) -> p b t", b=SB),
                              biasd[:, c, 0:ST].unsqueeze(1).broadcast_to([P, SB, ST]), ALU.add),
                           s["mf_dve"] if c == 1 else None)
                m = mixT[:, 6:8, i * P:i * P + rows(i)]
                do(tt(m, m, sptmp[:, :, 0:rows(i)], ALU.mult), s["sp_done"] if i == LAST else None)
            def pooled(c):
                n = HP + NP + SB * (HP + ST)
                row = [wk[:, r, :] for r in range(3)]
                dve.wait_ge(s["px_ready"], c + 1)
                if c == 1:
                    m_wait(dve, "pm02")
                steps = [(0, 1)] if c == 0 else [(0, 1), (1, 2), (2, 4)]
                src, lo_, at_ = row[0], 0, 0
                turn = [row[1], row[2]] if c == 0 else [row[2], row[1], row[2], row[1]]
                for k, shift in steps:
                    dst = turn[at_]
                    at_ += 1
                    lo_ += shift
                    do(tt(dst[:, lo_:n], src[:, lo_:n], src[:, lo_ - shift:n - shift], ALU.add))
                    src = dst
                shift = 2 if c == 0 else 8
                dst = turn[at_]
                do(stt(dst[:, HP:n], src[:, HP - shift:n - shift], topm[:, 0:1], src[:, HP:n],
                       ALU.mult, ALU.add))
                d = row[1 + c]
                for y, x, z in zip(work(d, HP), work(dst, HP), work(row[0], HP)):
                    if y.shape == [P, NP] or len(y.shape) == 2:
                        do(tt(y[:, 0:HP], x[:, 0:HP], icnt[:, c, :], ALU.mult))
                        do(tt(y[:, 0:HP], y[:, 0:HP], z[:, 0:HP], ALU.subtract))
                        y, x, z = y[:, HP:], x[:, HP:], z[:, HP:]
                    do(stt(y, x, iwin[:, c:c + 1], z, ALU.mult, ALU.subtract))
                do(v.tensor_copy(sc[:, 7:8], ones[:, 0:1]), s["pd_ready"])

            pooled(0)
            taps_c(1, 16, 20)
            pooled(1)
            taps_c(1, 20, 31)
            do(v.tensor_copy(sc[:, 7:8], ones[:, 0:1]), s["conv_ready"])

            def a_input(c, p):
                name = f"ax{c}"
                wait_piece(dve, p)
                dve.wait_ge(s["ac_ready"], c + 1)
                gp = z_parts(name, *mix_parts(c))
                for n, (dst, src) in enumerate(z_parts(name, *work(wk[:, c, :], HA))):
                    do(tt(dst, src, gp[n][0], ALU.mult), s["zf_dve"] if n == 2 else None)
                do(v.tensor_copy(sc[:, 7:8], ones[:, 0:1]), s["ua_ready"])

            def a_taps(c):
                for k in range(3):
                    w = par[:, c, 31 + k:32 + k]
                    for y, x in zip(mix_parts(c), work(wk[:, c, :], HA, HA - k)):
                        if k == 0:
                            do(ts(y, x, w, None, ALU.mult))
                        else:
                            do(stt(y, x, w, y, ALU.mult, ALU.add))

            def a_gate(c, p):
                name = f"ab{c}"
                wait_piece(dve, p)
                for n, (dst, src) in enumerate(z_parts(name, *mix_parts(c))):
                    do(tt(dst, dst, src, ALU.mult), s["zf_dve"] if n == 2 else None)

            def c_mean(r):
                t0, t1 = LN_RANGES[r]
                name = f"mean{r}"
                m_wait(dve, name)
                y = mixT[:, 4:6, t0:t1]
                mean = ps[:, m_bank(name), 0:t1 - t0].unsqueeze(1).broadcast_to([P, 2, t1 - t0])
                do(tt(y, y, mean, ALU.subtract), s["mf_dve"])
                do(v.tensor_copy(sc[:, 7:8], ones[:, 0:1]), s["c_mean"])

            def c_norm(r):
                t0, t1 = LN_RANGES[r]
                mf_wait(dve, f"var{r}")
                d = lnsq2[:, 0, :] if r == 2 else lnsq[:, r, 0, :]
                y = mixT[:, 4:6, t0:t1]
                do(v.reciprocal(d, d))
                do(tt(y, y, d.unsqueeze(1).broadcast_to([P, 2, t1 - t0]), ALU.mult),
                   s["c_norm"] if r == 2 else None)

            a_input(0, 11)
            a_taps(0)
            for r in range(3):
                c_mean(r)
            a_input(1, 13)
            a_taps(1)
            for r in range(3):
                c_norm(r)
            a_gate(0, 14)
            a_gate(1, 15)
            do(v.tensor_copy(sc[:, 7:8], ones[:, 0:1]), s["mix_ready"])

            def wo_lo(k):
                hi_wait(dve, NPIECE + k)
                do(tt(wo[:, 1, k, :], landing(NPIECE + k)[0], wo[:, 0, k, :].bitcast(F32),
                      ALU.subtract), s["lo_dve"])

            def mix_lo(i):
                n = rows(i)
                dve.wait_ge(s["mh_hi"], i + 1)
                hi, low = (ring[:, i % 2, m, :].rearrange("p (k t) -> p k t", k=KC)[:, :, 0:n]
                           for m in range(2))
                do(tt(low, mixT[:, :, i * P:i * P + n], hi.bitcast(F32), ALU.subtract), s["mh_lo"])

            def residual(i):
                n = rows(i)
                dve.wait_ge(s["o_done"], i + 1)
                b = 2 * (i % 2)
                do(tt(x1[0:n, i, :].rearrange("p (r d) -> p r d", r=2),
                      x1[0:n, i, :].rearrange("p (r d) -> p r d", r=2), ps[0:n, b:b + 2, :], ALU.add),
                   s["x1_ready"])

            def route(i):
                n = rows(i)
                q = slice(0, n)
                name = f"lg{i}"
                z = i % 2
                m_wait(dve, name)
                b = ps[q, m_bank(name), :]
                do(tt(lg8[q, 0:NG], b[:, 0:NG], rb[q, 0:NG], ALU.add))
                do(tt(le[q, :], b[:, NG:NG + NE], rb[q, NG:NG + NE], ALU.add), s["mf_dve"])
                do(v.max(m8[q, :], lg8[q, :]))
                do(ts(sc[q, 0:1], m8[q, 0:1], -1.0, None, ALU.mult), s["lgmax"])
                do(v.max_index(i8[q, :], m8[q, :], lg8[q, :]))
                do(v.tensor_copy(gidx[q, :], i8[q, 0:1]))
                do(ts(goh[q, :], io4[q, :], gidx[q, :], None, ALU.is_equal))
                do(ts(sel8[q, :], le[q, 0:EG], goh[q, 0:1], None, ALU.mult))
                for m in range(1, NG):
                    do(stt(sel8[q, :], le[q, m * EG:(m + 1) * EG], goh[q, m:m + 1], sel8[q, :],
                           ALU.mult, ALU.add))
                do(v.max(n8[q, :], sel8[q, :]))
                do(ts(sc[q, 1:2], n8[q, 0:1], -1.0, None, ALU.mult), s["selmax"])
                do(v.max_index(j8[q, :], n8[q, :], sel8[q, :]))
                do(ts(sc[q, 2:3], gidx[q, :], float(EG), None, ALU.mult))
                do(ts(eidx[q, z, :], j8[q, 0:2], sc[q, 2:3], None, ALU.add))
                for k in range(2):
                    do(ts(oh[q, z, k, :], io32[q, :], eidx[q, z, k:k + 1], None, ALU.is_equal))
                do(tt(msum[q, z, :], oh[q, z, 0, :], oh[q, z, 1, :], ALU.add), s["m_onehot"])
                dve.wait_ge(s["lgexp"], i + 1)
                dve.wait_ge(s["selexp"], i + 1)
                do(ts(sc[q, 3:4], acts[q, 1:2], 1.0, None, ALU.add))
                do(ts(sc[q, 4:5], acts[q, 0:1], sc[q, 3:4], None, ALU.mult))
                do(v.reciprocal(gates[q, i, 0:1], sc[q, 4:5]))
                do(ts(gates[q, i, 1:2], acts[q, 1:2], gates[q, i, 0:1], None, ALU.mult))

            def places(i):
                n = rows(i)
                q = slice(0, n)
                name = f"cum{i}"
                z = i % 2
                m_wait(dve, name)
                b = ps[:, m_bank(name), :]
                do(tt(rank[q, :], b[q, 0:NE], carry[q, :], ALU.add))
                do(tt(carry[:], b[:, NE:2 * NE], carry[:], ALU.add), s["mf_dve"])
                for k in range(2):
                    do(stt(rjunk[q, :], rank[q, :], 0.0, oh[q, z, k, :], ALU.add, ALU.mult,
                           accum_out=rk[q, k:k + 1]))
                do(v.tensor_copy(rki[q, :], rk[q, :]))
                do(ts(rlo[q, :], rki[q, :], P - 1, None, ALU.bitwise_and))
                do(ts(rhi[q, :], rki[q, :], 7, None, ALU.logical_shift_right))
                do(stt(rhi[q, :], rlo[q, :], float(TCOLS), rhi[q, :], ALU.mult, ALU.add))
                do(stt(addr[q, i, :], eidx[q, z, :], float(CAPB), rhi[q, :], ALU.mult, ALU.add),
                   s["addr_ready"])

            wo_lo(0)
            mix_lo(0)
            for k in range(1, KC):
                if k not in POOL_LO:
                    wo_lo(k)
            dve.wait_ge(s["gain_ffn_in"], 16)
            for i in range(TILES + 3):
                if i + 1 < TILES:
                    mix_lo(i + 1)
                if i < TILES:
                    residual(i)
                    dve.wait_ge(s["rs_ready"], TILES + i + 1)
                    if i >= 2:
                        dve.wait_ge(s["t2_done"], i - 1)
                        dve.wait_ge(h2_stored[i % 2], 16 * (i // 2))
                    normed(i, 1, "h2_ready")
                if 2 <= i < TILES + 2:
                    route(i - 2)
                if i >= 3:
                    places(i - 3)

            dve.wait_ge(s["tab_in"], 16)
            do(ts(gidxs[:], tab[:], 1, None, ALU.logical_shift_right), s["idx_ready"])
            n_e, incl = ov[:, 0, :], ov[:, 1, :]
            do(ts(ovi[:], carry[0:1, :], float(P - 1), None, ALU.add))
            do(ts(ovi[:], ovi[:], 7, None, ALU.logical_shift_right))
            do(ts(n_e, ovi[:], 1.0, -1.0, ALU.max, ALU.add))
            do(v.tensor_tensor_scan(incl, ones[0:1, 0:NE], n_e, 0.0, ALU.mult, ALU.add))
            grid = [1, OVER, NE]
            for k in range(2):
                dve.wait_ge(h2_stored[k], 16 * ((TILES + 1 - k) // 2))
            do(tt(otmp[:], incl.unsqueeze(1).broadcast_to(grid), iob[:].unsqueeze(2).broadcast_to(grid),
                  ALU.is_le))
            do(v.tensor_reduce(ovb[:, 0, :], otmp[:], AX_X, ALU.add))
            do(tt(otmp2[:], otmp[:], n_e.unsqueeze(1).broadcast_to(grid), ALU.mult))
            do(v.tensor_reduce(ovb[:, 1, :], otmp2[:], AX_X, ALU.add))
            do(ts(ovb[:, 0, :], ovb[:, 0, :], float(NE - 1), None, ALU.min))
            do(v.tensor_copy(ovt[:, 0:OVER], ovb[:, 0, :]))
            do(tt(ovb[:, 2, :], iob[:], ovb[:, 1, :], ALU.subtract))
            do(stt(ovb[:, 2, :], ovb[:, 0, :], float(CAPB), ovb[:, 2, :], ALU.mult, ALU.add))
            do(ts(ovb[:, 2, :], ovb[:, 2, :], 1.0, float(TCOLS - 1), ALU.add, ALU.min))
            do(v.tensor_copy(ovt[:, OVER:2 * OVER], ovb[:, 2, :]))
            do(v.tensor_copy(ovt[:, 2 * OVER:2 * OVER + 1], incl[:, NE - 1:NE]), s["ov_ready"])

            def expert_act(i, j):
                b = i * 4 + j
                dve.wait_ge(s["sg_ready"], b + 1)
                if not (isinstance(b, int) and b < 2):
                    dve.wait_ge(s["at_done"], b - 1)
                v.tensor_tensor(actv[:, j % 2, :], sg[:, j % 2, :], ps[:, 2 + j % 2, FF:2 * FF],
                                ALU.mult).then_inc(s["act_ready"], 1)

            def expert_out(i, j):
                b = i * 4 + j
                dve.wait_ge(s["d_done"], b + 1)
                if not (isinstance(b, int) and b < 2):
                    dve.wait_ge(scat[j % 2], 16 * (i * 2 + j // 2))
                v.tensor_copy(outb[:, j % 2, 512:D], ps[:, 6, :]).then_inc(s["ob_dve"], 1)

            def step(i, j, first):
                expert_act(i, j)
                if not first:
                    expert_out(i, j - 1)

            for j in range(4):
                step(0, j, first=j == 0)
            with dve.Fori(1, NE // 4) as i:
                for j in range(4):
                    step(i, j, first=False)
            expert_out(NE // 4 - 1, 3)
            total = dve.value_load(ovt[0:1, 2 * OVER:2 * OVER + 1], min_val=0, max_val=OVER)
            with dve.Fori(0, OVER // 4) as i:
                with dve.If(i * 4 < total):
                    for j in range(4):
                        with dve.If(i * 4 + j < total):
                            expert_act(i + NE // 4, j)
                            expert_out(i + NE // 4, j)

            dve.wait_ge(s["moe_done"], 1)
            dve.wait_ge(s["gain_fin_in"], 16)
            for i in range(TILES + 1):
                if i < TILES:
                    n = rows(i)
                    dve.wait_ge(pair_in[i % 2], 16 * (i // 2 + 1))
                    for k in range(2):
                        do(stt(x1[0:n, i, :], opair[0:n, i % 2, k * D:(k + 1) * D],
                               gates[0:n, i, k:k + 1], x1[0:n, i, :], ALU.mult, ALU.add),
                           s["y_sum"] if k == 1 else None)
                if i >= 1:
                    m = i - 1
                    n = rows(m)
                    dve.wait_ge(s["rs_ready"], 2 * TILES + m + 1)
                    do(stt(x1[0:n, m, :], x1[0:n, m, :], rs[0:n, 2, m:m + 1], gain[0:n, :], ALU.mult,
                           ALU.mult), s["y_done"])

        @block.tensor
        def _(pe):
            def m_open(name):
                n = M_AT[name]
                if n >= 2:
                    mf_wait(pe, M_USES[n - 2][0])
                return ps[:, m_bank(name), :]

            def transposes(i, banks):
                n = rows(i)
                for k in range(KC):
                    mm = pe.transpose(ps[:, banks + k // 4, k % 4 * P:k % 4 * P + n],
                                      wk[0:n, i % 2, k * P:(k + 1) * P], ident[0:n, 0:n])
                return mm

            pe.wait_ge(s["ident_ready"], 1)
            for i in range(TILES):
                pe.wait_ge(s["h_ready"], i + 1)
                if i >= 3:
                    pe.wait_ge(s["ht_lo"], i - 2)
                transposes(i, 2 * (i % 3)).then_inc(s["ht_T"], 1)

            def z(p):
                name = PIECES[p][0]
                n = ZS.index(name)
                lo_wait(pe, p)
                if p == 0:
                    pe.wait_ge(s["ht_lo"], TILES)
                if n >= 2:
                    user = Z_USER[n - 2]
                    pe.wait_ge(s["zf_" + user], nth(Z_USER, n - 2))
                piece_matmuls(pe, ps, piece_slot(p), hT, z_bank(name)).then_inc(s["piece_done"], 1)

            z(0)
            pe.wait_ge(s["small_in"], 16 * 10)
            b = m_open("par")
            for c in range(2):
                mm = pe.transpose(b[:, c * 64:c * 64 + NPAR], par_rows[0:NPAR, c * P:(c + 1) * P],
                                  ident[0:NPAR, 0:NPAR])
            mm.then_inc(s["m_ready"], 1)
            b = m_open("stc")
            for c in range(2):
                for h in range(2):
                    q = (2 * c + h) * 120
                    mm = pe.transpose(b[:, q:q + 120], st_rows[0:120, h, c * P:(c + 1) * P],
                                      ident[0:120, 0:120])
            mm.then_inc(s["m_ready"], 1)
            b = m_open("stpa")
            for r, n, q in ((2, SB * HP, 0), (3, SB * HA, 240)):
                for c in range(2):
                    mm = pe.transpose(b[:, q + c * n:q + (c + 1) * n], st_rows[0:n, r, c * P:(c + 1) * P],
                                      ident[0:n, 0:n])
            mm.then_inc(s["m_ready"], 1)
            b = m_open("ws")
            pe.wait_ge(s["ws_in"], 16)
            for h in range(NG):
                mm = pe.transpose(b[:, h * P:(h + 1) * P], ws_rows[:, h, :], ident[:])
            mm.then_inc(s["m_ready"], 1)

            for p in range(1, 4):
                z(p)
            lo_wait(pe, 5)
            lo_wait(pe, 4)
            vw = vpair[:, :, 0:2 * D].rearrange("p s (part n) -> p s part n", part=2)
            for i in range(TILES):
                n = rows(i)
                b = m_open(f"v{i}")
                for k in range(KC):
                    for hpart, wpart in ((0, 0), (0, 1), (1, 0)):
                        mm = pe.matmul(b[0:n, 0:W].rearrange("p (s c) -> p s c", s=2),
                                       hT[:, hpart, k, i * P:i * P + n],
                                       vw[:, ::-1, wpart, k * P:(k + 1) * P],
                                       start=(k, hpart, wpart) == (0, 0, 0),
                                       stop=(k, hpart, wpart) == (KC - 1, 1, 0))
                mm.then_inc(s["m_ready"], 1)

            def tails(name, row, hist, keep, halves=1):
                b = m_open(name)
                pe.transpose(b[0:keep, 0:P], row[:, hist + NP - keep:hist + NP], ident[:])
                tail = sptmp[:].rearrange("p c t -> p (c t)")
                pe.wait_ge(s["tail_ready"], [n for n, _ in M_USES if "st" in n and n[-1] in "01"]
                           .index(name) + 1)
                n = SB * keep // halves
                for h in range(halves):
                    mm = pe.transpose(b[0:n, P * (h + 1):P * (h + 2)], tail[:, h * n:(h + 1) * n],
                                      ident[:])
                mm.then_inc(s["m_ready"], 1)

            def conv_tails(c):
                pe.wait_ge(s["uc_ready"], c + 1)
                tails(f"cst{c}", uc[:, c, :], HC, HC, halves=2)

            z(6)
            conv_tails(0)
            z(7)
            conv_tails(1)
            z(8)
            pe.wait_ge(s["v_ready"], 1)
            pe.wait_ge(s["wsb_in"], 16 * SB)
            for i in range(TILES):
                n = rows(i)
                b = m_open(f"sp{i}")
                for h in range(NG):
                    mm = pe.matmul(b[h % 2 * 64:h % 2 * 64 + 64, h // 2 * P:h // 2 * P + n],
                                   vall[0:n, i, h * 64:(h + 1) * 64],
                                   wsT[:, h, :] if i < LAST else wsb[:, h, :], start=True, stop=True)
                mm.then_inc(s["m_ready"], 1)
            z(9)
            pe.wait_ge(s["px_ready"], 1)
            tails("pst0", wk[:, 0, :], HP, HP)

            def pool_product(c):
                pe.wait_ge(s["pd_ready"], c + 1)
                pe.wait_ge(s["pw_in"], 16 * 4)
                prompt, sample = work(wk[:, 1 + c, :], HP)
                for r, (t0, t1) in enumerate(LN_RANGES):
                    b = m_open(f"pm{c}{r}")
                    x = sample if r == 2 else prompt[:, t0:t1]
                    y = b[:, 0:NS].rearrange("p (b t) -> p b t", b=SB) if r == 2 else b
                    pe.matmul(y, pw[:, c, :], x, start=True, stop=True).then_inc(s["m_ready"], 1)

            pool_product(0)
            z(10)
            pe.wait_ge(s["px_ready"], 2)
            tails("pst1", wk[:, 0, :], HP, HP)
            z(11)
            pool_product(1)
            z(12)

            def over_channels(what, r, src):
                n = LN_RANGES[r][1] - LN_RANGES[r][0]
                b = m_open(f"{what}{r}")
                for c in range(2):
                    mm = pe.matmul(b[:, 0:n], avg[:], src[:, c, :], start=c == 0, stop=c == 1)
                mm.then_inc(s["m_ready"], 1)

            pe.wait_ge(s["conv_ready"], 1)
            for r, (t0, t1) in enumerate(LN_RANGES):
                over_channels("mean", r, mixT[:, 4:6, t0:t1])
            z(13)
            pe.wait_ge(s["ua_ready"], 1)
            tails("ast0", wk[:, 0, :], HA, HA)
            for r in range(3):
                pe.wait_ge(s["c_sq"], r + 1)
                over_channels("var", r, lnsq2[:] if r == 2 else lnsq[:, r, :, :])
            z(14)
            pe.wait_ge(s["ua_ready"], 2)
            tails("ast1", wk[:, 1, :], HA, HA)
            z(15)

            def project(i):
                n = rows(i)
                b = 2 * (i % 2)
                pe.wait_ge(s["mh_lo"], i + 1)
                if i >= 2:
                    pe.wait_ge(s["x1_ready"], i - 1)
                for k in range(KC):
                    if i == 0:
                        lo_wait(pe, NPIECE + k)
                    for mpart, wpart in ((0, 0), (0, 1), (1, 0)):
                        for r in range(2):
                            mm = pe.matmul(ps[0:n, b + r, :], ring[:, i % 2, mpart, k * P:k * P + n],
                                           wo[:, wpart, k, r * 512:(r + 1) * 512],
                                           start=(k, mpart, wpart) == (0, 0, 0),
                                           stop=(k, mpart, wpart) == (KC - 1, 1, 0))
                mm.then_inc(s["o_done"], 1)

            pe.wait_ge(s["mix_ready"], 1)
            for i in range(TILES + 3):
                if i < TILES:
                    project(i)
                if 2 <= i < TILES + 2:
                    t = i - 2
                    n = rows(t)
                    b = m_open(f"lg{t}")
                    pe.wait_ge(s["h2T_ready"], t + 1)
                    pe.wait_ge(s["late_in"], 16 * 8)
                    for k in range(KC):
                        mm = pe.matmul(b[0:n, 0:NG + NE], h2T[:, t % 2, k, 0:n], rw[:, k, :],
                                       start=k == 0, stop=k == KC - 1)
                    mm.then_inc(s["m_ready"], 1)
                if i >= 3:
                    t = i - 3
                    n = rows(t)
                    b = m_open(f"cum{t}")
                    pe.wait_ge(s["m_onehot"], t + 1)
                    pe.matmul(b[0:n, 0:NE], upper[0:n, 0:n], msum[0:n, t % 2, :], start=True, stop=True)
                    pe.matmul(b[:, NE:2 * NE], ones[0:n, :], msum[0:n, t % 2, :], start=True, stop=True)\
                        .then_inc(s["m_ready"], 1)
                if 1 <= i <= TILES:
                    pe.wait_ge(s["h2_ready"], i)
                    if i >= 2:
                        pe.wait_ge(s["h2T_ready"], i - 1)
                    transposes(i - 1, 4).then_inc(s["t2_done"], 1)

            def early(b, n):
                return isinstance(b, int) and b < n

            def expert_T(i, j):
                b = i * 4 + j
                if not early(b, 1):
                    pe.wait_ge(s["htm_ready"], b)
                pe.wait_ge(gath[j % 4], 16 * lap(i, j) + 16)
                for k in range(KC):
                    mm = pe.transpose(ps[:, k // 4, k % 4 * P:(k % 4 + 1) * P],
                                      xg[:, j % 4, k * P:(k + 1) * P], ident[:])
                mm.then_inc(s["xt_done"], 1)

            def expert_GU(i, j):
                b = i * 4 + j
                pe.wait_ge(s["htm_ready"], b + 1)
                if not early(b, 2):
                    pe.wait_ge(s["act_ready"], b - 1)
                pe.wait_ge(w_in_sem[j % 4], 48 * lap(i, j) + 48)
                w = wexp[:, j % 4, 0:2 * D].rearrange("p (g k f) -> p g k f", g=2, k=KC)
                for k in range(KC):
                    mm = pe.matmul(ps[:, 2 + j % 2, 0:2 * FF].rearrange("p (g f) -> p g f", g=2),
                                   hTm[:, j % 2, k, :], w[:, :, k, :], start=k == 0, stop=k == KC - 1)
                mm.then_inc(s["gu_done"], 1)

            def expert_AT(i, j):
                b = i * 4 + j
                if not early(b, 1):
                    pe.wait_ge(s["att_ready"], b)
                pe.wait_ge(s["act_ready"], b + 1)
                pe.transpose(ps[:, 4, 0:P], actv[:, j % 2, :], ident[:]).then_inc(s["at_done"], 1)

            def expert_D(i, j):
                b = i * 4 + j
                if not early(b, 1):
                    pe.wait_ge(s["ob_act"], b)
                    pe.wait_ge(s["ob_dve"], b)
                pe.wait_ge(s["att_ready"], b + 1)
                for r in range(2):
                    q = 2 * D + r * 512
                    mm = pe.matmul(ps[:, 5 + r, :], actT[:, j % 2, :], wexp[:, j % 4, q:q + 512],
                                   start=True, stop=True)
                mm.then_inc(s["d_done"], 1)

            def step(i, j, first, last):
                if not last:
                    expert_T(i, j + 1)
                else:
                    with pe.If(total > 0):
                        expert_T(i, j + 1)
                expert_GU(i, j)
                if not first:
                    expert_AT(i, j - 1)
                    expert_D(i, j - 1)

            pe.wait_ge(s["xg_zero"], 1)
            pe.wait_ge(s["addr_ready"], TILES)
            expert_T(0, 0)
            for j in range(4):
                step(0, j, first=j == 0, last=False)
            with pe.Fori(1, NE // 4 - 1) as i:
                for j in range(4):
                    step(i, j, first=False, last=False)
            pe.wait_ge(s["ov_ready"], 1)
            total = pe.value_load(ovt[0:1, 2 * OVER:2 * OVER + 1], min_val=0, max_val=OVER)
            for j in range(4):
                step(NE // 4 - 1, j, first=False, last=j == 3)
            expert_AT(NE // 4 - 1, 3)
            expert_D(NE // 4 - 1, 3)
            with pe.Fori(0, OVER // 4) as i:
                with pe.If(i * 4 < total):
                    for j in range(4):
                        with pe.If(i * 4 + j < total):
                            with pe.If(i * 4 + j + 1 < total):
                                expert_T(i + NE // 4, j + 1)
                            for part in (expert_GU, expert_AT, expert_D):
                                part(i + NE // 4, j)


_INS = ["x_prompt", "x_sample", "state_conv_a", "state_pool", "state_conv_c", "g_mix", "w_in",
        "conv_a_w", "pool_w", "pool_scale", "conv_c_w", "conv_c_b", "ln_c_g", "ln_c_b", "ln_d_g",
        "ln_d_b", "sgu_w", "sgu_b", "w_out", "g_ffn", "router_group_w", "router_group_b",
        "router_expert_w", "router_expert_b", "expert_w_gate", "expert_w_up", "expert_w_down",
        "g_final"]
_OUTS = [("y_prompt", (1, NP, D)), ("y_sample", (SB, ST, D)), ("new_conv_a_prompt", (1, 1, HA, W)),
         ("new_pool_prompt", (1, 1, HP, W)), ("new_conv_c_prompt", (1, 1, HC, W)),
         ("new_conv_a_sample", (1, SB, HA, W)), ("new_pool_sample", (1, SB, HP, W)),
         ("new_conv_c_sample", (1, SB, HC, W)), ("chunk_v_sample", (1, SB, ST, W))]


def kernel(**inputs):
    import numpy as np
    import concourse.bacc as bacc
    from concourse.bass_utils import run_bass_kernel_spmd

    nc = bacc.Bacc("TRN2", target_bir_lowering=False, num_devices=1)
    arrays, args = {}, {}
    for name in _INS:
        x = np.ascontiguousarray(inputs[name])
        arrays[f"in_{name}"] = x
        args[name] = nc.dram_tensor(f"in_{name}", x.shape, mybir.dt.from_np(x.dtype),
                                    kind="ExternalInput").ap()
    for name, shape in _OUTS:
        args[name] = nc.dram_tensor(f"out_{name}", shape, F32, kind="ExternalOutput").ap()
    build_layer(nc, args)
    r = run_bass_kernel_spmd(nc, [arrays], core_ids=[0])
    return tuple(r.results[0][f"out_{name}"] for name, _ in _OUTS)
```

```python
from contextlib import ExitStack

import concourse.bass as bass
from concourse import mybir

F32 = mybir.dt.float32
F32R = mybir.dt.float32r
I32 = mybir.dt.int32
U32 = mybir.dt.uint32
ALU = mybir.AluOpType
ACT = mybir.ActivationFunctionType
AX_X = mybir.AxisListType.X

P = 128
D = 1024
KC = D // P
NP = 1024
SB, ST = 8, 8
NS = SB * ST
NT = NP + NS
TILES = NT // P + 1
LAST = TILES - 1
W = 256
HA, HP, HC = 2, 15, 30
EPS = 1e-6
NE, NG, EG, FF = 32, 4, 8, 128
CAPB = -(-NT // P)
TCOLS = NE * CAPB
OVER = (2 * NT - 1) // P
Q = P // 4
NONE = 1 << 20
LAP = 8
AHEAD = 1
XG = 4
NPAR = 31 + 3 + 4

PIECES = [("cg0", 1280), ("ca0", 1024), ("cg1", 1408), ("ca1", 1152), ("v0", 1792), ("v1", 1920),
          ("du0", 1536), ("du1", 1664), ("p0", 768), ("p1", 896),
          ("ac0", 256), ("ax0", 512), ("ac1", 384), ("ax1", 640), ("ab0", 0), ("ab1", 128)]
NPIECE = len(PIECES)
RAW_AGAIN = {3: (0, 2), 4: (1, 2), 7: (0, 3)}
LOADS = list(range(2, NPIECE)) + [NPIECE + k for k in (0, 1, 2, 5, 6, 3, 4, 7)]
SPLITS = [0, 1, 2, 3, 5, 4] + list(range(6, NPIECE))
SLOT = [0, 1, 0, 1, 0, 2] + [(p + 1) % 2 for p in range(6, NPIECE)]
Y_POOL = 6
POOL_TAPS = 6
POOL_LO = (2, 6)
ZS = [n for n, _ in PIECES if n[0] != "v"]
Z_BY = {"cg": "act", "ca": "dve", "du": "act", "p": "act", "ac": "act", "ax": "dve", "ab": "dve"}
Z_USER = [Z_BY[n[:-1]] for n in ZS]
RANGES = [(0, 384), (384, 768), (768, NT)]
LN_RANGES = [(0, 512), (512, 1024), (1024, NT)]

M_USES = [("par", "act"), ("stc", "act"), ("stpa", "act"), ("ws", "act")]
M_USES += [(f"v{i}", "act") for i in range(TILES)]
M_USES += [("cst0", "act"), ("cst1", "act")]
M_USES += [(f"sp{i}", "dve") for i in range(TILES)]
M_USES += [("pst0", "act")] + [(f"pm0{r}", "act") for r in range(3)] + [("pst1", "act")]
M_USES += [(f"pm1{r}", "act") for r in range(3)]
M_USES += [(f"mean{r}", "dve") for r in range(3)] + [("ast0", "act")]
M_USES += [(f"var{r}", "act") for r in range(3)] + [("ast1", "act")]


def _router_uses():
    out = []
    for i in range(1, TILES + 2):
        if i >= 2:
            out.append((f"cum{i - 2}", "dve"))
        if i <= TILES:
            out.append((f"lg{i - 1}", "dve"))
    return out


M_USES += _router_uses()
M_AT = {n: i for i, (n, _) in enumerate(M_USES)}


def nth(users, n):
    return sum(u == users[n] for u in users[:n + 1])


class Chain:

    def __init__(self, eng, sem):
        self.eng, self.sem, self.n = eng, sem, {}

    def __call__(self, ins, sem=None):
        sem, key = (self.sem, "chain") if sem is None else (sem, id(sem))
        self.n[key] = self.n.get(key, 0) + 1
        ins.then_inc(sem, 1)
        self.eng.wait_ge(sem, self.n[key])


def rows(i):
    return NS if i == LAST else P


def piece_matmuls(pe, ps, w, hT, bank, ranges=range(3)):
    first, last = (0, 0, 0), (KC - 1, 1, 0)
    for k in range(KC):
        for wpart, hpart in ((0, 0), (0, 1), (1, 0)):
            for r in ranges:
                t0, t1 = RANGES[r]
                mm = pe.matmul(ps[:, bank + r, 0:t1 - t0], w[:, wpart, k * P:(k + 1) * P],
                               hT[:, hpart, k, t0:t1], start=(k, wpart, hpart) == first,
                               stop=(k, wpart, hpart) == last)
    return mm


def build_layer(nc, a):
    with ExitStack() as ctx:
        def sb(name, shape, dt=F32):
            return ctx.enter_context(nc.sbuf_tensor("sb_" + name, shape, dt))

        def sem(name):
            return ctx.enter_context(nc.semaphore(name))

        WL, CL = 1232, HC + NP + SB * (HC + ST)
        o_hT = 0
        o_mix = o_hT + 2 * KC * NT * 4
        o_raw = o_mix + KC * NT * 4
        o_ring = o_raw + 2 * D * 4
        o_x1 = o_ring + 4 * D * 4
        o_w = o_x1 + TILES * D * 4
        o_uc = o_w + 3 * WL * 4
        o_end = o_uc + 2 * CL * 4
        lo, _ = nc.bump_sbuf(o_end)

        def at(name, shape, offset, dt=F32):
            return nc.alloc_sbuf_tensor_at("at_" + name, shape, dt, offset=lo + offset)

        hT = at("hT", [P, 2, KC, NT], o_hT, F32R)
        wo = at("wo", [P, 2, KC, D], o_hT, F32R)
        o_xg = o_hT + LAP * 3 * D * 4
        o_hTm = o_xg + XG * D * 4
        o_sg = o_hTm + 2 * D * 4
        wexp = at("wexp", [P, LAP, 3 * D], o_hT)
        xg = at("xg", [P, XG, D], o_xg)
        mixT = at("mixT", [P, KC, NT], o_mix)
        hTm = at("hTm", [P, 2, KC, P], o_hTm)
        outb = at("outb", [P, 2, D], o_w)
        opair = at("opair", [P, TILES, 2 * D], o_hT)
        raw = at("raw", [P, 2, D], o_raw)
        far = (o_ring - o_mix) // 4 - 2 * NT
        rings = at("rings", [P, 2 * far], o_mix + 2 * NT * 4, F32R)
        ring = rings[:, far:far + 4 * D].rearrange("p (s m n) -> p s m n", s=2, m=2)
        ring2 = rings[:, 0:2 * D].rearrange("p (m n) -> p m n", m=2)
        vpair = rings[:].rearrange("p (s n) -> p s n", s=2)
        ovt = at("ovt", [1, 2 * OVER + 1], o_sg + 3712, I32)
        gcol = at("gcol", [P, OVER], o_sg + 3904, I32)
        scol = at("scol", [P, OVER], o_sg + 3968, I32)
        sg = at("sg", [P, 2, FF], o_sg)
        actv = at("actv", [P, 2, FF], o_sg + 1024)
        actT = at("actT", [P, 2, P], o_sg + 2048)
        ov = at("ov", [1, 2, NE], o_sg + 3072)
        ovi = at("ovi", [1, NE], o_sg + 3328, I32)
        ovb = at("ovb", [1, 3, OVER], o_sg + 3456)
        x1 = at("x1", [P, TILES, D], o_x1)
        wk = at("wk", [P, 3, WL], o_w)
        vall = at("vall", [P, TILES, W], o_w)
        uc = at("uc", [P, 2, CL], o_uc)
        lnsq = at("lnsq", [P, 2, 2, 512], o_uc)
        lnsq2 = at("lnsq2", [P, 2, NS], o_uc + 8192)
        h2T = at("h2T", [P, 2, KC, P], o_uc)
        wo_wk = at("wo_wk", [P, D], o_w + 2 * WL * 4)
        wo_uc = at("wo_uc", [P, 2, D], o_uc)
        st_rows = at("st_rows", [P, 4, W], o_mix + 6 * NT * 4)
        par_rows = at("par_rows", [P, W], o_mix + 7 * NT * 4)
        ws_rows = at("ws_rows", [P, NG, P], o_mix + 7 * NT * 4 + 1024)
        lng = at("lng", [P, W], o_mix)
        lnb = at("lnb", [P, W], o_mix + W * 4)
        prow = at("prow", [P, 2, P], o_hT + 2 * KC * D * 4, F32R)
        pcol = at("pcol", [P, 2, TCOLS], o_hT + 2 * KC * D * 4 + 2 * P * 4, F32R)
        empty = at("empty", [P, TCOLS], o_hT + 2 * KC * D * 4 + 2 * P * 4)
        tab = at("tab", [P, TCOLS], o_uc + 8192 + TCOLS * 4, I32)
        gidxs = at("gidxs", [P, TCOLS], o_uc + 8192, I32)
        otmp = at("otmp", [1, OVER, NE], o_w + 8192)
        otmp2 = at("otmp2", [1, OVER, NE], o_w + 10240)

        ident = sb("ident", [P, P])
        ones = sb("ones", [P, P])
        avg = sb("avg", [P, P])
        upper = sb("upper", [P, P])
        gain = sb("gain", [P, D])
        wsT = sb("wsT", [P, NG, P])
        wsb = sb("wsb", [NS, NG, NS])
        pw = sb("pw", [P, 2, P])
        rw = sb("rw", [P, KC, 8 + NE])
        rb = sb("rb", [P, 8 + NE])
        biasd = sb("biasd", [P, 2, P])
        par = sb("par", [P, 2, NPAR])
        hist_p = sb("hist_p", [P, 2, SB * HP])
        hist_a = sb("hist_a", [P, 2, SB * HA])
        iwin = sb("iwin", [P, 2])
        topm = sb("topm", [P, 1])
        icnt = sb("icnt", [P, 2, HP])
        sptmp = sb("sptmp", [P, 2, P])
        st6 = sb("st6", [P, TILES, 6])
        mv = sb("mv", [P, TILES, 2])
        rsd = sb("rsd", [P, TILES])
        ss = sb("ss", [P, 3, TILES])
        rs = sb("rs", [P, 3, TILES])
        epsc = sb("epsc", [P, 1])
        io4 = sb("io4", [P, NG])
        io32 = sb("io32", [P, NE])
        iob = sb("iob", [1, OVER])
        pid = sb("pid", [P, TILES, 2])
        mhalf = sb("mhalf", [P, TILES])
        acts = sb("acts", [P, 1])
        pooljunk = sb("pooljunk", [P, 1])
        i8 = sb("i8", [P, 8], U32)
        sel8 = sb("sel8", [P, 8])
        j8 = sb("j8", [P, 8], U32)
        goh = sb("goh", [P, NG])
        sc = sb("sc", [P, 8])
        gidx = sb("gidx", [P, 1])
        gates = sb("gates", [P, TILES, 2])
        eidx = sb("eidx", [P, 2, 2])
        oh = sb("oh", [P, 2, 2, NE])
        msum = sb("msum", [P, 2, NE])
        carry = sb("carry", [P, NE])
        rank = sb("rank", [P, NE])
        rjunk = sb("rjunk", [P, NE])
        rk = sb("rk", [P, 2])
        stage = sb("stage", [P, 3, W])
        rki = sb("rki", [P, 2], I32)
        flat = stage[:].rearrange("p m c -> p (m c)")
        lge = flat[:, 0:TILES * 40].rearrange("p (t n) -> p t n", t=TILES)
        m8 = flat[:, TILES * 40:TILES * 48].rearrange("p (t n) -> p t n", t=TILES)
        n8 = flat[:, TILES * 48:TILES * 56].rearrange("p (t n) -> p t n", t=TILES)
        gex = flat[:, TILES * 56:TILES * 61].rearrange("p (t n) -> p t n", t=TILES)
        gsum = flat[:, TILES * 61:TILES * 62]
        rlo = sb("rlo", [P, 2], I32)
        rhi = sb("rhi", [P, 2], I32)
        row = sb("row", [P, 2])
        col = sb("col", [P, 2])
        cols = wsT[:].rearrange("p h i -> p (h i)")[:, 0:TCOLS]

        ps = ctx.enter_context(nc.psum_tensor("ps", [P, 8, 512], F32))

        hs = nc.dram_tensor("scratch_h", [NT, D], F32, kind="Internal").ap()
        orow = nc.dram_tensor("scratch_out", [2 * NT, D], F32, kind="Internal").ap()

        s = {n: sem(n) for n in (
            "dve_chain", "act_chain", "pool_chain",
            "const_ready", "ident_ready", "gcol_ready", "scol_ready", "zero_ready",
            "small_in", "ws_in", "late_in", "gain_mix_in", "ln_d_in",
            "gain_ffn_in", "gain_fin_in", "pw_in", "wsT_masked", "wsb_in",
            "sq_done", "rs_ready", "h_ready", "ht_T", "ht_hi", "ht_lo",
            "hi_ready", "lo_pool", "lo_dve", "piece_done", "zf_act", "zf_dve",
            "m_ready", "mf_act", "mf_dve", "uc_ready", "v_stats", "v_rsd", "v_norm",
            "v_ready", "v_out", "px_ready", "pd_ready", "ac_ready", "ua_ready",
            "tail_ready", "sp_done", "c_mean", "c_sq", "taps_begun", "begun_used",
            "ab1_first", "mix_first", "c_norm", "c_ready", "conv_ready", "mix_ready",
            "stage_out", "mh_hi", "mh_lo", "o_done", "x1_ready", "h2_ready",
            "t2_done", "h2T_ready", "pads_ready", "gex_in", "gex_out", "m_onehot",
            "place_ready", "table_added", "cols_ready", "idx_ready", "ov_ready", "xg_zero",
            "xt_done", "htm_ready", "gu_done", "sg_ready", "act_ready", "at_done", "att_ready",
            "d_done", "ob_act", "ob_dve", "moe_done", "y_sum", "y_scaled", "y_pool", "y_done", "y_out")}
        x_in = [sem(f"x_in{i}") for i in range(TILES)]
        raw_in = [sem(f"raw_in{i}") for i in range(2)]
        wo_in = [sem(f"w_out_in{k}") for k in (2, 5, 6)]
        w_in_sem = [sem(f"expert_in{i}") for i in range(LAP)]
        gath = [sem(f"gathered{i}") for i in range(XG)]
        scat = [sem(f"scattered{i}") for i in range(2)]
        h2_stored = [sem(f"h2_stored{i}") for i in range(2)]
        pair_in = [sem(f"pair_in{i}") for i in range(TILES)]

        def wait_piece(eng, p):
            if PIECES[p][0][0] == "v":
                eng.wait_ge(s["m_ready"], M_AT[f"v{LAST}"] + 1)
            else:
                eng.wait_ge(s["piece_done"], p + 1 if p < 4 else p - 1)

        def slot_wait(eng, p):
            last = [q for q in range(p) if SLOT[q] == SLOT[p]]
            if last:
                wait_piece(eng, last[-1])

        def piece_slot(p):
            return ring2 if SLOT[p] == 2 else ring[:, SLOT[p]]

        def hi_wait(eng, p):
            eng.wait_ge(s["hi_ready"], (SPLITS.index(p) if p < NPIECE else p) + 1)

        def lo_wait(eng, p):
            k = p - NPIECE
            if k < 0:
                eng.wait_ge(s["lo_pool"], SPLITS.index(p) + 1)
            elif k in POOL_LO:
                eng.wait_ge(s["lo_pool"], NPIECE + POOL_LO.index(k) + 1)
            else:
                eng.wait_ge(s["lo_dve"], sum(m not in POOL_LO for m in range(k + 1)))

        def landing(p):
            k = p - NPIECE
            if k < 2:
                return raw[:, p % 2, :], raw_in[p % 2], p // 2 + 1
            if k in RAW_AGAIN:
                slot, n = RAW_AGAIN[k]
                return raw[:, slot, :], raw_in[slot], NPIECE // 2 + n
            dst, n = {2: (wo_wk[:], 0), 5: (wo_uc[:, 0, :], 1), 6: (wo_uc[:, 1, :], 2)}[k]
            return dst, wo_in[n], 1

        def m_bank(name):
            return 6 + M_AT[name] % 2

        def m_area(name):
            if name[:2] == "lg":
                return ps[:, 6, 0:64]
            if name[:3] == "cum":
                return ps[:, 6, 64:128]
            return ps[:, m_bank(name), :]

        def m_wait(eng, name):
            eng.wait_ge(s["m_ready"], M_AT[name] + 1)

        def z_bank(name):
            return 3 * (ZS.index(name) % 2)

        def z_parts(name, prompt, sample):
            b = z_bank(name)
            return [(prompt[:, 0:768].rearrange("p (r t) -> p r t", r=2), ps[:, b:b + 2, 0:384]),
                    (prompt[:, 768:1024], ps[:, b + 2, 0:256]),
                    (sample, ps[:, b + 2, 256:320].rearrange("p (b t) -> p b t", b=SB))]

        def mix_parts(c):
            return mixT[:, c, 0:NP], mixT[:, c, NP:NT].rearrange("p (b t) -> p b t", b=SB)

        def work(row, hist, shift=0):
            sm = row[:, hist + NP:hist + NP + SB * (hist + ST)].rearrange("p (b t) -> p b t", b=SB)
            return (row[:, hist - shift:hist - shift + NP], sm[:, :, hist - shift:hist - shift + ST])

        def mf_wait(eng, name):
            n = M_AT[name]
            eng.wait_ge(s["mf_" + M_USES[n][1]], nth([u for _, u in M_USES], n))

        def zf_wait(eng, name):
            n = ZS.index(name)
            eng.wait_ge(s["zf_" + Z_USER[n]], nth(Z_USER, n))

        def lap(i, j):
            return i + j // LAP

        def result_out(eng, i):
            n = rows(i)
            if i < Y_POOL:
                eng.wait_ge(s["y_pool"], i + 1)
            else:
                eng.wait_ge(s["y_done"], i - Y_POOL + 1)
            dst = a["y_sample"].rearrange("b t d -> (b t) d") if i == LAST \
                else a["y_prompt"][0, i * P:(i + 1) * P, :]
            eng.dma_start(dst, x1[0:n, i, :]).then_inc(s["y_out"], 16)

        block = ctx.enter_context(nc.Block())

        @block.sync
        def _(sp):
            def load_piece(p):
                k = p - NPIECE
                dst, arrived, _ = landing(p)
                if 2 <= p < NPIECE + 2 or k in RAW_AGAIN:
                    last = p - 2 if k < 2 else NPIECE + {3: 0, 4: 1, 7: 3}[k]
                    hi_wait(sp, last)
                    lo_wait(sp, last)
                if p < NPIECE:
                    c = PIECES[p][1]
                    src = a["w_in"][0, :, c:c + P].rearrange("(q k) n -> q k n", k=KC)
                    dst = dst.rearrange("q (k n) -> q k n", k=KC)
                else:
                    src = a["w_out"][0, k * P:(k + 1) * P, :]
                if k == 2:
                    m_wait(sp, "pm12")
                if k == 5:
                    sp.wait_ge(s["c_norm"], 1)
                sp.dma_start(dst, src).then_inc(arrived, 16)

            for i in range(TILES):
                src = a["x_sample"].rearrange("b t d -> (b t) d") if i == LAST \
                    else a["x_prompt"][0, i * P:(i + 1) * P, :]
                sp.dma_start(x1[0:rows(i), i, :], src).then_inc(x_in[i], 16)
                if i == 0:
                    sp.dma_start(gain[:], a["g_mix"].to_broadcast([P, D]))\
                        .then_inc(s["gain_mix_in"], 16)
                if i in (3, 7):
                    load_piece(i // 4)
            pools = a["state_pool"][0].rearrange("b r c -> (b r) c")
            half = SB // 2
            for h in range(2):
                sp.dma_start(st_rows[0:half * HC, h, :],
                             a["state_conv_c"][0, h * half:(h + 1) * half].rearrange("b r c -> (b r) c"))\
                    .then_inc(s["small_in"], 16)
            sp.dma_start(st_rows[0:SB * HP, 2, :], pools).then_inc(s["small_in"], 16)
            sp.dma_start(st_rows[0:SB * HA, 3, :], a["state_conv_a"][0].rearrange("b r c -> (b r) c"))\
                .then_inc(s["small_in"], 16)
            for name, r0, n in (("conv_c_w", 0, 31), ("conv_a_w", 31, 3)):
                sp.dma_start(par_rows[r0:r0 + n, :], a[name][0]).then_inc(s["small_in"], 16)
            for name, r0 in (("pool_scale", 34), ("conv_c_b", 35), ("ln_c_g", 36), ("ln_c_b", 37)):
                sp.dma_start(par_rows[r0:r0 + 1, :], a[name]).then_inc(s["small_in"], 16)
            sp.dma_start(ws_rows[:], a["sgu_w"][0].rearrange("h i j -> i h j")).then_inc(s["ws_in"], 16)
            for h in range(NG):
                sp.dma_start(biasd[h % 2 * 64:h % 2 * 64 + 64, h // 2, :],
                             a["sgu_b"][0, h:h + 1, :].to_broadcast([64, P]))\
                    .then_inc(s["late_in"], 16)
            for n0, n, w, b in ((0, NG, "router_group_w", "router_group_b"),
                                (8, NE, "router_expert_w", "router_expert_b")):
                if n0 == 0:
                    sp.wait_ge(s["pads_ready"], 1)
                sp.dma_start(rw[:, :, n0:n0 + n], a[w][0].rearrange("(q k) n -> q k n", k=KC))\
                    .then_inc(s["late_in"], 16)
                sp.dma_start(rb[:, n0:n0 + n], a[b].to_broadcast([P, n])).then_inc(s["late_in"], 16)
            sp.wait_ge(s["zero_ready"], 1)
            for g in range(4):
                q = g % 2 * 64
                sp.dma_start(pw[q:q + 64, g // 2, q:q + 64], a["pool_w"][0, g])\
                    .then_inc(s["pw_in"], 16)
            for p in LOADS:
                load_piece(p)
                if p == 5:
                    sp.wait_ge(s["wsT_masked"], 1)
                    for b in range(SB):
                        sp.dma_start(wsb[b * ST:(b + 1) * ST, :, b * ST:(b + 1) * ST],
                                     wsT[0:ST, :, 0:ST]).then_inc(s["wsb_in"], 16)
                if p == 4:
                    sp.wait_ge(s["h_ready"], TILES)
                    sp.dma_start(gain[:], a["g_ffn"].to_broadcast([P, D]))\
                        .then_inc(s["gain_ffn_in"], 16)
                    sp.wait_ge(s["uc_ready"], 1)
                    sp.dma_start(lng[:], a["ln_d_g"].to_broadcast([P, W])).then_inc(s["ln_d_in"], 16)
                    sp.dma_start(lnb[:], a["ln_d_b"].to_broadcast([P, W])).then_inc(s["ln_d_in"], 16)
            for i in range(TILES):
                sp.wait_ge(s["h2_ready"], i + 1)
                sp.dma_start(hs[i * P:i * P + rows(i), :], wk[0:rows(i), i % 2, 0:D])\
                    .then_inc(h2_stored[i % 2], 16)
            sp.dma_start(gain[:], a["g_final"].rearrange("(o d) -> o d", o=1).to_broadcast([P, D]))\
                .then_inc(s["gain_fin_in"], 16)

            def load_expert(i, j, e, first):
                for m, w in enumerate(("expert_w_gate", "expert_w_up", "expert_w_down")):
                    if m == 1 and not (first and j < AHEAD):
                        sp.wait_ge(w_in_sem[(j - AHEAD) % LAP], 48 * (lap(i, j - AHEAD) + 1))
                    src = a[w][0, bass.ds(e, 1), :, :].rearrange("o (q k) f -> q (o k f)", q=P)
                    sp.dma_start(wexp[:, j % LAP, m * D:(m + 1) * D], src)\
                        .then_inc(w_in_sem[j % LAP], 16)

            def expert_block(i, j, e, first=False):
                if not first:
                    sp.wait_ge(s["d_done"], i * LAP + j - LAP + 1)
                load_expert(i, j, e, first)

            sp.wait_ge(s["o_done"], TILES)
            for j in range(3):
                expert_block(0, j, j, first=True)
            sp.wait_ge(gath[2], 16)
            for j in range(3, LAP):
                expert_block(0, j, j, first=True)
            with sp.Fori(1, NE // LAP) as i:
                for j in range(LAP):
                    expert_block(i, j, i * LAP + j)
            sp.wait_ge(s["ov_ready"], 1)
            total = sp.value_load(ovt[0:1, 2 * OVER:2 * OVER + 1], min_val=0, max_val=OVER)
            with sp.Fori(0, OVER // LAP) as i:
                with sp.If(i * LAP < total):
                    for j in range(LAP):
                        with sp.If(i * LAP + j < total):
                            e = sp.value_load(ovt[0:1, bass.ds(i * LAP + j, 1)], min_val=0,
                                              max_val=NE - 1)
                            expert_block(i + NE // LAP, j, e)
            sp.wait_ge(s["moe_done"], 1)
            for i in range(TILES):
                n = rows(i)
                src = orow[2 * i * P:2 * (i * P + n), :].rearrange("(t k) d -> t (k d)", k=2)
                sp.dma_start(opair[0:n, i, :], src).then_inc(pair_in[i], 16)
            sp.wait_ge(s["stage_out"], 16 * 7)
            sp.wait_ge(s["v_out"], 16)
            sp.wait_ge(s["y_out"], 16 * TILES)

        @block.scalar
        def _(act):
            do = Chain(act, s["act_chain"])
            A = nc.scalar.activation
            def square(i, norm):
                n = rows(i)
                do(A(wk[0:n, 2, 0:D], x1[0:n, i, :], ACT.Square, accum_out=ss[0:n, norm, i:i + 1]),
                   s["sq_done"])

            def hT_hi(i):
                n = rows(i)
                act.wait_ge(s["ht_T"], i + 1)
                src = ps[:, 3 + 2 * (i % 2):5 + 2 * (i % 2), :].rearrange("p b (k t) -> p (b k) t", t=P)
                do(A(hT[:, 0, :, i * P:i * P + n], src[:, :, 0:n], ACT.Copy), s["ht_hi"])

            def m_out(name, dst, src):
                m_wait(act, name)
                for n, (x, y) in enumerate(zip(dst, src)):
                    do(A(x, y, ACT.Copy), s["mf_act"] if n == len(dst) - 1 else None)

            def part_hi(p):
                src, arrived, n = landing(p)
                act.wait_ge(arrived, 16 * n)
                if p < NPIECE:
                    slot_wait(act, p)
                    dst = piece_slot(p)[:, 0, :]
                else:
                    if p == NPIECE:
                        wait_piece(act, NPIECE - 1)
                    dst = wo[:, 0, p - NPIECE, :]
                do(A(dst, src, ACT.Copy), s["hi_ready"])

            for i in range(TILES + 2):
                if i < TILES:
                    act.wait_ge(x_in[i], 16)
                    square(i, 0)
                if i >= 2:
                    hT_hi(i - 2)
                if i in (3, 8):
                    part_hi(i // 8)

            def sigmoid(p, c):
                name = f"cg{c}"
                wait_piece(act, p)
                parts = z_parts(name, *mix_parts(c))
                for n, (dst, src) in enumerate(parts):
                    do(A(dst, src, ACT.Sigmoid), s["zf_act"] if n == 2 else None)

            def empty(p, dst_prompt, dst_sample):
                name = PIECES[p][0]
                wait_piece(act, p)
                for n, (dst, src) in enumerate(z_parts(name, dst_prompt, dst_sample)):
                    do(A(dst, src, ACT.Copy), s["zf_act"] if n == 2 else None)

            stages = [0]

            def tail_copy(row, hist, keep):
                sm = row[:, hist + NP:hist + NP + SB * (hist + ST)].rearrange("p (b t) -> p b t", b=SB)
                dst = sptmp[:].rearrange("p c t -> p (c t)")[:, 0:SB * keep]
                do(A(dst.rearrange("p (b t) -> p b t", b=SB), sm[:, :, hist + ST - keep:hist + ST],
                     ACT.Copy), s["tail_ready"])

            wait_piece(act, 0)
            part_hi(2)
            sigmoid(0, 0)
            b6, b7 = ps[:, 6, :], ps[:, 7, :]
            m_out("par", [par[:]],
                  [b6[:, 0:2 * 64].rearrange("p (c n) -> p c n", c=2)[:, :, 0:NPAR]])
            smp = [uc[:, c, HC + NP:CL].rearrange("p (b r) -> p b r", b=SB)[:, :, 0:HC]
                   for c in range(2)]
            m_out("stc", smp, [b7[:, c * 240:c * 240 + 240].rearrange("p (b r) -> p b r", b=SB)
                               for c in range(2)])
            part_hi(3)
            m_out("stpa", [hist_p[:], hist_a[:]],
                  [b6[:, 0:240].rearrange("p (c n) -> p c n", c=2),
                   b6[:, 240:272].rearrange("p (c n) -> p c n", c=2)])
            m_out("ws", [wsT[:]], [b7.rearrange("p (h i) -> p h i", h=NG)])
            part_hi(5)
            part_hi(4)
            sigmoid(2, 1)
            part_hi(6)
            for i in range(TILES):
                n = rows(i)
                name = f"v{i}"
                m_out(name, [vall[0:n, i, :]], [ps[0:n, m_bank(name), 0:W]])
            part_hi(7)
            stc_out = a["new_conv_c_sample"][0].rearrange("(h b) r c -> h (b r) c", h=2)
            c_outs = [(HC, 0, a["new_conv_c_prompt"][0, 0]), (120, 128, stc_out[0]),
                      (120, 256, stc_out[1])]

            def conv_state_part(c):
                name = f"cst{c}"
                b = ps[:, m_bank(name), :]
                m_out(name, [stage[0:n, m, c * P:(c + 1) * P] for m, (n, _, _) in enumerate(c_outs)],
                      [b[0:n, q:q + P] for n, q, _ in c_outs])
                if c == 1:
                    for m, (n, _, dst) in enumerate(c_outs):
                        act.dma_start(dst, stage[0:n, m, :]).then_inc(s["stage_out"], 16)
                        stages[0] += 16

            act.wait_ge(s["uc_ready"], 1)
            tail_copy(uc[:, 0, :], HC, HC)
            part_hi(8)
            act.wait_ge(s["taps_begun"], 1)
            empty(6, *mix_parts(6))
            conv_state_part(0)
            act.wait_ge(s["uc_ready"], 2)
            tail_copy(uc[:, 1, :], HC, HC)
            part_hi(9)
            act.wait_ge(s["begun_used"], 1)
            empty(7, *mix_parts(7))
            conv_state_part(1)
            act.wait_ge(s["v_ready"], 1)
            act.dma_start(a["chunk_v_sample"][0].rearrange("b t c -> (b t) c"), vall[0:NS, LAST, :])\
                .then_inc(s["v_out"], 16)
            part_hi(10)

            def pool_input(p, c):
                name = f"p{c}"
                sm = wk[:, 0, HP + NP:HP + NP + SB * (HP + ST)].rearrange("p (b t) -> p b t", b=SB)
                do(nc.scalar.mul(wk[:, 0, 0:HP], ones[:, 0:HP], 0.0))
                do(A(sm[:, :, 0:HP], hist_p[:, c, :].rearrange("p (b r) -> p b r", b=SB), ACT.Copy))
                empty(p, *work(wk[:, 0, :], HP))

            def pool_out(c):
                for r, (t0, t1) in enumerate(LN_RANGES):
                    name = f"pm{c}{r}"
                    m_wait(act, name)
                    do(A(mixT[:, 2 + c, t0:t1], ps[:, m_bank(name), 0:t1 - t0], ACT.Copy,
                         scale=par[:, c, 34:35]), s["mf_act"])

            m_wait(act, f"sp{LAST}")
            act.wait_ge(s["v_out"], 16)
            pool_input(8, 0)
            do(A(acts[:], ones[:, 0:1], ACT.Copy), s["px_ready"])
            act.wait_ge(s["sp_done"], 1)
            tail_copy(wk[:, 0, :], HP, HP)
            pool_state = [(HP, 0, None), (SB * HP, 128, None)]

            def pool_state_part(c):
                name = f"pst{c}"
                if c == 0:
                    act.wait_ge(s["stage_out"], stages[0])
                b = ps[:, m_bank(name), :]
                m_out(name, [stage[0:n, m, c * P:(c + 1) * P] for m, (n, _, _) in enumerate(pool_state)],
                      [b[0:n, q:q + P] for n, q, _ in pool_state])
                if c == 1:
                    act.dma_start(a["new_pool_prompt"][0, 0], stage[0:HP, 0, :])\
                        .then_inc(s["stage_out"], 16)
                    act.dma_start(a["new_pool_sample"][0].rearrange("b r c -> (b r) c"),
                                  stage[0:SB * HP, 1, :]).then_inc(s["stage_out"], 16)
                    stages[0] += 32

            part_hi(11)
            pool_state_part(0)
            act.wait_ge(s["pd_ready"], 1)
            pool_out(0)
            pool_input(9, 1)
            do(A(acts[:], ones[:, 0:1], ACT.Copy), s["px_ready"])
            tail_copy(wk[:, 0, :], HP, HP)
            part_hi(12)

            def a_hist(c):
                sm = wk[:, c, HA + NP:HA + NP + SB * (HA + ST)].rearrange("p (b t) -> p b t", b=SB)
                do(nc.scalar.mul(wk[:, c, 0:HA], ones[:, 0:HA], 0.0))
                do(A(sm[:, :, 0:HA], hist_a[:, c, :].rearrange("p (b r) -> p b r", b=SB), ACT.Copy))

            empty(10, *mix_parts(0))
            pool_state_part(1)
            act.wait_ge(s["pd_ready"], 2)
            a_hist(0)
            a_hist(1)
            do(A(acts[:], ones[:, 0:1], ACT.Copy), s["ac_ready"])
            part_hi(13)
            pool_out(1)
            part_hi(14)
            empty(12, *mix_parts(1))
            do(A(acts[:], ones[:, 0:1], ACT.Copy), s["ac_ready"])

            def ln_square(r):
                t0, t1 = LN_RANGES[r]
                dst = lnsq2[:] if r == 2 else lnsq[:, r, :, :]
                act.wait_ge(s["c_mean"], r + 1)
                do(A(dst, mixT[:, 4:6, t0:t1], ACT.Square), s["c_sq"])

            def deviation(r):
                n = LN_RANGES[r][1] - LN_RANGES[r][0]
                name = f"var{r}"
                dst = lnsq2[:, 0, :] if r == 2 else lnsq[:, r, 0, :]
                m_wait(act, name)
                do(A(dst, ps[:, m_bank(name), 0:n], ACT.Sqrt, bias=epsc[:]), s["mf_act"])

            for r in range(3):
                ln_square(r)
            a_outs = [(HA, 0), (SB * HA, 128)]

            def a_state_part(c):
                name = f"ast{c}"
                b = ps[:, m_bank(name), :]
                m_out(name, [stage[0:n, m, c * P:(c + 1) * P] for m, (n, _) in enumerate(a_outs)],
                      [b[0:n, q:q + P] for n, q in a_outs])

            act.wait_ge(s["ua_ready"], 1)
            tail_copy(wk[:, 0, :], HA, HA)
            part_hi(15)
            act.wait_ge(s["stage_out"], stages[0])
            a_state_part(0)
            for r in range(3):
                deviation(r)
            act.wait_ge(s["ua_ready"], 2)
            tail_copy(wk[:, 1, :], HA, HA)
            for c in range(2):
                act.wait_ge(s["c_norm"], 1)
                do(A(mixT[:, 4 + c, :], mixT[:, 4 + c, :], ACT.Silu, bias=par[:, c, 37:38],
                     scale=par[:, c, 36:37]), s["c_ready"])
            a_state_part(1)
            act.dma_start(a["new_conv_a_prompt"][0, 0], stage[0:HA, 0, :]).then_inc(s["stage_out"], 16)
            act.dma_start(a["new_conv_a_sample"][0].rearrange("b r c -> (b r) c"),
                          stage[0:SB * HA, 1, :]).then_inc(s["stage_out"], 16)

            def mix_hi(i):
                n = rows(i)
                if i == 0:
                    act.wait_ge(s["mix_first"], 1)
                if i == 1:
                    act.wait_ge(s["mix_ready"], 1)
                if i >= 2:
                    act.wait_ge(s["o_done"], i - 1)
                dst = ring[:, 1 - i % 2, 0, :].rearrange("p (k t) -> p k t", k=KC)
                do(A(dst[:, :, 0:n], mixT[:, :, i * P:i * P + n], ACT.Copy), s["mh_hi"])

            def h2T_out(i):
                n = rows(i)
                act.wait_ge(s["t2_done"], i + 1)
                if i >= 2:
                    m_wait(act, f"lg{i - 2}")
                src = ps[:, 4:6, :].rearrange("p b (k t) -> p (b k) t", t=P)
                do(A(h2T[:, i % 2, :, 0:n], src[:, :, 0:n], ACT.Copy), s["h2T_ready"])

            mix_hi(0)
            for k in range(KC):
                part_hi(NPIECE + k)
            for i in range(TILES + 1):
                if i + 1 < TILES:
                    mix_hi(i + 1)
                if i >= 1:
                    h2T_out(i - 1)
                if i < TILES:
                    act.wait_ge(s["x1_ready"], i + 1)
                    square(i, 1)
            act.wait_ge(s["gex_in"], 1)
            do(A(gex[:], gex[:], ACT.Exp), s["gex_out"])

            def expert_hT(i, j):
                b = i * LAP + j
                act.wait_ge(s["xt_done"], b + 1)
                if not (isinstance(b, int) and b < 2):
                    act.wait_ge(s["gu_done"], b - 1)
                src = ps[:, 0:2, :].rearrange("p b (k t) -> p (b k) t", t=P)
                nc.scalar.activation(hTm[:, j % 2, :, :], src, ACT.Copy).then_inc(s["htm_ready"], 1)

            def expert_silu(i, j):
                b = i * LAP + j
                act.wait_ge(s["gu_done"], b + 1)
                if not (isinstance(b, int) and b < 2):
                    act.wait_ge(s["act_ready"], b - 1)
                nc.scalar.activation(sg[:, j % 2, :], ps[:, 2 + j % 2, 0:FF], ACT.Silu)\
                    .then_inc(s["sg_ready"], 1)

            def expert_actT(i, j):
                b = i * LAP + j
                act.wait_ge(s["at_done"], b + 1)
                if not (isinstance(b, int) and b < 2):
                    act.wait_ge(s["d_done"], b - 1)
                nc.scalar.activation(actT[:, j % 2, :], ps[:, 4, 0:P], ACT.Copy)\
                    .then_inc(s["att_ready"], 1)

            def expert_out(i, j):
                b = i * LAP + j
                act.wait_ge(s["d_done"], b + 1)
                if not (isinstance(b, int) and b < 2):
                    act.wait_ge(scat[j % 2], 16 * (i * (LAP // 2) + j // 2))
                nc.scalar.activation(outb[:, j % 2, 0:512], ps[:, 5, :], ACT.Copy)\
                    .then_inc(s["ob_act"], 1)

            def step(i, j, first, last):
                if not last:
                    expert_hT(i, j + 1)
                else:
                    with act.If(total > 0):
                        expert_hT(i, j + 1)
                if not first:
                    expert_actT(i, j - 1)
                expert_silu(i, j)
                if not first:
                    expert_out(i, j - 1)

            act.wait_ge(s["o_done"], TILES)
            expert_hT(0, 0)
            for j in range(LAP):
                step(0, j, first=j == 0, last=False)
            with act.Fori(1, NE // LAP - 1) as i:
                for j in range(LAP):
                    step(i, j, first=False, last=False)
            act.wait_ge(s["ov_ready"], 1)
            total = act.value_load(ovt[0:1, 2 * OVER:2 * OVER + 1], min_val=0, max_val=OVER)
            for j in range(LAP):
                step(NE // LAP - 1, j, first=False, last=j == LAP - 1)
            with act.If(total < 1):
                expert_actT(NE // LAP - 1, LAP - 1)
                expert_out(NE // LAP - 1, LAP - 1)
            with act.Fori(0, OVER // LAP) as i:
                with act.If(i * LAP < total):
                    for j in range(LAP):
                        with act.If(i * LAP + j < total):
                            with act.If(i * LAP + j + 1 < total):
                                expert_hT(i + NE // LAP, j + 1)
                            expert_actT(i + NE // LAP, j - 1)
                            expert_silu(i + NE // LAP, j)
                            expert_out(i + NE // LAP, j - 1)
                            with act.If(i * LAP + j + 2 > total):
                                expert_actT(i + NE // LAP, j)
                                expert_out(i + NE // LAP, j)

            def scaled(i):
                act.wait_ge(s["rs_ready"], 2 * TILES + i + 1)
                do(A(x1[:, i, :], x1[:, i, :], ACT.Copy, scale=rs[:, 2, i:i + 1]), s["y_scaled"])

            act.wait_ge(s["moe_done"], 1)
            for i in range(TILES):
                n = rows(i)
                act.wait_ge(s["y_sum"], i + 1)
                square(i, 2)
                if 1 <= i <= Y_POOL:
                    scaled(i - 1)
                if i >= 2:
                    result_out(act, i - 2)
            result_out(act, TILES - 2)
            result_out(act, TILES - 1)

        @block.gpsimd
        def _(pool):
            do = Chain(pool, s["pool_chain"])
            g = nc.gpsimd
            do(g.memset(ident[:], 0.0))
            do(g.affine_select(out=ident[:], in_=ident[:], compare_op=ALU.not_equal, fill=1.0, base=0,
                               pattern=[[-1, P]], channel_multiplier=1))
            do(g.memset(mhalf[:], -0.5), s["ident_ready"])

            def inv_root(norm, i, n, scale):
                do(g.tensor_scalar(ss[0:n, norm, i:i + 1], ss[0:n, norm, i:i + 1], scale, EPS,
                                   ALU.mult, ALU.add))
                do(g.tensor_tensor(rs[0:n, norm, i:i + 1], ss[0:n, norm, i:i + 1], mhalf[0:n, 0:1],
                                   ALU.pow), s["rs_ready"])

            def rms(norm, i):
                pool.wait_ge(s["sq_done"], norm * TILES + i + 1)
                inv_root(norm, i, rows(i), 1.0 / D)

            do(g.memset(rw[:, :, NG:8], 0.0))
            do(g.memset(rb[:, NG:8], -3.0e38), s["pads_ready"])
            def part_lo(p):
                hi_wait(pool, p)
                if p < NPIECE:
                    slot_wait(pool, p)
                    hi, lo = piece_slot(p)[:, 0, :], piece_slot(p)[:, 1, :]
                else:
                    hi, lo = wo[:, 0, p - NPIECE, :], wo[:, 1, p - NPIECE, :]
                do(g.tensor_tensor(lo, landing(p)[0], hi.bitcast(F32), ALU.subtract), s["lo_pool"])

            rms(0, 0)
            rms(0, 1)
            do(g.memset(pw[:], 0.0), s["zero_ready"])
            rms(0, 2)
            do(g.memset(wsb[:], 0.0))
            do(g.memset(ones[:], 1.0))
            do(g.memset(avg[:], 1.0 / W))
            do(g.affine_select(out=upper[:], in_=ones[:], compare_op=ALU.is_gt, fill=0.0, base=0,
                               pattern=[[1, P]], channel_multiplier=-1))
            rms(0, 3)
            for c in range(2):
                do(g.memset(uc[:, c, 0:HC], 0.0))
            do(g.memset(epsc[:], EPS))
            do(g.memset(mv[:], 1.0))
            do(g.memset(carry[:], 0.0))
            rms(0, 4)
            part_lo(0)
            rms(0, 5)
            rms(0, 6)
            for c in range(2):
                for h in range(2):
                    do(g.memset(iwin[h * 64:h * 64 + 64, c:c + 1], 1.0 / (2 << (2 * c + h))))
                    do(g.memset(topm[h * 64:h * 64 + 64, :], float(h)))
            flt = dict(allow_small_or_imprecise_dtypes=True)
            do(g.iota(icnt[:], [[0, 2], [1, HP]], base=1, channel_multiplier=0, **flt))
            do(g.iota(io4[:], [[1, NG]], base=0, channel_multiplier=0, **flt))
            do(g.iota(io32[:], [[1, NE]], base=0, channel_multiplier=0, **flt))
            do(g.iota(iob[:], [[1, OVER]], base=0, channel_multiplier=0, **flt))
            do(g.iota(pid[:], [[2 * P, TILES], [1, 2]], base=1, channel_multiplier=2, **flt),
               s["const_ready"])
            for i in range(7, TILES):
                rms(0, i)

            for n, p in enumerate(SPLITS[1:8], 1):
                part_lo(p)
                if p == 6:
                    pool.wait_ge(s["uc_ready"], 2)
                    mf_wait(pool, "ws")
                    for k in range(POOL_TAPS):
                        for y, x in zip(mix_parts(7), work(uc[:, 1, :], HC, HC - k)):
                            if k == 0:
                                do(g.tensor_scalar(y, x, par[:, 1, 0:1], par[:, 1, 35:36], ALU.mult,
                                                   ALU.add))
                            else:
                                t = mix_parts(6)[len(y.shape) - 2]
                                do(g.tensor_scalar(t, x, par[:, 1, k:k + 1], 0.0, ALU.mult, ALU.add))
                                do(g.tensor_tensor(y, y, t, ALU.add))
                    do(g.memset(pooljunk[:], 0.0), s["taps_begun"])
                if n == 3:
                    mf_wait(pool, "ws")
                    do(g.affine_select(out=wsT[:], in_=wsT[:], compare_op=ALU.is_ge, fill=0.0, base=0,
                                       pattern=[[0, NG], [1, P]], channel_multiplier=-1), s["wsT_masked"])
            pool.wait_ge(s["v_stats"], 1)
            do(g.tensor_scalar(rsd[:], mv[:, :, 1], 1.0, EPS, ALU.mult, ALU.add))
            do(g.tensor_tensor(rsd[:], rsd[:], mhalf[:], ALU.pow), s["v_rsd"])
            part_lo(8)
            pool.wait_ge(s["v_norm"], 1)
            pool.wait_ge(s["ln_d_in"], 16 * 2)
            full = [P, LAST, W]
            do(g.tensor_tensor(vall[:, 0:LAST, :], vall[:, 0:LAST, :],
                               lng[:].unsqueeze(1).broadcast_to(full), ALU.mult))
            do(g.tensor_tensor(vall[:, 0:LAST, :], vall[:, 0:LAST, :],
                               lnb[:].unsqueeze(1).broadcast_to(full), ALU.add))
            do(g.tensor_tensor(vall[0:NS, LAST, :], vall[0:NS, LAST, :], lng[0:NS, :], ALU.mult))
            do(g.tensor_tensor(vall[0:NS, LAST, :], vall[0:NS, LAST, :], lnb[0:NS, :], ALU.add),
               s["v_ready"])
            for p in range(9, NPIECE):
                part_lo(p)
                if p == 11:
                    m_wait(pool, f"sp{LAST}")
                    pool.wait_ge(s["wsb_in"], 16 * SB)
                    do(g.iota(cols, [[1, TCOLS]], base=0, channel_multiplier=0, **flt),
                       s["cols_ready"])
            for k in POOL_LO:
                part_lo(NPIECE + k)

            for i in range(TILES):
                rms(1, i)

            last_token, last_pair = pool.to_reg(NT - 1), pool.to_reg(2 * NT - 1)

            def by_size(pairs, move):
                def has(r):
                    return pool.value_load(pairs[r:r + 1, :], min_val=0, max_val=NONE) < NONE

                with pool.If(has(2 * Q)):
                    with pool.If(has(3 * Q)):
                        move(4 * Q)
                    with pool.Else():
                        move(3 * Q)
                with pool.Else():
                    with pool.If(has(Q)):
                        move(2 * Q)
                    with pool.Else():
                        move(Q)

            def gather(b, index, pairs, free=None):
                def move(n):
                    if free is not None:
                        pool.wait_ge(s["xt_done"], free)
                    g.indirect_dma_start(xg[0:n, b % XG, :], None, hs,
                                         bass.IndirectOffsetOnAxis(ap=index[0:n, :], axis=0),
                                         bounds_check=last_token, oob_is_err=False)\
                        .then_inc(gath[b % XG], 16)

                if b == 0:
                    move(P)
                else:
                    by_size(pairs, move)

            def scatter(b, index):
                def move(n):
                    pool.wait_ge(s["ob_act"], b + 1)
                    pool.wait_ge(s["ob_dve"], b + 1)
                    g.indirect_dma_start(orow, bass.IndirectOffsetOnAxis(ap=index[0:n, :], axis=0),
                                         outb[0:n, b % 2, :], None, bounds_check=last_pair,
                                         oob_is_err=False).then_inc(scat[b % 2], 16)

                by_size(index, move)

            pool.wait_ge(s["o_done"], TILES)
            do(g.memset(xg[:].rearrange("p s d -> p (s d)"), 0.0), s["xg_zero"])
            for k in range(2):
                pool.wait_ge(h2_stored[k], 16 * ((TILES + 1 - k) // 2))
            pool.wait_ge(s["idx_ready"], 1)
            def gather_over(o):
                with pool.If(total > o):
                    col = pool.value_load(ovt[0:1, OVER + o:OVER + o + 1], min_val=0,
                                          max_val=TCOLS - 1)
                    do(g.tensor_copy(gcol[:, o:o + 1], gidxs[:, bass.ds(col, 1)]), s["gcol_ready"])
                    do(g.tensor_copy(scol[:, o:o + 1], tab[:, bass.ds(col, 1)]), s["scol_ready"])
                    gather(NE + o, gcol[:, o:o + 1], scol[:, o:o + 1], NE + o - 3)

            for b in range(-3, NE + 1):
                if b + 3 < NE:
                    c = (b + 3) * CAPB
                    gather(b + 3, gidxs[:, c:c + 1], tab[:, c:c + 1], b if b >= 1 else None)
                else:
                    if b + 3 == NE:
                        pool.wait_ge(s["ov_ready"], 1)
                        total = pool.value_load(ovt[0:1, 2 * OVER:2 * OVER + 1], min_val=0,
                                                max_val=OVER)
                    gather_over(b + 3 - NE)
                if b >= 1:
                    c = (b - 1) * CAPB
                    scatter(b - 1, tab[:, c:c + 1])

            def all_scattered(n):
                for k in range(2):
                    pool.wait_ge(scat[k], 16 * ((n + 1 - k) // 2))

            def over_from(o):
                if o == OVER:
                    return
                with pool.If(total > o):
                    if o + 4 < OVER:
                        gather_over(o + 4)
                    scatter(NE + o, scol[:, o:o + 1])
                    with pool.If(total < o + 2):
                        all_scattered(NE + o + 1)
                    over_from(o + 1)

            with pool.If(total < 1):
                all_scattered(NE)
            over_from(0)
            do(g.memset(gcol[:, 0:1], 0), s["moe_done"])
            pool.wait_ge(s["gain_fin_in"], 16)
            for i in range(TILES):
                rms(2, i)
                if 1 <= i <= Y_POOL:
                    pool.wait_ge(s["y_scaled"], i)
                    do(g.tensor_tensor(x1[:, i - 1, :], x1[:, i - 1, :], gain[:], ALU.mult), s["y_pool"])

        @block.vector
        def _(dve):
            do = Chain(dve, s["dve_chain"])
            v = nc.vector
            stt, tt, ts = v.scalar_tensor_tensor, v.tensor_tensor, v.tensor_scalar

            def normed(i, norm, done):
                n = rows(i)
                do(stt(wk[0:n, i % 2, 0:D].rearrange("p (k q) -> p q k", k=KC),
                       x1[0:n, i, :].rearrange("p (q k) -> p q k", k=KC), rs[0:n, norm, i:i + 1],
                       gain[0:n, :].rearrange("p (q k) -> p q k", k=KC), ALU.mult, ALU.mult), s[done])

            def hT_lo(i):
                n = rows(i)
                dve.wait_ge(s["ht_hi"], i + 1)
                src = ps[:, 3 + 2 * (i % 2):5 + 2 * (i % 2), :].rearrange("p b (k t) -> p (b k) t", t=P)
                do(tt(hT[:, 1, :, i * P:i * P + n], src[:, :, 0:n],
                      hT[:, 0, :, i * P:i * P + n].bitcast(F32), ALU.subtract), s["ht_lo"])

            dve.wait_ge(s["gain_mix_in"], 16)
            for i in range(TILES + 2):
                if i < TILES:
                    dve.wait_ge(s["rs_ready"], i + 1)
                    if i >= 2:
                        dve.wait_ge(s["ht_T"], i - 1)
                    normed(i, 0, "h_ready")
                if i >= 2:
                    hT_lo(i - 2)
            dve.wait_ge(s["const_ready"], 1)
            for c in range(2):
                for h in range(2):
                    q = slice(h * 64, h * 64 + 64)
                    do(ts(icnt[q, c, :], icnt[q, c, :], float(2 << (2 * c + h)), None, ALU.min))
            do(v.reciprocal(icnt[:], icnt[:]))

            def glu(c, p):
                name = f"ca{c}"
                wait_piece(dve, p)
                mf_wait(dve, "stc")
                zf_wait(dve, f"cg{c}")
                gp = z_parts(name, *mix_parts(c))
                for n, (dst, src) in enumerate(z_parts(name, *work(uc[:, c, :], HC))):
                    do(tt(dst, src, gp[n][0], ALU.mult), s["zf_dve"] if n == 2 else None)
                do(v.tensor_copy(sc[:, 7:8], ones[:, 0:1]), s["uc_ready"])

            def taps_c(c, k0, k1):
                for k in range(k0, k1):
                    xs = work(uc[:, c, :], HC, HC - k)
                    for y, x in zip(mix_parts(4 + c), xs):
                        if c == 1 and k == POOL_TAPS:
                            part = mix_parts(7)[len(y.shape) - 2]
                            do(stt(y, x, par[:, c, k:k + 1], part, ALU.mult, ALU.add),
                               s["begun_used"] if len(y.shape) == 3 else None)
                        elif k == 0:
                            do(ts(y, x, par[:, c, 0:1], par[:, c, 35:36], ALU.mult, ALU.add))
                        else:
                            do(stt(y, x, par[:, c, k:k + 1], y, ALU.mult, ALU.add))

            glu(0, 1)
            mf_wait(dve, "par")
            taps_c(0, 0, 14)
            glu(1, 3)
            taps_c(0, 14, 31)
            mf_wait(dve, f"v{LAST}")
            for i in range(TILES):
                n = rows(i)
                do(v.bn_stats(st6[0:n, i, :], vall[0:n, i, :]))
            for i in range(TILES):
                n = rows(i)
                do(v.bn_aggr(mv[0:n, i, :], st6[0:n, i, :]), s["v_stats"] if i == LAST else None)
            dve.wait_ge(s["v_rsd"], 1)
            for i in range(TILES):
                n = rows(i)
                do(ts(vall[0:n, i, :], vall[0:n, i, :], mv[0:n, i, 0:1], rsd[0:n, i:i + 1],
                      ALU.subtract, ALU.mult), s["v_norm"] if i == LAST else None)
            dve.wait_ge(s["taps_begun"], 1)
            taps_c(1, POOL_TAPS, 14)
            wait_piece(dve, 7)
            dve.wait_ge(s["late_in"], 16 * 8)
            zf_wait(dve, "du1")
            for i in range(TILES):
                name = f"sp{i}"
                m_wait(dve, name)
                b = ps[:, m_bank(name), :]
                if i < LAST:
                    do(tt(sptmp[:], b[:, 0:W].rearrange("p (c t) -> p c t", c=2), biasd[:], ALU.add),
                       s["mf_dve"])
                else:
                    for c in range(2):
                        do(tt(sptmp[:, c, 0:NS].rearrange("p (b t) -> p b t", b=SB),
                              b[:, c * P:c * P + NS].rearrange("p (b t) -> p b t", b=SB),
                              biasd[:, c, 0:ST].unsqueeze(1).broadcast_to([P, SB, ST]), ALU.add),
                           s["mf_dve"] if c == 1 else None)
                m = mixT[:, 6:8, i * P:i * P + rows(i)]
                do(tt(m, m, sptmp[:, :, 0:rows(i)], ALU.mult), s["sp_done"] if i == LAST else None)
            def pooled(c):
                n = HP + NP + SB * (HP + ST)
                row = [wk[:, r, :] for r in range(3)]
                dve.wait_ge(s["px_ready"], c + 1)
                if c == 1:
                    m_wait(dve, "pm02")
                steps = [(0, 1)] if c == 0 else [(0, 1), (1, 2), (2, 4)]
                src, lo_, at_ = row[0], 0, 0
                turn = [row[1], row[2]] if c == 0 else [row[2], row[1], row[2], row[1]]
                for k, shift in steps:
                    dst = turn[at_]
                    at_ += 1
                    lo_ += shift
                    do(tt(dst[:, lo_:n], src[:, lo_:n], src[:, lo_ - shift:n - shift], ALU.add))
                    src = dst
                shift = 2 if c == 0 else 8
                dst = turn[at_]
                do(stt(dst[:, HP:n], src[:, HP - shift:n - shift], topm[:, 0:1], src[:, HP:n],
                       ALU.mult, ALU.add))
                d = row[1 + c]
                for y, x, z in zip(work(d, HP), work(dst, HP), work(row[0], HP)):
                    if y.shape == [P, NP] or len(y.shape) == 2:
                        do(tt(y[:, 0:HP], x[:, 0:HP], icnt[:, c, :], ALU.mult))
                        do(tt(y[:, 0:HP], y[:, 0:HP], z[:, 0:HP], ALU.subtract))
                        y, x, z = y[:, HP:], x[:, HP:], z[:, HP:]
                    do(stt(y, x, iwin[:, c:c + 1], z, ALU.mult, ALU.subtract))
                do(v.tensor_copy(sc[:, 7:8], ones[:, 0:1]), s["pd_ready"])

            pooled(0)
            taps_c(1, 14, 18)
            pooled(1)
            taps_c(1, 18, 31)
            do(v.tensor_copy(sc[:, 7:8], ones[:, 0:1]), s["conv_ready"])

            def a_input(c, p):
                name = f"ax{c}"
                wait_piece(dve, p)
                dve.wait_ge(s["ac_ready"], c + 1)
                gp = z_parts(name, *mix_parts(c))
                for n, (dst, src) in enumerate(z_parts(name, *work(wk[:, c, :], HA))):
                    do(tt(dst, src, gp[n][0], ALU.mult), s["zf_dve"] if n == 2 else None)
                do(v.tensor_copy(sc[:, 7:8], ones[:, 0:1]), s["ua_ready"])

            def a_taps(c):
                for k in range(3):
                    w = par[:, c, 31 + k:32 + k]
                    for y, x in zip(mix_parts(c), work(wk[:, c, :], HA, HA - k)):
                        if k == 0:
                            do(ts(y, x, w, None, ALU.mult))
                        else:
                            do(stt(y, x, w, y, ALU.mult, ALU.add))

            def mix_lo(i):
                n = rows(i)
                dve.wait_ge(s["mh_hi"], i + 1)
                hi, low = (ring[:, 1 - i % 2, m, :].rearrange("p (k t) -> p k t", k=KC)[:, :, 0:n]
                           for m in range(2))
                do(tt(low, mixT[:, :, i * P:i * P + n], hi.bitcast(F32), ALU.subtract), s["mh_lo"])

            def a_gate(c, p):
                name = f"ab{c}"
                if c == 0:
                    wait_piece(dve, p)
                else:
                    dve.wait_ge(s["ab1_first"], 1)
                for n, (dst, src) in enumerate(z_parts(name, *mix_parts(c))):
                    do(tt(dst, dst, src, ALU.mult), s["mix_first"] if n == 0 and c == 1 else
                       s["zf_dve"] if n == 2 else None)
                    if n == 0 and c == 1:
                        mix_lo(0)
                        wait_piece(dve, p)

            def c_mean(r):
                t0, t1 = LN_RANGES[r]
                name = f"mean{r}"
                m_wait(dve, name)
                y = mixT[:, 4:6, t0:t1]
                mean = ps[:, m_bank(name), 0:t1 - t0].unsqueeze(1).broadcast_to([P, 2, t1 - t0])
                do(tt(y, y, mean, ALU.subtract), s["mf_dve"])
                do(v.tensor_copy(sc[:, 7:8], ones[:, 0:1]), s["c_mean"])

            def c_norm(r):
                t0, t1 = LN_RANGES[r]
                mf_wait(dve, f"var{r}")
                d = lnsq2[:, 0, :] if r == 2 else lnsq[:, r, 0, :]
                y = mixT[:, 4:6, t0:t1]
                do(v.reciprocal(d, d))
                do(tt(y, y, d.unsqueeze(1).broadcast_to([P, 2, t1 - t0]), ALU.mult),
                   s["c_norm"] if r == 2 else None)

            a_input(0, 11)
            a_taps(0)
            for r in range(3):
                c_mean(r)
            a_input(1, 13)
            a_taps(1)
            for r in range(3):
                c_norm(r)
            a_gate(0, 14)
            a_gate(1, 15)
            do(v.tensor_copy(sc[:, 7:8], ones[:, 0:1]), s["mix_ready"])

            def wo_lo(k):
                hi_wait(dve, NPIECE + k)
                do(tt(wo[:, 1, k, :], landing(NPIECE + k)[0], wo[:, 0, k, :].bitcast(F32),
                      ALU.subtract), s["lo_dve"])

            def residual(i):
                n = rows(i)
                dve.wait_ge(s["o_done"], i + 1)
                b = 2 * (i % 2)
                do(tt(x1[0:n, i, :].rearrange("p (r d) -> p r d", r=2),
                      x1[0:n, i, :].rearrange("p (r d) -> p r d", r=2), ps[0:n, b:b + 2, :], ALU.add),
                   s["x1_ready"])

            def route(i):
                n = rows(i)
                q = slice(0, n)
                name = f"lg{i}"
                z = i % 2
                m_wait(dve, name)
                do(tt(lge[q, i, :], m_area(name)[q, 0:8 + NE], rb[q, :], ALU.add), s["mf_dve"])
                do(v.max(m8[q, i, :], lge[q, i, 0:8]))
                do(v.max_index(i8[q, :], m8[q, i, :], lge[q, i, 0:8]))
                do(v.tensor_copy(gidx[q, :], i8[q, 0:1]))
                do(ts(goh[q, :], io4[q, :], gidx[q, :], None, ALU.is_equal))
                le = lge[q, i, 8:].rearrange("p (g e) -> p g e", g=NG)
                do(tt(rjunk[q, :].rearrange("p (g e) -> p g e", g=NG), le,
                      goh[q, :].unsqueeze(2).broadcast_to([n, NG, EG]), ALU.mult))
                do(v.tensor_reduce(sel8[q, :], rjunk[q, :].rearrange("p (g e) -> p e g", g=NG), AX_X,
                                   ALU.add))
                do(v.max(n8[q, i, :], sel8[q, :]))
                do(v.max_index(j8[q, :], n8[q, i, :], sel8[q, :]))
                do(ts(sc[q, 2:3], gidx[q, :], float(EG), None, ALU.mult))
                do(ts(eidx[q, z, :], j8[q, 0:2], sc[q, 2:3], None, ALU.add))
                grid = [n, 2, NE]
                do(tt(oh[q, z, :, :], io32[q, :].unsqueeze(1).broadcast_to(grid),
                      eidx[q, z, :].unsqueeze(2).broadcast_to(grid), ALU.is_equal))
                do(tt(msum[q, z, :], oh[q, z, 0, :], oh[q, z, 1, :], ALU.add), s["m_onehot"])

            def places(i):
                n = rows(i)
                q = slice(0, n)
                name = f"cum{i}"
                z = i % 2
                m_wait(dve, name)
                b = m_area(name)
                do(tt(rank[q, :], b[q, 0:NE], carry[q, :], ALU.add))
                do(tt(carry[:], b[:, NE:2 * NE], carry[:], ALU.add), s["mf_dve"])
                for k in range(2):
                    do(stt(rjunk[q, :], rank[q, :], 0.0, oh[q, z, k, :], ALU.add, ALU.mult,
                           accum_out=rk[q, k:k + 1]))
                do(v.tensor_copy(rki[q, :], rk[q, :]))
                do(ts(rlo[q, :], rki[q, :], P - 1, None, ALU.bitwise_and))
                do(ts(rhi[q, :], rki[q, :], 7, None, ALU.logical_shift_right))
                do(v.tensor_copy(row[q, :], rlo[q, :]))
                do(stt(col[q, :], eidx[q, z, :], float(CAPB), rhi[q, :], ALU.mult, ALU.add))

            def table_parts(i):
                n = rows(i)
                q = slice(0, n)
                if i == 0:
                    dve.wait_ge(s["cols_ready"], 1)
                else:
                    dve.wait_ge(s["table_added"], i)
                for k in range(2):
                    do(ts(prow[q, k, :], cols[q, 0:P], row[q, k:k + 1], None, ALU.is_equal))
                for k in range(2):
                    do(ts(pcol[q, k, :], cols[q, :], col[q, k:k + 1], pid[q, i, k:k + 1],
                          ALU.is_equal, ALU.mult), s["place_ready"] if k == 1 else None)

            for k in range(KC):
                if k not in POOL_LO:
                    wo_lo(k)
            dve.wait_ge(s["gain_ffn_in"], 16)
            dve.wait_ge(s["stage_out"], 16 * 7)
            do(v.memset(flat[:], 0.0))
            for i in range(TILES + 2):
                if i + 1 < TILES:
                    mix_lo(i + 1)
                if i >= 2:
                    places(i - 2)
                    if i < TILES:
                        table_parts(i - 2)
                if i < TILES:
                    residual(i)
                    dve.wait_ge(s["rs_ready"], TILES + i + 1)
                    if i >= 2:
                        dve.wait_ge(s["t2_done"], i - 1)
                        dve.wait_ge(h2_stored[i % 2], 16 * (i // 2))
                    normed(i, 1, "h2_ready")
                if 1 <= i <= TILES:
                    route(i - 1)
                if i >= TILES:
                    table_parts(i - 2)

            dve.wait_ge(s["table_added"], TILES)
            do(ts(empty[:], ps[:, 7, 0:TCOLS], 0.0, float(NONE + 1), ALU.is_equal, ALU.mult))
            do(stt(tab[:], empty[:], -1.0, ps[:, 7, 0:TCOLS], ALU.add, ALU.add))
            do(ts(gidxs[:], tab[:], 1, None, ALU.logical_shift_right), s["idx_ready"])
            full = [P, TILES, NG]
            do(tt(gex[:, :, 0:NG], lge[:, :, 0:NG], m8[:, :, 0:1].broadcast_to(full), ALU.subtract))
            do(tt(gex[:, :, NG:NG + 1], n8[:, :, 1:2], n8[:, :, 0:1], ALU.subtract), s["gex_in"])
            n_e, incl = ov[:, 0, :], ov[:, 1, :]
            do(ts(ovi[:], carry[0:1, :], float(P - 1), None, ALU.add))
            do(ts(ovi[:], ovi[:], 7, None, ALU.logical_shift_right))
            do(ts(n_e, ovi[:], 1.0, -1.0, ALU.max, ALU.add))
            do(v.tensor_tensor_scan(incl, ones[0:1, 0:NE], n_e, 0.0, ALU.mult, ALU.add))
            grid = [1, OVER, NE]
            for k in range(2):
                dve.wait_ge(h2_stored[k], 16 * ((TILES + 1 - k) // 2))
            do(tt(otmp[:], incl.unsqueeze(1).broadcast_to(grid), iob[:].unsqueeze(2).broadcast_to(grid),
                  ALU.is_le))
            do(v.tensor_reduce(ovb[:, 0, :], otmp[:], AX_X, ALU.add))
            do(tt(otmp2[:], otmp[:], n_e.unsqueeze(1).broadcast_to(grid), ALU.mult))
            do(v.tensor_reduce(ovb[:, 1, :], otmp2[:], AX_X, ALU.add))
            do(ts(ovb[:, 0, :], ovb[:, 0, :], float(NE - 1), None, ALU.min))
            do(v.tensor_copy(ovt[:, 0:OVER], ovb[:, 0, :]))
            do(tt(ovb[:, 2, :], iob[:], ovb[:, 1, :], ALU.subtract))
            do(stt(ovb[:, 2, :], ovb[:, 0, :], float(CAPB), ovb[:, 2, :], ALU.mult, ALU.add))
            do(ts(ovb[:, 2, :], ovb[:, 2, :], 1.0, float(TCOLS - 1), ALU.add, ALU.min))
            do(v.tensor_copy(ovt[:, OVER:2 * OVER], ovb[:, 2, :]))
            do(v.tensor_copy(ovt[:, 2 * OVER:2 * OVER + 1], incl[:, NE - 1:NE]), s["ov_ready"])

            def expert_act(i, j):
                b = i * LAP + j
                dve.wait_ge(s["sg_ready"], b + 1)
                if not (isinstance(b, int) and b < 2):
                    dve.wait_ge(s["at_done"], b - 1)
                v.tensor_tensor(actv[:, j % 2, :], sg[:, j % 2, :], ps[:, 2 + j % 2, FF:2 * FF],
                                ALU.mult).then_inc(s["act_ready"], 1)

            def expert_out(i, j):
                b = i * LAP + j
                dve.wait_ge(s["d_done"], b + 1)
                if not (isinstance(b, int) and b < 2):
                    dve.wait_ge(scat[j % 2], 16 * (i * (LAP // 2) + j // 2))
                v.tensor_copy(outb[:, j % 2, 512:D], ps[:, 6, :]).then_inc(s["ob_dve"], 1)

            def step(i, j, first):
                expert_act(i, j)
                if not first:
                    expert_out(i, j - 1)

            for j in range(LAP):
                step(0, j, first=j == 0)
            with dve.Fori(1, NE // LAP) as i:
                for j in range(LAP):
                    step(i, j, first=False)
            total = dve.value_load(ovt[0:1, 2 * OVER:2 * OVER + 1], min_val=0, max_val=OVER)
            with dve.If(total < 1):
                expert_out(NE // LAP - 1, LAP - 1)
            with dve.Fori(0, OVER // LAP) as i:
                with dve.If(i * LAP < total):
                    for j in range(LAP):
                        with dve.If(i * LAP + j < total):
                            expert_act(i + NE // LAP, j)
                            expert_out(i + NE // LAP, j - 1)
                            with dve.If(i * LAP + j + 2 > total):
                                expert_out(i + NE // LAP, j)

            dve.wait_ge(s["gex_out"], 1)
            do(v.tensor_reduce(gsum[:], gex[:, :, 0:NG], AX_X, ALU.add))
            do(ts(gates[:, :, 0], gex[:, :, NG], 1.0, None, ALU.add))
            do(tt(gates[:, :, 0], gates[:, :, 0], gsum[:], ALU.mult))
            do(v.reciprocal(gates[:, :, 0], gates[:, :, 0]))
            do(tt(gates[:, :, 1], gates[:, :, 0], gex[:, :, NG], ALU.mult))

            dve.wait_ge(s["moe_done"], 1)
            dve.wait_ge(s["gain_fin_in"], 16)
            for i in range(TILES + 1):
                if i < TILES:
                    n = rows(i)
                    dve.wait_ge(pair_in[i], 16)
                    for k in range(2):
                        do(stt(x1[0:n, i, :], opair[0:n, i, k * D:(k + 1) * D],
                               gates[0:n, i, k:k + 1], x1[0:n, i, :], ALU.mult, ALU.add),
                           s["y_sum"] if k == 1 else None)
                if i >= 1:
                    m = i - 1
                    n = rows(m)
                    if m < Y_POOL:
                        continue
                    dve.wait_ge(s["rs_ready"], 2 * TILES + m + 1)
                    do(stt(x1[0:n, m, :], x1[0:n, m, :], rs[0:n, 2, m:m + 1], gain[0:n, :], ALU.mult,
                           ALU.mult), s["y_done"])

        @block.tensor
        def _(pe):
            def m_open(name):
                n = M_AT[name]
                if n >= 2:
                    mf_wait(pe, M_USES[n - 2][0])
                if name[:2] == "lg" or name[:3] == "cum":
                    mf_wait(pe, M_USES[n - 1][0])
                return m_area(name)

            def transposes(i, banks):
                n = rows(i)
                for k in range(KC):
                    mm = pe.transpose(ps[:, banks + k // 4, k % 4 * P:k % 4 * P + n],
                                      wk[0:n, i % 2, k * P:(k + 1) * P], ident[0:n, 0:n])
                return mm

            pe.wait_ge(s["ident_ready"], 1)
            def first_piece(r, k0, k1):
                t0, t1 = RANGES[r]
                pe.wait_ge(s["ht_lo"], 3 * r + 3)
                for k in range(k0, k1):
                    for wpart, hpart in ((0, 0), (0, 1), (1, 0)):
                        mm = pe.matmul(ps[:, r, 0:t1 - t0], ring[:, 0, wpart, k * P:(k + 1) * P],
                                       hT[:, hpart, k, t0:t1], start=(k, wpart, hpart) == (0, 0, 0),
                                       stop=(k, wpart, hpart) == (KC - 1, 1, 0))
                return mm

            for i in range(TILES):
                pe.wait_ge(s["h_ready"], i + 1)
                if i >= 2:
                    pe.wait_ge(s["ht_lo"], i - 1)
                transposes(i, 3 + 2 * (i % 2)).then_inc(s["ht_T"], 1)
                if i == 4:
                    lo_wait(pe, 0)
                    first_piece(0, 0, 4)
                if i == 5:
                    first_piece(0, 4, KC)
                if i == 7:
                    first_piece(1, 0, 4)
            first_piece(1, 4, KC)
            first_piece(2, 0, KC).then_inc(s["piece_done"], 1)

            def z(p):
                name = PIECES[p][0]
                n = ZS.index(name)
                lo_wait(pe, p)
                if n >= 2:
                    user = Z_USER[n - 2]
                    pe.wait_ge(s["zf_" + user], nth(Z_USER, n - 2))
                args = (pe, ps, piece_slot(p), hT, z_bank(name))
                if p < NPIECE - 1:
                    piece_matmuls(*args).then_inc(s["piece_done"], 1)
                else:
                    piece_matmuls(*args, ranges=(0, 1)).then_inc(s["ab1_first"], 1)
                    piece_matmuls(*args, ranges=(2,)).then_inc(s["piece_done"], 1)

            pe.wait_ge(s["small_in"], 16 * 10)
            b = m_open("par")
            for c in range(2):
                mm = pe.transpose(b[:, c * 64:c * 64 + NPAR], par_rows[0:NPAR, c * P:(c + 1) * P],
                                  ident[0:NPAR, 0:NPAR])
            mm.then_inc(s["m_ready"], 1)
            b = m_open("stc")
            for c in range(2):
                for h in range(2):
                    q = (2 * c + h) * 120
                    mm = pe.transpose(b[:, q:q + 120], st_rows[0:120, h, c * P:(c + 1) * P],
                                      ident[0:120, 0:120])
            mm.then_inc(s["m_ready"], 1)
            z(1)
            b = m_open("stpa")
            for r, n, q in ((2, SB * HP, 0), (3, SB * HA, 240)):
                for c in range(2):
                    mm = pe.transpose(b[:, q + c * n:q + (c + 1) * n], st_rows[0:n, r, c * P:(c + 1) * P],
                                      ident[0:n, 0:n])
            mm.then_inc(s["m_ready"], 1)
            b = m_open("ws")
            pe.wait_ge(s["ws_in"], 16)
            for h in range(NG):
                mm = pe.transpose(b[:, h * P:(h + 1) * P], ws_rows[:, h, :], ident[:])
            mm.then_inc(s["m_ready"], 1)
            z(2)
            z(3)
            lo_wait(pe, 5)
            lo_wait(pe, 4)
            vw = vpair[:, :, 0:2 * D].rearrange("p s (part n) -> p s part n", part=2)
            for i in range(TILES):
                n = rows(i)
                b = m_open(f"v{i}")
                for k in range(KC):
                    for hpart, wpart in ((0, 0), (0, 1), (1, 0)):
                        mm = pe.matmul(b[0:n, 0:W].rearrange("p (s c) -> p s c", s=2),
                                       hT[:, hpart, k, i * P:i * P + n],
                                       vw[:, ::-1, wpart, k * P:(k + 1) * P],
                                       start=(k, hpart, wpart) == (0, 0, 0),
                                       stop=(k, hpart, wpart) == (KC - 1, 1, 0))
                mm.then_inc(s["m_ready"], 1)

            def tails(name, row, hist, keep, halves=1):
                b = m_open(name)
                pe.transpose(b[0:keep, 0:P], row[:, hist + NP - keep:hist + NP], ident[:])
                tail = sptmp[:].rearrange("p c t -> p (c t)")
                pe.wait_ge(s["tail_ready"], [n for n, _ in M_USES if "st" in n and n[-1] in "01"]
                           .index(name) + 1)
                n = SB * keep // halves
                for h in range(halves):
                    mm = pe.transpose(b[0:n, P * (h + 1):P * (h + 2)], tail[:, h * n:(h + 1) * n],
                                      ident[:])
                mm.then_inc(s["m_ready"], 1)

            def conv_tails(c):
                pe.wait_ge(s["uc_ready"], c + 1)
                tails(f"cst{c}", uc[:, c, :], HC, HC, halves=2)

            z(6)
            conv_tails(0)
            z(7)
            conv_tails(1)
            z(8)
            pe.wait_ge(s["v_ready"], 1)
            pe.wait_ge(s["wsb_in"], 16 * SB)
            for i in range(TILES):
                n = rows(i)
                b = m_open(f"sp{i}")
                for h in range(NG):
                    mm = pe.matmul(b[h % 2 * 64:h % 2 * 64 + 64, h // 2 * P:h // 2 * P + n],
                                   vall[0:n, i, h * 64:(h + 1) * 64],
                                   wsT[:, h, :] if i < LAST else wsb[:, h, :], start=True, stop=True)
                mm.then_inc(s["m_ready"], 1)
            z(9)
            pe.wait_ge(s["px_ready"], 1)
            tails("pst0", wk[:, 0, :], HP, HP)

            def pool_product(c):
                pe.wait_ge(s["pd_ready"], c + 1)
                pe.wait_ge(s["pw_in"], 16 * 4)
                prompt, sample = work(wk[:, 1 + c, :], HP)
                for r, (t0, t1) in enumerate(LN_RANGES):
                    b = m_open(f"pm{c}{r}")
                    x = sample if r == 2 else prompt[:, t0:t1]
                    y = b[:, 0:NS].rearrange("p (b t) -> p b t", b=SB) if r == 2 else b
                    pe.matmul(y, pw[:, c, :], x, start=True, stop=True).then_inc(s["m_ready"], 1)

            pool_product(0)
            z(10)
            pe.wait_ge(s["px_ready"], 2)
            tails("pst1", wk[:, 0, :], HP, HP)
            z(11)
            pool_product(1)
            z(12)

            def over_channels(what, r, src):
                n = LN_RANGES[r][1] - LN_RANGES[r][0]
                b = m_open(f"{what}{r}")
                for c in range(2):
                    mm = pe.matmul(b[:, 0:n], avg[:], src[:, c, :], start=c == 0, stop=c == 1)
                mm.then_inc(s["m_ready"], 1)

            pe.wait_ge(s["conv_ready"], 1)
            for r, (t0, t1) in enumerate(LN_RANGES):
                over_channels("mean", r, mixT[:, 4:6, t0:t1])
            z(13)
            pe.wait_ge(s["ua_ready"], 1)
            tails("ast0", wk[:, 0, :], HA, HA)
            for r in range(3):
                pe.wait_ge(s["c_sq"], r + 1)
                over_channels("var", r, lnsq2[:] if r == 2 else lnsq[:, r, :, :])
            z(14)
            pe.wait_ge(s["ua_ready"], 2)
            tails("ast1", wk[:, 1, :], HA, HA)
            z(15)

            def project(i, half):
                n = rows(i)
                b = 2 * (i % 2)
                if half == 0:
                    pe.wait_ge(s["mh_lo"], i + 1)
                    if i >= 2:
                        pe.wait_ge(s["x1_ready"], i - 1)
                for k in range(half * KC // 2, (half + 1) * KC // 2):
                    if i == 0:
                        lo_wait(pe, NPIECE + k)
                    for mpart, wpart in ((0, 0), (0, 1), (1, 0)):
                        for r in range(2):
                            mm = pe.matmul(ps[0:n, b + r, :], ring[:, 1 - i % 2, mpart, k * P:k * P + n],
                                           wo[:, wpart, k, r * 512:(r + 1) * 512],
                                           start=(k, mpart, wpart) == (0, 0, 0),
                                           stop=(k, mpart, wpart) == (KC - 1, 1, 0))
                if half == 1:
                    mm.then_inc(s["o_done"], 1)

            pe.wait_ge(s["mix_ready"], 1)
            def table_add(t):
                n = rows(t)
                pe.wait_ge(s["place_ready"], t + 1)
                for k in range(2):
                    mm = pe.matmul(ps[:, 7, 0:TCOLS], prow[0:n, k, :], pcol[0:n, k, :],
                                   start=(t, k) == (0, 0), stop=(t, k) == (LAST, 1))
                mm.then_inc(s["table_added"], 1)

            for i in range(TILES + 2):
                if i < TILES:
                    project(i, 0)
                if 1 <= i <= TILES:
                    pe.wait_ge(s["h2_ready"], i)
                    if i >= 2:
                        pe.wait_ge(s["h2T_ready"], i - 1)
                    transposes(i - 1, 4).then_inc(s["t2_done"], 1)
                if i >= 2:
                    t = i - 2
                    n = rows(t)
                    b = m_open(f"cum{t}")
                    pe.wait_ge(s["m_onehot"], t + 1)
                    pe.matmul(b[0:n, 0:NE], upper[0:n, 0:n], msum[0:n, t % 2, :], start=True, stop=True)
                    pe.matmul(b[:, NE:2 * NE], ones[0:n, :], msum[0:n, t % 2, :], start=True, stop=True)\
                        .then_inc(s["m_ready"], 1)
                if i == TILES + 1:
                    table_add(LAST - 1)
                if i < TILES:
                    project(i, 1)
                if 1 <= i <= TILES:
                    t = i - 1
                    n = rows(t)
                    b = m_open(f"lg{t}")
                    pe.wait_ge(s["h2T_ready"], t + 1)
                    pe.wait_ge(s["late_in"], 16 * 8)
                    for k in range(KC):
                        mm = pe.matmul(b[0:n, 0:8 + NE], h2T[:, t % 2, k, 0:n], rw[:, k, :],
                                       start=k == 0, stop=k == KC - 1)
                    mm.then_inc(s["m_ready"], 1)
                if 2 <= i < TILES:
                    table_add(i - 2)
            table_add(LAST)

            def early(b, n):
                return isinstance(b, int) and b < n

            def expert_T(i, j):
                b = i * LAP + j
                if not early(b, 1):
                    pe.wait_ge(s["htm_ready"], b)
                pe.wait_ge(gath[j % XG], 16 * (i * (LAP // XG) + j // XG) + 16)
                for k in range(KC):
                    mm = pe.transpose(ps[:, k // 4, k % 4 * P:(k % 4 + 1) * P],
                                      xg[:, j % XG, k * P:(k + 1) * P], ident[:])
                mm.then_inc(s["xt_done"], 1)

            def expert_GU(i, j):
                b = i * LAP + j
                pe.wait_ge(s["htm_ready"], b + 1)
                if not early(b, 2):
                    pe.wait_ge(s["act_ready"], b - 1)
                pe.wait_ge(w_in_sem[j % LAP], 48 * lap(i, j) + 48)
                w = wexp[:, j % LAP, 0:2 * D].rearrange("p (g k f) -> p g k f", g=2, k=KC)
                for k in range(KC):
                    mm = pe.matmul(ps[:, 2 + j % 2, 0:2 * FF].rearrange("p (g f) -> p g f", g=2),
                                   hTm[:, j % 2, k, :], w[:, :, k, :], start=k == 0, stop=k == KC - 1)
                mm.then_inc(s["gu_done"], 1)

            def expert_AT(i, j):
                b = i * LAP + j
                if not early(b, 1):
                    pe.wait_ge(s["att_ready"], b)
                pe.wait_ge(s["act_ready"], b + 1)
                pe.transpose(ps[:, 4, 0:P], actv[:, j % 2, :], ident[:]).then_inc(s["at_done"], 1)

            def expert_D(i, j):
                b = i * LAP + j
                if not early(b, 1):
                    pe.wait_ge(s["ob_act"], b)
                    pe.wait_ge(s["ob_dve"], b)
                pe.wait_ge(s["att_ready"], b + 1)
                for r in range(2):
                    q = 2 * D + r * 512
                    mm = pe.matmul(ps[:, 5 + r, :], actT[:, j % 2, :], wexp[:, j % LAP, q:q + 512],
                                   start=True, stop=True)
                mm.then_inc(s["d_done"], 1)

            def step(i, j, first, last):
                if not last:
                    expert_T(i, j + 1)
                else:
                    with pe.If(total > 0):
                        expert_T(i, j + 1)
                if not first:
                    expert_AT(i, j - 1)
                expert_GU(i, j)
                if not first:
                    expert_D(i, j - 1)

            pe.wait_ge(s["xg_zero"], 1)
            pe.wait_ge(s["place_ready"], TILES)
            expert_T(0, 0)
            for j in range(LAP):
                step(0, j, first=j == 0, last=False)
            with pe.Fori(1, NE // LAP - 1) as i:
                for j in range(LAP):
                    step(i, j, first=False, last=False)
            pe.wait_ge(s["ov_ready"], 1)
            total = pe.value_load(ovt[0:1, 2 * OVER:2 * OVER + 1], min_val=0, max_val=OVER)
            for j in range(LAP):
                step(NE // LAP - 1, j, first=False, last=j == LAP - 1)
            with pe.If(total < 1):
                expert_AT(NE // LAP - 1, LAP - 1)
                expert_D(NE // LAP - 1, LAP - 1)
            with pe.Fori(0, OVER // LAP) as i:
                with pe.If(i * LAP < total):
                    for j in range(LAP):
                        with pe.If(i * LAP + j < total):
                            with pe.If(i * LAP + j + 1 < total):
                                expert_T(i + NE // LAP, j + 1)
                            expert_AT(i + NE // LAP, j - 1)
                            expert_GU(i + NE // LAP, j)
                            expert_D(i + NE // LAP, j - 1)
                            with pe.If(i * LAP + j + 2 > total):
                                expert_AT(i + NE // LAP, j)
                                expert_D(i + NE // LAP, j)


_INS = ["x_prompt", "x_sample", "state_conv_a", "state_pool", "state_conv_c", "g_mix", "w_in",
        "conv_a_w", "pool_w", "pool_scale", "conv_c_w", "conv_c_b", "ln_c_g", "ln_c_b", "ln_d_g",
        "ln_d_b", "sgu_w", "sgu_b", "w_out", "g_ffn", "router_group_w", "router_group_b",
        "router_expert_w", "router_expert_b", "expert_w_gate", "expert_w_up", "expert_w_down",
        "g_final"]
_OUTS = [("y_prompt", (1, NP, D)), ("y_sample", (SB, ST, D)), ("new_conv_a_prompt", (1, 1, HA, W)),
         ("new_pool_prompt", (1, 1, HP, W)), ("new_conv_c_prompt", (1, 1, HC, W)),
         ("new_conv_a_sample", (1, SB, HA, W)), ("new_pool_sample", (1, SB, HP, W)),
         ("new_conv_c_sample", (1, SB, HC, W)), ("chunk_v_sample", (1, SB, ST, W))]


def kernel(**inputs):
    import numpy as np
    import concourse.bacc as bacc
    from concourse.bass_utils import run_bass_kernel_spmd

    nc = bacc.Bacc("TRN2", target_bir_lowering=False, num_devices=1)
    arrays, args = {}, {}
    for name in _INS:
        x = np.ascontiguousarray(inputs[name])
        arrays[f"in_{name}"] = x
        args[name] = nc.dram_tensor(f"in_{name}", x.shape, mybir.dt.from_np(x.dtype),
                                    kind="ExternalInput").ap()
    for name, shape in _OUTS:
        args[name] = nc.dram_tensor(f"out_{name}", shape, F32, kind="ExternalOutput").ap()
    build_layer(nc, args)
    r = run_bass_kernel_spmd(nc, [arrays], core_ids=[0])
    return tuple(r.results[0][f"out_{name}"] for name, _ in _OUTS)
```
